# Optimizing a Trainium2 kernel written in Bass

```python
import jax, jax.numpy as jnp
from jax import lax
import numpy as np
import math
import jax
import jax.numpy as jnp

D_MODEL = 1024
BATCH = 1
SEQ = 256
DEPTH = 2

D_CONV_A = 512
CONV_A_WIDTH = 3
D_CONV_B = 512
CONV_B_WIDTH = 31
N_HEADS = 16
HEAD_DIM = 64
D_ATTN = N_HEADS * HEAD_DIM
BLOCK_Q = 128
N_GROUPS = 4
EXPERTS_PER_GROUP = 8
N_EXPERTS = N_GROUPS * EXPERTS_PER_GROUP
TOP_K = 2
D_EXPERT = 512
ROW_CHUNK = 256
LN_EPS = 1e-5
DEEPNORM_ALPHA = (2 * DEPTH) ** 0.25
DEEPNORM_BETA = (8 * DEPTH) ** -0.25

N_EVEN = (DEPTH + 1) // 2
N_ODD = DEPTH // 2
D_IN_EVEN = 3 * D_CONV_A + 2 * D_CONV_B
D_MIX_EVEN = D_CONV_A + D_CONV_B


def layer_norm(x, g, b):
    xf = x.astype(jnp.float32)
    mu = jnp.mean(xf, axis=-1, keepdims=True)
    var = jnp.mean(jnp.square(xf - mu), axis=-1, keepdims=True)
    y = (xf - mu) * lax.rsqrt(var + LN_EPS)
    return (y * g + b).astype(x.dtype)

def causal_depthwise_conv(x, w):
    k = w.shape[0]
    return lax.conv_general_dilated(
        x, w[:, None, :].astype(x.dtype), window_strides=(1,), padding=[(k - 1, 0)],
        dimension_numbers=("NWC", "WIO", "NWC"), feature_group_count=x.shape[-1])

def conv_mixers(x, w_in, conv_a, conv_b_w, conv_b_bias, norm_b_g, norm_b_b, w_out):
    u = jnp.einsum("bsd,de->bse", x, w_in)
    a_b, a_c, a_v, b_val, b_gate = jnp.split(
        u, [D_CONV_A, 2 * D_CONV_A, 3 * D_CONV_A, 3 * D_CONV_A + D_CONV_B], axis=-1)
    y_a = a_b * causal_depthwise_conv(a_c * a_v, conv_a)
    g = b_val * jax.nn.sigmoid(b_gate)
    g = causal_depthwise_conv(g, conv_b_w) + conv_b_bias
    y_b = jax.nn.silu(layer_norm(g, norm_b_g, norm_b_b))
    return jnp.einsum("bse,ed->bsd", jnp.concatenate([y_a, y_b], axis=-1), w_out)

def stick_breaking_attention(x, w_qkv, w_o):
    b, s, _ = x.shape
    qkv = jnp.einsum("bsd,de->bse", x, w_qkv).reshape(b, s, 3, N_HEADS, HEAD_DIM)
    q = qkv[:, :, 0].transpose(0, 2, 1, 3)
    k = qkv[:, :, 1].transpose(0, 2, 1, 3)
    v = qkv[:, :, 2].transpose(0, 2, 1, 3)
    scale = HEAD_DIM ** -0.5
    outs = []
    for blk in range(s // BLOCK_Q):
        q0 = blk * BLOCK_Q
        kv_len = q0 + BLOCK_Q
        qb = q[:, :, q0:kv_len]
        kb = k[:, :, :kv_len]
        vb = v[:, :, :kv_len]
        z = jnp.einsum("bhqd,bhkd->bhqk", qb, kb,
                       preferred_element_type=jnp.float32) * scale
        t_idx = q0 + jnp.arange(BLOCK_Q)[:, None]
        s_idx = jnp.arange(kv_len)[None, :]
        causal = s_idx < t_idx
        log_keep = jnp.where(causal, jax.nn.log_sigmoid(-z), 0.0)
        later = lax.cumsum(log_keep, axis=3, reverse=True) - log_keep
        a = jnp.where(causal, jnp.exp(jax.nn.log_sigmoid(z) + later), 0.0)
        outs.append(jnp.einsum("bhqk,bhkd->bhqd", a.astype(vb.dtype), vb))
    o = jnp.concatenate(outs, axis=2).transpose(0, 2, 1, 3).reshape(b, s, D_ATTN)
    return jnp.einsum("bse,ed->bsd", o, w_o)

def hierarchical_moe(x, rg_w, rg_b, re_w, re_b, w_up, w_down):
    b, s, d = x.shape
    h = x.reshape(-1, d)
    t = h.shape[0]
    g_logits = jnp.matmul(h, rg_w).astype(jnp.float32) + rg_b
    grp = jnp.argmax(g_logits, axis=-1)
    g_gate = jnp.take_along_axis(jax.nn.softmax(g_logits, axis=-1), grp[:, None], axis=-1)
    e_logits = (jnp.matmul(h, re_w).astype(jnp.float32) + re_b).reshape(t, N_GROUPS, EXPERTS_PER_GROUP)
    e_logits = jnp.take_along_axis(e_logits, grp[:, None, None], axis=1)[:, 0]
    top_val, top_idx = lax.top_k(e_logits, TOP_K)
    weights = (g_gate * jax.nn.softmax(top_val, axis=-1)).reshape(-1)
    ids = (grp[:, None] * EXPERTS_PER_GROUP + top_idx).reshape(-1).astype(jnp.int32)
    n_assign = t * TOP_K
    order = jnp.argsort(ids)
    sorted_ids = ids[order]
    tok = order // TOP_K
    sizes = jnp.bincount(ids, length=N_EXPERTS)
    padded = (sizes + ROW_CHUNK - 1) // ROW_CHUNK * ROW_CHUNK
    pad_end = jnp.cumsum(padded)
    pad_start = pad_end - padded
    start = jnp.cumsum(sizes) - sizes
    dest = pad_start[sorted_ids] + jnp.arange(n_assign) - start[sorted_ids]
    n_chunks = -(-n_assign // ROW_CHUNK) + N_EXPERTS
    rows = jnp.zeros((n_chunks * ROW_CHUNK, d), h.dtype).at[dest].set(h[tok])
    chunk_expert = jnp.minimum(
        jnp.searchsorted(pad_end, jnp.arange(n_chunks) * ROW_CHUNK, side="right"), N_EXPERTS - 1)

    def expert_chunk(args):
        xc, e = args
        gate, up = jnp.split(jnp.matmul(xc, w_up[e]), 2, axis=-1)
        return jnp.matmul(jax.nn.silu(gate) * up, w_down[e])

    y_rows = lax.map(expert_chunk, (rows.reshape(n_chunks, ROW_CHUNK, d), chunk_expert))
    y = y_rows.reshape(-1, d)[dest] * weights[order][:, None].astype(h.dtype)
    out = jnp.zeros((t, d), h.dtype).at[tok].add(y)
    return out.reshape(b, s, d)

def first_inputs(seed: int = 0) -> dict:
    key = jax.random.key(seed)
    ks = jax.random.split(key, 24)
    nrm = jax.random.normal
    f32 = jnp.float32
    x = nrm(ks[0], (BATCH, SEQ, D_MODEL), f32)
    even_w_in = nrm(ks[1], (N_EVEN, D_MODEL, D_IN_EVEN), f32) * D_MODEL ** -0.5
    even_conv_a = nrm(ks[2], (N_EVEN, CONV_A_WIDTH, D_CONV_A), f32) * CONV_A_WIDTH ** -0.5
    even_conv_b_w = nrm(ks[3], (N_EVEN, CONV_B_WIDTH, D_CONV_B), f32) * CONV_B_WIDTH ** -0.5
    even_conv_b_bias = nrm(ks[4], (N_EVEN, D_CONV_B), f32) * 0.02
    even_norm_b_g = 1.0 + 0.1 * nrm(ks[5], (N_EVEN, D_CONV_B), f32)
    even_norm_b_b = 0.02 * nrm(ks[6], (N_EVEN, D_CONV_B), f32)
    even_w_out = nrm(ks[7], (N_EVEN, D_MIX_EVEN, D_MODEL), f32) * (D_MIX_EVEN ** -0.5 * DEEPNORM_BETA)
    v_scale = jnp.concatenate([jnp.ones((2 * D_ATTN,), f32), jnp.full((D_ATTN,), DEEPNORM_BETA, f32)])
    odd_w_qkv = nrm(ks[8], (N_ODD, D_MODEL, 3 * D_ATTN), f32) * D_MODEL ** -0.5 * v_scale
    odd_w_o = nrm(ks[9], (N_ODD, D_ATTN, D_MODEL), f32) * (D_ATTN ** -0.5 * DEEPNORM_BETA)
    ln_mix_g = 1.0 + 0.1 * nrm(ks[10], (DEPTH, D_MODEL), f32)
    ln_mix_b = 0.02 * nrm(ks[11], (DEPTH, D_MODEL), f32)
    ln_ffn_g = 1.0 + 0.1 * nrm(ks[12], (DEPTH, D_MODEL), f32)
    ln_ffn_b = 0.02 * nrm(ks[13], (DEPTH, D_MODEL), f32)
    router_group_w = nrm(ks[14], (DEPTH, D_MODEL, N_GROUPS), f32) * D_MODEL ** -0.5
    router_group_b = 0.01 * nrm(ks[15], (DEPTH, N_GROUPS), f32)
    router_expert_w = nrm(ks[16], (DEPTH, D_MODEL, N_EXPERTS), f32) * D_MODEL ** -0.5
    router_expert_b = 0.01 * nrm(ks[17], (DEPTH, N_EXPERTS), f32)
    expert_w_up = nrm(ks[18], (DEPTH, N_EXPERTS, D_MODEL, 2 * D_EXPERT), f32) * D_MODEL ** -0.5
    expert_w_down = nrm(ks[19], (DEPTH, N_EXPERTS, D_EXPERT, D_MODEL), f32) * (D_EXPERT ** -0.5 * DEEPNORM_BETA)
    return {"x": x, "even_w_in": even_w_in, "even_conv_a": even_conv_a,
            "even_conv_b_w": even_conv_b_w, "even_conv_b_bias": even_conv_b_bias,
            "even_norm_b_g": even_norm_b_g, "even_norm_b_b": even_norm_b_b,
            "even_w_out": even_w_out, "odd_w_qkv": odd_w_qkv, "odd_w_o": odd_w_o,
            "ln_mix_g": ln_mix_g, "ln_mix_b": ln_mix_b, "ln_ffn_g": ln_ffn_g, "ln_ffn_b": ln_ffn_b,
            "router_group_w": router_group_w, "router_group_b": router_group_b,
            "router_expert_w": router_expert_w, "router_expert_b": router_expert_b,
            "expert_w_up": expert_w_up, "expert_w_down": expert_w_down}

def first_block(x, even_w_in, even_conv_a, even_conv_b_w, even_conv_b_bias, even_norm_b_g,
              even_norm_b_b, even_w_out, odd_w_qkv, odd_w_o, ln_mix_g, ln_mix_b, ln_ffn_g,
              ln_ffn_b, router_group_w, router_group_b, router_expert_w, router_expert_b,
              expert_w_up, expert_w_down):
    for layer in range(DEPTH):
        i = layer // 2
        if layer % 2 == 0:
            mix = conv_mixers(x, even_w_in[i], even_conv_a[i], even_conv_b_w[i],
                              even_conv_b_bias[i], even_norm_b_g[i], even_norm_b_b[i],
                              even_w_out[i])
        else:
            mix = stick_breaking_attention(x, odd_w_qkv[i], odd_w_o[i])
        x = layer_norm(DEEPNORM_ALPHA * x + mix, ln_mix_g[layer], ln_mix_b[layer])
        ffn = hierarchical_moe(x, router_group_w[layer], router_group_b[layer],
                               router_expert_w[layer], router_expert_b[layer],
                               expert_w_up[layer], expert_w_down[layer])
        x = layer_norm(DEEPNORM_ALPHA * x + ffn, ln_ffn_g[layer], ln_ffn_b[layer])
    return x


RMS_EPS = 1e-6
ROPE_THETA = 500000.0

SSD_HEAD_DIM = 64
SSD_D_INNER = D_MODEL
SSD_HEADS = SSD_D_INNER // SSD_HEAD_DIM
SSD_GROUPS = 4
SSD_D_STATE = 128
SSD_CONV = 4
SSD_CHUNK = 256
SSD_CONV_DIM = SSD_D_INNER + 2 * SSD_GROUPS * SSD_D_STATE

DIL_PAIRS = ((128, 1), (512, 4), (2048, 16))
DIL_HEAD_DIM = 64
DIL_HEADS_PER_GROUP = 8
DIL_HEADS = DIL_HEADS_PER_GROUP * len(DIL_PAIRS)
DIL_QKV = DIL_HEADS * DIL_HEAD_DIM
DIL_OUT = DIL_HEADS_PER_GROUP * DIL_HEAD_DIM

MOBA_HEAD_DIM = 64
MOBA_WIDTH = D_MODEL
MOBA_HEADS = MOBA_WIDTH // MOBA_HEAD_DIM
MOBA_BLOCK = 256
MOBA_TOPK = 3
MOBA_Q_CHUNK = 16

EVEN_IN_SIZES = (SSD_D_INNER, SSD_CONV_DIM, SSD_HEADS, DIL_QKV, DIL_QKV, DIL_QKV, DIL_OUT)
EVEN_IN = sum(EVEN_IN_SIZES)
EVEN_MIX = SSD_D_INNER + DIL_OUT
ODD_IN = 4 * MOBA_WIDTH
N_EVEN_2 = (DEPTH + 1) // 2
N_ODD_2 = DEPTH // 2


def rms_norm(x, w):
    xf = x.astype(jnp.float32)
    y = xf * lax.rsqrt(jnp.mean(xf * xf, axis=-1, keepdims=True) + RMS_EPS)
    return (y * w.astype(jnp.float32)).astype(x.dtype)

def partial_rope(x, pos):
    e = x.shape[-1]
    rd = e // 4
    half = rd // 2
    inv = ROPE_THETA ** (-jnp.arange(half, dtype=jnp.float32) * 2.0 / rd)
    ang = pos.astype(jnp.float32)[:, None] * inv[None, :]
    cos = jnp.cos(ang)[:, None, :]
    sin = jnp.sin(ang)[:, None, :]
    xr = x[..., :rd].astype(jnp.float32)
    x1, x2 = xr[..., :half], xr[..., half:]
    rot = jnp.concatenate([x1 * cos - x2 * sin, x2 * cos + x1 * sin], axis=-1)
    return jnp.concatenate([rot.astype(x.dtype), x[..., rd:]], axis=-1)

def split_cols(t, sizes):
    outs, o = [], 0
    for s in sizes:
        outs.append(t[..., o:o + s])
        o += s
    return outs

def causal_dwconv(x, w, b):
    K = w.shape[1]
    rhs = jnp.transpose(w)[:, None, :].astype(x.dtype)
    y = lax.conv_general_dilated(x, rhs, window_strides=(1,), padding=((K - 1, 0),),
                                 dimension_numbers=("NWC", "WIO", "NWC"),
                                 feature_group_count=x.shape[-1])
    return y + b.astype(x.dtype)

def segsum(a):
    T = a.shape[-1]
    cs = jnp.cumsum(a, axis=-1)
    diff = cs[..., :, None] - cs[..., None, :]
    mask = jnp.tril(jnp.ones((T, T), dtype=bool))
    return jnp.where(mask, diff, -jnp.inf)

def ssd_chunked_scan(x, dt, A, Bm, Cm):
    Bsz, S, H, P = x.shape
    G, N = Bm.shape[2], Bm.shape[3]
    J = H // G
    L = SSD_CHUNK
    pad = (-S) % L
    xdt = x.astype(jnp.float32) * dt[..., None]
    a = dt * A
    Bf = Bm.astype(jnp.float32)
    Cf = Cm.astype(jnp.float32)
    if pad:
        padseq = lambda t: jnp.pad(t, [(0, 0), (0, pad)] + [(0, 0)] * (t.ndim - 2))
        xdt, a, Bf, Cf = padseq(xdt), padseq(a), padseq(Bf), padseq(Cf)
    nc = (S + pad) // L
    xdt = xdt.reshape(Bsz, nc, L, G, J, P)
    Bc = Bf.reshape(Bsz, nc, L, G, N)
    Cc = Cf.reshape(Bsz, nc, L, G, N)
    a = a.reshape(Bsz, nc, L, G, J).transpose(0, 3, 4, 1, 2)
    a_cs = jnp.cumsum(a, axis=-1)
    cb = jnp.einsum("bclgn,bcsgn->bgcls", Cc, Bc)
    m = cb[:, :, None] * jnp.exp(segsum(a))
    y_diag = jnp.einsum("bgjcls,bcsgjp->bclgjp", m, xdt)
    w_end = jnp.exp(a_cs[..., -1:] - a_cs).transpose(0, 3, 4, 1, 2)
    states = jnp.einsum("bclgn,bclgjp->bcgjpn", Bc, xdt * w_end[..., None])
    a_last = jnp.pad(a_cs[..., -1], [(0, 0)] * 3 + [(1, 0)])
    decay_chunk = jnp.exp(segsum(a_last))
    states0 = jnp.concatenate([jnp.zeros_like(states[:, :1]), states], axis=1)
    entering = jnp.einsum("bgjzc,bcgjpn->bzgjpn", decay_chunk, states0)[:, :-1]
    w_start = jnp.exp(a_cs).transpose(0, 3, 4, 1, 2)
    y_off = jnp.einsum("bclgn,bcgjpn->bclgjp", Cc, entering) * w_start[..., None]
    return (y_diag + y_off).reshape(Bsz, nc * L, H, P)[:, :S]

def dilated_group(q, k, v, window, dil):
    Bsz, S, h, e = q.shape
    band = window // dil
    Lsub = S // dil
    nb = -(-Lsub // band)
    Lp = nb * band

    def to_sub(t):
        t = t.astype(jnp.float32).reshape(Bsz, Lsub, dil, h, e).transpose(0, 3, 2, 1, 4)
        t = jnp.pad(t, ((0, 0), (0, 0), (0, 0), (0, Lp - Lsub), (0, 0)))
        return t.reshape(Bsz, h, dil, nb, band, e)

    def with_prev(t):
        prev = jnp.pad(t, ((0, 0), (0, 0), (0, 0), (1, 0), (0, 0), (0, 0)))[:, :, :, :-1]
        return jnp.concatenate([prev, t], axis=4)

    qs = to_sub(q)
    kb = with_prev(to_sub(k))
    vb = with_prev(to_sub(v))
    s = jnp.einsum("bhrnqe,bhrnke->bhrnqk", qs, kb) * (e ** -0.5)
    i = jnp.arange(band)[:, None]
    j = jnp.arange(2 * band)[None, :]
    dist = i + band - j
    n = jnp.arange(nb)[:, None, None]
    valid = (dist >= 0) & (dist <= band) & ((n * band + j[None] - band) >= 0)
    s = jnp.where(valid, s, -jnp.inf)
    mx = jnp.max(s, axis=-1, keepdims=True)
    p = jnp.exp(s - mx)
    den = jnp.sum(p, axis=-1)
    o = jnp.einsum("bhrnqk,bhrnke->bhrnqe", p, vb) / den[..., None]
    lse = mx[..., 0] + jnp.log(den)
    o = o.reshape(Bsz, h, dil, Lp, e)[:, :, :, :Lsub].transpose(0, 3, 2, 1, 4).reshape(Bsz, S, h, e)
    lse = lse.reshape(Bsz, h, dil, Lp)[:, :, :, :Lsub].transpose(0, 3, 2, 1).reshape(Bsz, S, h)
    return o, lse

def moba_attention(q, k, v):
    Bsz, S, H, e = q.shape
    blk = MOBA_BLOCK
    nblk = -(-S // blk)
    Sp = nblk * blk
    scale = e ** -0.5

    def heads_first(t):
        t = t.astype(jnp.float32).transpose(0, 2, 1, 3)
        return jnp.pad(t, ((0, 0), (0, 0), (0, Sp - S), (0, 0)))

    qh = heads_first(q)
    kb = heads_first(k).reshape(Bsz, H, nblk, blk, e)
    vb = heads_first(v).reshape(Bsz, H, nblk, blk, e)
    kmean = jnp.mean(kb, axis=3)
    gate = jnp.einsum("bhte,bhne->bhtn", qh, kmean)
    tblk = jnp.arange(Sp) // blk
    past = jnp.arange(nblk)[None, :] < tblk[:, None]
    gate = jnp.where(past, gate, -jnp.inf)
    ksel = min(MOBA_TOPK, nblk)
    _, sel = lax.top_k(gate, ksel)
    sel_valid = sel < tblk[:, None]

    Qc = MOBA_Q_CHUNK
    nq = Sp // Qc
    qc = qh.reshape(Bsz, H, nq, Qc, e).transpose(2, 0, 1, 3, 4)
    selc = sel.reshape(Bsz, H, nq, Qc, ksel).transpose(2, 0, 1, 3, 4)
    valc = sel_valid.reshape(Bsz, H, nq, Qc, ksel).transpose(2, 0, 1, 3, 4)
    bi = jnp.arange(Bsz)[:, None, None, None]
    hi = jnp.arange(H)[None, :, None, None]

    def one_chunk(args):
        c, q_c, sel_c, val_c = args
        own = (c * Qc) // blk
        k_sel = kb[bi, hi, sel_c]
        v_sel = vb[bi, hi, sel_c]
        s_sel = jnp.einsum("bhqe,bhqjke->bhqjk", q_c, k_sel) * scale
        s_sel = jnp.where(val_c[..., None], s_sel, -jnp.inf).reshape(Bsz, H, Qc, ksel * blk)
        k_own = lax.dynamic_index_in_dim(kb, own, axis=2, keepdims=False)
        v_own = lax.dynamic_index_in_dim(vb, own, axis=2, keepdims=False)
        s_own = jnp.einsum("bhqe,bhke->bhqk", q_c, k_own) * scale
        qpos = c * Qc + jnp.arange(Qc)
        kpos = own * blk + jnp.arange(blk)
        s_own = jnp.where(kpos[None, :] <= qpos[:, None], s_own, -jnp.inf)
        p = jax.nn.softmax(jnp.concatenate([s_sel, s_own], axis=-1), axis=-1)
        p_sel = p[..., :ksel * blk].reshape(Bsz, H, Qc, ksel, blk)
        return (jnp.einsum("bhqjk,bhqjke->bhqe", p_sel, v_sel)
                + jnp.einsum("bhqk,bhke->bhqe", p[..., ksel * blk:], v_own))

    out = lax.map(one_chunk, (jnp.arange(nq), qc, selc, valc))
    return out.transpose(1, 0, 3, 2, 4).reshape(Bsz, Sp, H, e)[:, :S]

def ssd_dilated_layer(x, norm_w, w_in, conv_w, conv_b, dt_bias, a_log, d_skip, ssd_norm_w,
                      q_norm, k_norm, w_out, pos):
    Bsz, S, _ = x.shape
    h = rms_norm(x, norm_w)
    proj = jnp.einsum("bsd,df->bsf", h, w_in.astype(h.dtype))
    z, xbc, dt, q, k, v, g = split_cols(proj, EVEN_IN_SIZES)
    xbc = jax.nn.silu(causal_dwconv(xbc, conv_w, conv_b))
    xs, bm, cm = split_cols(xbc, (SSD_D_INNER, SSD_GROUPS * SSD_D_STATE, SSD_GROUPS * SSD_D_STATE))
    xs = xs.reshape(Bsz, S, SSD_HEADS, SSD_HEAD_DIM)
    dt = jax.nn.softplus(dt.astype(jnp.float32) + dt_bias.astype(jnp.float32))
    A = -jnp.exp(a_log.astype(jnp.float32))
    y = ssd_chunked_scan(xs, dt, A, bm.reshape(Bsz, S, SSD_GROUPS, SSD_D_STATE),
                         cm.reshape(Bsz, S, SSD_GROUPS, SSD_D_STATE))
    y = y + d_skip.astype(jnp.float32)[:, None] * xs.astype(jnp.float32)
    y = y.reshape(Bsz, S, SSD_D_INNER) * jax.nn.silu(z.astype(jnp.float32))
    y = rms_norm(y.reshape(Bsz, S, SSD_GROUPS, -1),
                 ssd_norm_w.reshape(SSD_GROUPS, -1)).reshape(Bsz, S, SSD_D_INNER)
    q = partial_rope(rms_norm(q.reshape(Bsz, S, DIL_HEADS, DIL_HEAD_DIM), q_norm), pos)
    k = partial_rope(rms_norm(k.reshape(Bsz, S, DIL_HEADS, DIL_HEAD_DIM), k_norm), pos)
    v = v.reshape(Bsz, S, DIL_HEADS, DIL_HEAD_DIM)
    outs, lses = [], []
    for gi, (window, dil) in enumerate(DIL_PAIRS):
        hs = slice(gi * DIL_HEADS_PER_GROUP, (gi + 1) * DIL_HEADS_PER_GROUP)
        o_g, lse_g = dilated_group(q[:, :, hs], k[:, :, hs], v[:, :, hs], window, dil)
        outs.append(o_g)
        lses.append(lse_g)
    wts = jax.nn.softmax(jnp.stack(lses, axis=0), axis=0)
    o = jnp.sum(wts[..., None] * jnp.stack(outs, axis=0), axis=0)
    o = o.reshape(Bsz, S, DIL_OUT) * jax.nn.silu(g.astype(jnp.float32))
    mixed = jnp.concatenate([y.astype(jnp.float32), o], axis=-1).astype(x.dtype)
    return x + jnp.einsum("bsf,fd->bsd", mixed, w_out.astype(x.dtype))

def moba_layer(x, norm_w, w_in, q_norm, k_norm, w_out, pos):
    Bsz, S, _ = x.shape
    h = rms_norm(x, norm_w)
    proj = jnp.einsum("bsd,df->bsf", h, w_in.astype(h.dtype))
    q, k, v, g = split_cols(proj, (MOBA_WIDTH,) * 4)
    q = partial_rope(rms_norm(q.reshape(Bsz, S, MOBA_HEADS, MOBA_HEAD_DIM), q_norm), pos)
    k = partial_rope(rms_norm(k.reshape(Bsz, S, MOBA_HEADS, MOBA_HEAD_DIM), k_norm), pos)
    v = v.reshape(Bsz, S, MOBA_HEADS, MOBA_HEAD_DIM)
    o = moba_attention(q, k, v).reshape(Bsz, S, MOBA_WIDTH) * jax.nn.silu(g.astype(jnp.float32))
    return x + jnp.einsum("bsf,fd->bsd", o.astype(x.dtype), w_out.astype(x.dtype))

def second_inputs(seed: int = 0) -> dict:
    key = jax.random.key(seed)
    ks = jax.random.split(key, 20)
    f32 = jnp.float32
    nrm = lambda k, shape, s: jax.random.normal(k, shape, f32) * s
    x = jax.random.normal(ks[0], (BATCH, SEQ, D_MODEL), f32)
    even_norm_w = 1.0 + nrm(ks[1], (N_EVEN_2, D_MODEL), 0.05)
    even_w_in = nrm(ks[2], (N_EVEN_2, D_MODEL, EVEN_IN), D_MODEL ** -0.5)
    even_conv_w = nrm(ks[3], (N_EVEN_2, SSD_CONV_DIM, SSD_CONV), SSD_CONV ** -0.5)
    even_conv_b = nrm(ks[4], (N_EVEN_2, SSD_CONV_DIM), 0.01)
    dt0 = jnp.exp(jax.random.uniform(ks[5], (N_EVEN_2, SSD_HEADS), f32,
                                     math.log(1e-3), math.log(1e-1)))
    even_dt_bias = dt0 + jnp.log(-jnp.expm1(-dt0))
    even_a_log = jnp.log(jax.random.uniform(ks[6], (N_EVEN_2, SSD_HEADS), f32, 1.0, 16.0))
    even_d_skip = 1.0 + nrm(ks[7], (N_EVEN_2, SSD_HEADS), 0.1)
    even_ssd_norm_w = 1.0 + nrm(ks[8], (N_EVEN_2, SSD_D_INNER), 0.05)
    even_q_norm = 1.0 + nrm(ks[9], (N_EVEN_2, DIL_HEAD_DIM), 0.05)
    even_k_norm = 1.0 + nrm(ks[10], (N_EVEN_2, DIL_HEAD_DIM), 0.05)
    even_w_out = nrm(ks[11], (N_EVEN_2, EVEN_MIX, D_MODEL), EVEN_MIX ** -0.5)
    odd_norm_w = 1.0 + nrm(ks[12], (N_ODD_2, D_MODEL), 0.05)
    odd_w_in = nrm(ks[13], (N_ODD_2, D_MODEL, ODD_IN), D_MODEL ** -0.5)
    odd_q_norm = 1.0 + nrm(ks[14], (N_ODD_2, MOBA_HEAD_DIM), 0.05)
    odd_k_norm = 1.0 + nrm(ks[15], (N_ODD_2, MOBA_HEAD_DIM), 0.05)
    odd_w_out = nrm(ks[16], (N_ODD_2, MOBA_WIDTH, D_MODEL), MOBA_WIDTH ** -0.5)
    return {"x": x, "even_norm_w": even_norm_w, "even_w_in": even_w_in,
            "even_conv_w": even_conv_w, "even_conv_b": even_conv_b,
            "even_dt_bias": even_dt_bias, "even_a_log": even_a_log, "even_d_skip": even_d_skip,
            "even_ssd_norm_w": even_ssd_norm_w, "even_q_norm": even_q_norm,
            "even_k_norm": even_k_norm, "even_w_out": even_w_out,
            "odd_norm_w": odd_norm_w, "odd_w_in": odd_w_in, "odd_q_norm": odd_q_norm,
            "odd_k_norm": odd_k_norm, "odd_w_out": odd_w_out}

def second_block(x, even_norm_w, even_w_in, even_conv_w, even_conv_b, even_dt_bias, even_a_log,
              even_d_skip, even_ssd_norm_w, even_q_norm, even_k_norm, even_w_out,
              odd_norm_w, odd_w_in, odd_q_norm, odd_k_norm, odd_w_out):
    pos = jnp.arange(x.shape[1], dtype=jnp.int32)
    for layer in range(DEPTH):
        li = layer // 2
        if layer % 2 == 0:
            x = ssd_dilated_layer(x, even_norm_w[li], even_w_in[li], even_conv_w[li],
                                  even_conv_b[li], even_dt_bias[li], even_a_log[li],
                                  even_d_skip[li], even_ssd_norm_w[li], even_q_norm[li],
                                  even_k_norm[li], even_w_out[li], pos)
        else:
            x = moba_layer(x, odd_norm_w[li], odd_w_in[li], odd_q_norm[li], odd_k_norm[li],
                           odd_w_out[li], pos)
    return x


def setup_inputs(seed=0):
    out = dict(first_inputs(seed))
    for name, value in second_inputs(seed + 1).items():
        if name != "x":
            out[name + "_2"] = value
    return out


def reference(
    x, even_w_in, even_conv_a, even_conv_b_w, even_conv_b_bias, even_norm_b_g, even_norm_b_b,
    even_w_out, odd_w_qkv, odd_w_o, ln_mix_g, ln_mix_b, ln_ffn_g, ln_ffn_b, router_group_w,
    router_group_b, router_expert_w, router_expert_b, expert_w_up, expert_w_down, even_norm_w_2,
    even_w_in_2, even_conv_w_2, even_conv_b_2, even_dt_bias_2, even_a_log_2, even_d_skip_2,
    even_ssd_norm_w_2, even_q_norm_2, even_k_norm_2, even_w_out_2, odd_norm_w_2, odd_w_in_2,
    odd_q_norm_2, odd_k_norm_2, odd_w_out_2,
):
    x = first_block(
        x, even_w_in, even_conv_a, even_conv_b_w, even_conv_b_bias, even_norm_b_g,
        even_norm_b_b, even_w_out, odd_w_qkv, odd_w_o, ln_mix_g, ln_mix_b, ln_ffn_g, ln_ffn_b,
        router_group_w, router_group_b, router_expert_w, router_expert_b, expert_w_up,
        expert_w_down,
    )
    return second_block(
        x, even_norm_w_2, even_w_in_2, even_conv_w_2, even_conv_b_2, even_dt_bias_2,
        even_a_log_2, even_d_skip_2, even_ssd_norm_w_2, even_q_norm_2, even_k_norm_2,
        even_w_out_2, odd_norm_w_2, odd_w_in_2, odd_q_norm_2, odd_k_norm_2, odd_w_out_2,
    )


_drawn_inputs = setup_inputs


def setup_inputs(seed=0):
    import zlib

    import numpy as np

    out = dict(_drawn_inputs(seed))
    spreads = {}
    factors = {'even_conv_b_bias': 3.97,
     'even_norm_b_b': 7.411,
     'router_group_b': 8.0,
     'router_expert_b': 6.291,
     'even_conv_b_2': 6.188,
     'even_q_norm_2': 8.0,
     'even_k_norm_2': 8.0,
     'odd_norm_w_2': 5.751,
     'odd_q_norm_2': 8.0,
     'odd_k_norm_2': 8.0}
    for name, (base, spread) in spreads.items():
        noise = np.random.default_rng([zlib.crc32(name.encode()), seed]).standard_normal(out[name].shape)
        drawn = base * np.exp(spread * noise) if base else spread * noise
        out[name] = jnp.asarray(drawn.astype(out[name].dtype))
    for name, factor in factors.items():
        out[name] = (out[name] * factor).astype(out[name].dtype)
    return out
```

```python
from contextlib import ExitStack

import numpy as np

import concourse.bass as bass
from concourse import mybir

F32 = mybir.dt.float32
I32 = mybir.dt.int32
ALU = mybir.AluOpType
ACT = mybir.ActivationFunctionType
AX = mybir.AxisListType.X

P = 128
TOK = 256
D = 1024
KT = D // P
ALPHA = 4 ** 0.25
LN_EPS, RMS_EPS = 1e-5, 1e-6
NEG = -1e30

EXPERTS, GROUPS, PER_GROUP = 32, 4, 8
PAIRS = EXPERTS // 2
SLOTS = 64
ROUNDS = TOK // SLOTS
FFN = 512

SB_HEADS = 16
SSD_HEADS = 16
CONV_A, CONV_B = 3, 31
HEAD_COLS = 384

RING = 6
SLOT_WORDS = 4096
ARENA = 15800

STAGE_CHUNKS = [7, 6 * PAIRS, 8, 6 * PAIRS, 19, 10]
BASE = [sum(STAGE_CHUNKS[:n]) for n in range(len(STAGE_CHUNKS))]
CONV, MOE0, STICK, MOE1, SSD, MOBA = range(6)

TURNS = ["x0", "x1", "x2", "x3", "h4", "y4", "qk0", "qk1", "qk2", "h5", "qk3", "qk4"]
TURN = {name: n for n, name in enumerate(TURNS)}


def layout(items):
    at, out = 0, {}
    for name, n in items:
        out[name] = (at, at + n)
        at += n
    return out, at


CONST, CONST_WORDS = layout([
    ("ident", P), ("alpha", P), ("upto", P), ("ones", P), ("before", P), ("from_on", P),
    ("mean", P), ("iota", SLOTS), ("rev8", 8), ("rev4", 4), ("stick_mul", HEAD_COLS),
    ("stick_add", HEAD_COLS), ("ssd_add", HEAD_COLS), ("att_add", 4 * HEAD_COLS),
    ("cos", 16), ("sin", 16)])
PARAM, PARAM_WORDS = layout([
    ("conv_a", 4 * CONV_A), ("conv_b", 4 * CONV_B), ("conv_bb", 4), ("norm_g", 4), ("norm_b", 4),
    ("router_w", 2 * KT * 36), ("router_b", 72), ("dt_w", KT * 16), ("conv2_w", 64),
    ("conv2_b", 16), ("norm4", 8), ("norm5", 8), ("ssd_norm", 8), ("dt_b", 16), ("a_log", 16),
    ("d_skip", 16), ("qk4", 128), ("qk5", 128)])


def constants():
    r = np.arange(P)
    row, col = r[:, None], r[None, :]
    c = np.zeros((P, CONST_WORDS), np.float32)

    def put(name, value, at=0):
        a, b = CONST[name]
        value = np.asarray(value, np.float32)
        c[:, a + at:a + at + value.shape[-1]] = value

    put("ident", row == col)
    put("alpha", (row == col) * np.float32(ALPHA))
    put("upto", row <= col)
    put("ones", np.ones((P, P)))
    put("before", row < col)
    put("from_on", row >= col)
    put("mean", np.full((P, P), 1.0 / 512))
    put("iota", np.broadcast_to(np.arange(SLOTS), (P, SLOTS)))
    put("rev8", np.broadcast_to(8 - np.arange(8), (P, 8)))
    put("rev4", np.broadcast_to(4 - np.arange(4), (P, 4)))

    def blocks(valid, keys_first):
        out = []
        for t, s in ((0, 0), (1, 0), (1, 1)):
            if keys_first:
                out.append(valid(t * P + col, s * P + row))
            else:
                out.append(valid(t * P + row, s * P + col))
        return np.concatenate(out, 1)

    strict = blocks(lambda t, s: s < t, True)
    put("stick_mul", strict)
    put("stick_add", np.where(strict, 0.0, NEG))
    put("ssd_add", np.where(blocks(lambda t, s: s <= t, True), 0.0, NEG))
    for n, (band, dil) in enumerate(((P, 1), (TOK, 4), (TOK, 16), (TOK, 1))):
        ok = blocks(lambda t, s: (s <= t) & (t - s <= band) & ((t - s) % dil == 0), False)
        put("att_add", np.where(ok, 0.0, NEG), n * HEAD_COLS)
    inv = np.float32(500000.0) ** (-np.arange(8, dtype=np.float32) * 2.0 / 16)
    ang = np.arange(TOK, dtype=np.float32)[:, None] * inv[None, :].astype(np.float32)
    for name, f in (("cos", np.cos), ("sin", np.sin)):
        table = f(ang.astype(np.float32)).reshape(2, P, 8).transpose(1, 0, 2).reshape(P, 16)
        put(name, table)
    return c


def build(nc, a, out, first=0, last=5):
    on = range(first, last + 1)
    turns = [n for n in TURNS if int({"x": n[1:], "h": n[1:], "y": n[1:], "q": "4" if n in
             ("qk0", "qk1", "qk2") else "5"}[n[0]]) in on]
    turn = {n: k for k, n in enumerate(turns)}
    base, at = {}, 0
    for n in on:
        base[n] = at
        at += STAGE_CHUNKS[n]

    ctx = ExitStack()
    with ctx:
        def sb(name, words, dt=F32):
            return ctx.enter_context(nc.sbuf_tensor(name, [P, words], dt))

        sems = {}

        def sem(name):
            if name not in sems:
                sems[name] = ctx.enter_context(nc.semaphore(name))
            return sems[name]

        ring = sb("ring", RING * SLOT_WORDS)
        con = sb("constants_sb", CONST_WORDS)
        par = sb("params_sb", PARAM_WORDS)
        x_w = sb("x_tok", 2 * D)
        xT_w = sb("xT", KT * TOK)
        ln_w = sb("ln_rows", 2 * D)
        arena = sb("arena", ARENA)
        ps = ctx.enter_context(nc.psum_tensor("ps", [P, 8, 512], F32))

        def bank(b):
            return ps[:, b, :]

        def C(name):
            return con[:, CONST[name][0]:CONST[name][1]]

        def Q(name):
            return par[:, PARAM[name][0]:PARAM[name][1]]

        class Region:

            def __init__(self, at=0, whole=None, size=ARENA):
                self.at, self.whole, self.size = at, arena if whole is None else whole, size

            def __call__(self, words, pattern=None, **dims):
                v = self.whole[:, self.at:self.at + words]
                self.at += words
                assert self.at <= self.size, self.at
                return v.rearrange(pattern, **dims) if pattern else v

        ident, ones = C("ident"), C("ones")
        x = x_w[:, :].rearrange("p (t c) -> p t c", t=2)
        xT = xT_w[:, :].rearrange("p (k t) -> p k t", k=KT)
        lnr = ln_w[:, :].rearrange("p (r c) -> p r c", r=2)
        slot8 = [ring[:, s * SLOT_WORDS:(s + 1) * SLOT_WORDS].rearrange("p (k n) -> p k n", k=8)
                 for s in range(RING)]
        slot4 = [ring[:, s * SLOT_WORDS:(s + 1) * SLOT_WORDS].rearrange("p (k n) -> p k n", k=4)
                 for s in range(RING)]

        sm = Region(whole=sb("small", 640), size=640)
        stats = sm(24, "p (t n s) -> p t n s", t=2, n=2)
        mv = sm(4, "p (t s) -> p t s", t=2)
        rstd = sm(2, "p (t s) -> p t s", t=2)
        lg = sm(72, "p (t n) -> p t n", t=2)
        gm = sm(2, "p (t n) -> p t n", t=2)
        ge = sm(8, "p (t n) -> p t n", t=2)
        gate = sm(2, "p (t n) -> p t n", t=2)
        g1h = sm(8, "p (t n) -> p t n", t=2)
        tie4 = sm(8, "p (t n) -> p t n", t=2)
        picked = sm(64, "p (t g j) -> p t g j", t=2, g=4)
        el = sm(16, "p (t n) -> p t n", t=2)
        tie8 = sm(16, "p (t n) -> p t n", t=2)
        top = sm(4, "p (n t o) -> p n t o", n=2, t=2)
        one_hot = sm(32, "p (n t j) -> p n t j", n=2, t=2)
        dexp = sm(2, "p (t n) -> p t n", t=2)
        w12 = sm(4, "p (n t o) -> p n t o", n=2, t=2)
        s8 = sm(16, "p (t n) -> p t n", t=2)
        w8 = sm(16, "p (t n) -> p t n", t=2)
        s32 = sm(64, "p (t n) -> p t n", t=2)
        wt32 = sm(64, "p (t n) -> p t n", t=2)
        rankm = sm(68, "p (t n) -> p t n", t=2)
        cnt_f = sm(1)
        ge_m = sm(8, "p (t n) -> p t n", t=2)
        gap, gidx = sm(2), sm(2)
        cnt_i = sb("cnt_i", 1, I32)
        root_w = sb("root_w", 3 * TOK)

        x_in = sem("x_in")
        const_in = sem("const_in")
        ln_in = sem("ln_in")
        w_in = [sem(f"w_in{s}") for s in range(RING)]
        chunk_done = sem("chunk_done")
        transposed = sem("transposed")
        moved_T = sem("moved_T")
        x_ready = sem("x_ready")
        out_done = sem("out_done")

        def arrive(eng, g):
            eng.wait_ge(w_in[g % RING], 16 * (g // RING + 1))

        def wait_x(eng, stage):
            if stage == first:
                eng.wait_ge(x_in, 16)
            else:
                eng.wait_ge(x_ready, stage - first)

        class Steps:

            def __init__(self, eng, name):
                self.eng, self.sem, self.n = eng, sem(name), 0

            def add(self, ins):
                ins.then_inc(self.sem, 1)
                self.n += 1

            def settle(self):
                if self.n:
                    self.eng.wait_ge(self.sem, self.n)

            def settle_but(self, n):
                self.eng.wait_ge(self.sem, self.n - n)

            def run(self, ins):
                self.add(ins)
                self.settle()

        r = Region()
        cv_mixT = r(KT * TOK, "p (k t) -> p k t", k=KT)
        cv_sig = r(4 * TOK)
        cv_gpad = r(4 * (TOK + CONV_B - 1), "p (m t) -> p m t", m=4)
        cv_g = r(4 * TOK, "p (m t) -> p m t", m=4)
        cv_sq = r(4 * TOK, "p (m t) -> p m t", m=4)
        cv_a = r(3 * 4 * TOK, "p (c m t) -> p c m t", c=3, m=4)
        cv_apad = r(4 * (TOK + CONV_A - 1), "p (m t) -> p m t", m=4)
        cv_y = r(4 * TOK, "p (m t) -> p m t", m=4)
        cv_rstd = r(TOK)

        r = Region()
        pick = r(2 * 2 * SLOTS, "p (t e s) -> p t e s", t=2, e=2)
        pick_w = r(2 * 2 * SLOTS, "p (t e s) -> p t e s", t=2, e=2)
        back = r(TOK)
        xg = r(KT * P, "p (k s) -> p k s", k=KT)
        sg = r(2 * 4 * SLOTS, "p (e c) -> p e c", e=2)
        hid = r(4 * P, "p (k s) -> p k s", k=4)
        yg = r(D)

        r = Region()
        sk_mixT = r(KT * TOK, "p (k t) -> p k t", k=KT)
        sk_qk = r(2 * KT * TOK, "p (k t) -> p k t", k=2 * KT)
        sk_v = r(2 * D, "p (t c) -> p t c", t=2)
        sk_az = r(2 * HEAD_COLS, "p (b c) -> p b c", b=2)
        sk_e = r(2 * HEAD_COLS, "p (b c) -> p b c", b=2)
        sk_l = r(2 * HEAD_COLS, "p (b c) -> p b c", b=2)
        sk_sp = r(2 * HEAD_COLS, "p (b c) -> p b c", b=2)
        sk_spm = r(2 * HEAD_COLS, "p (b c) -> p b c", b=2)
        sk_arg = r(2 * HEAD_COLS, "p (b c) -> p b c", b=2)
        sk_d = r(2 * HEAD_COLS, "p (b c) -> p b c", b=2)
        sk_a = r(2 * HEAD_COLS, "p (b c) -> p b c", b=2)

        xa = arena[:, 0:16 * TOK].rearrange("p (m t) -> p m t", m=16)
        mixT12 = arena[:, 0:12 * TOK].rearrange("p (k t) -> p k t", k=12)
        r = Region(4096)
        ss_z = r(2 * D, "p (t c) -> p t c", t=2)
        ss_pad = r(2 * 4 * (TOK + 3), "p (b m t) -> p b m t", b=2, m=4)
        ss_x = r(2 * D, "p (t c) -> p t c", t=2)
        ss_cb = r(4 * HEAD_COLS, "p (g c) -> p g c", g=4)
        ss_arg = r(2 * HEAD_COLS, "p (b c) -> p b c", b=2)
        ss_m = r(2 * HEAD_COLS, "p (b c) -> p b c", b=2)
        ss_y = r(2 * D, "p (t c) -> p t c", t=2)
        ss_s = r(400)
        dt_v = [ss_s[:, 32 * n:32 * n + 32].rearrange("p (t h) -> p t h", t=2) for n in range(8)]
        ss_ss = ss_s[:, 256:264]

        at_pT = arena[:, 3072:3072 + 2 * HEAD_COLS].rearrange("p (h c) -> p h c", h=2)
        r = Region(4096)
        at_qk = r(2 * D, "p (t c) -> p t c", t=2)
        at_w = r(2 * D)
        at_sq = at_w.rearrange("p (t c) -> p t c", t=2)
        at_rope = at_w[:, 0:D].rearrange("p (n t h j) -> p n t h j", n=4, t=2, h=16)
        at_sm = at_w[:, 0:4 * HEAD_COLS].rearrange("p (b h c) -> p b h c", b=2, h=2)
        at_qkT = r(KT * TOK, "p (k t) -> p k t", k=KT)
        at_v = r(2 * 512, "p (t c) -> p t c", t=2)
        at_o_words = r(4 * D)
        at_o = at_o_words[:, 0:3 * D].rearrange("p (g t c) -> p g t c", g=3, t=2)
        at_g4 = at_o_words[:, 3 * D:4 * D].rearrange("p (t c) -> p t c", t=2)
        at_g5 = at_o_words[:, 2 * D:4 * D].rearrange("p (t c) -> p t c", t=2)
        at_stat = r(260)
        at_p = ln_w[:, 0:4 * HEAD_COLS].rearrange("p (b h c) -> p b h c", b=2, h=2)
        at_h = at_qk
        junk = lnr

        def stat(n0, n, **dims):
            return at_stat[:, n0:n0 + n].rearrange(
                "p (g t h) -> p g t h" if "g" in dims else "p (t h) -> p t h", **dims)

        at_ss = stat(0, 32, t=2)
        at_mx, at_nmx = stat(32, 16, t=2), stat(48, 16, t=2)
        at_den, at_rden = stat(64, 16, t=2), stat(80, 16, t=2)
        at_lse, at_lw = stat(96, 48, g=3, t=2), stat(144, 48, g=3, t=2)
        at_lm, at_ls = stat(192, 16, t=2), stat(208, 16, t=2)

        def layer_no(stage):
            return sum(s in on for s in (MOE0, MOE1) if s <= stage)

        def g_no(n):
            return n if SSD in on else n - 3

        def qk_turn(n):
            return f"qk{n if SSD in on else n + 3}"

        def cols(w, c0, n=512):
            return w.rearrange("(k p) n -> p k n", p=P)[:, :, c0:c0 + n]

        def rows(w, c):
            return w[c * 512:(c + 1) * 512, :].rearrange("(k p) n -> p k n", p=P)

        up_v = a["expert_w_up"].rearrange("l e (k p) n -> l e p k n", p=P)
        down_v = a["expert_w_down"].rearrange("l e (k p) n -> l e p k n", p=P)
        out_v = out[0].rearrange("(t p) c -> p t c", p=P)

        def streamed(stage):
            if stage == CONV:
                w = a["even_w_in"][0]
                return [(8, cols(w, c)) for c in (2048, 1536, 512, 1024, 0)] + \
                    [(4, rows(a["even_w_out"][0], c)) for c in range(2)]
            if stage == STICK:
                return [(8, cols(a["odd_w_qkv"][0], 512 * c)) for c in range(6)] + \
                    [(4, rows(a["odd_w_o"][0], c)) for c in range(2)]
            if stage == SSD:
                w = a["even_w_in_2"][0]
                xbc = [1024 + 512 * c for c in range(4)]
                qkv = [q0 + 512 * g for g in range(3) for q0 in (3088, 6160, 4624)]
                return [(8, cols(w, c)) for c in xbc + [0, 512] + qkv + [7696]] + \
                    [(4, rows(a["even_w_out_2"][0], c)) for c in range(3)]
            w = a["odd_w_in_2"][0]
            return [(8, cols(w, q0 + 512 * g)) for g in range(2) for q0 in (0, 2048, 1024)] + \
                [(8, cols(w, 3072 + 512 * c)) for c in range(2)] + \
                [(4, rows(a["odd_w_out_2"][0], c)) for c in range(2)]

        block = ctx.enter_context(nc.Block())

        @block.sync
        def _(sp):
            sp.dma_start(x, a["x"][0].rearrange("(t p) c -> p t c", p=P)).then_inc(x_in, 16)

            def load(g, wide, src):
                if g >= RING:
                    sp.wait_ge(chunk_done, g - RING + 1)
                dst = (slot8 if wide == 8 else slot4)[g % RING]
                sp.dma_start(dst, src).then_inc(w_in[g % RING], 16)

            def expert_chunk(layer, pair, j):
                if j < 4:
                    return 8, up_v[layer, 2 * pair + j // 2, :, :, (j % 2) * FFN:(j % 2 + 1) * FFN]
                return 4, down_v[layer, 2 * pair + j - 4]

            def experts(stage, layer):
                b0 = base[stage]
                for j in range(6):
                    load(b0 + j, *expert_chunk(layer, 0, j))
                with sp.Fori(1, PAIRS) as i:
                    for j in range(6):
                        g = b0 + j
                        sp.wait_ge(chunk_done, i * 6 + (g - RING + 1))
                        wide, src = expert_chunk(layer, i, j)
                        sp.dma_start((slot8 if wide == 8 else slot4)[g % RING], src)\
                            .then_inc(w_in[g % RING], 16)
                sp.wait_ge(sem(f"m{layer}_counted"), 1)
                n = sp.value_load(cnt_i[0:1, :], min_val=0, max_val=TOK)
                with sp.If(n > SLOTS):
                    sp.wait_ge(chunk_done, b0 + 6 * PAIRS)

                    def pair(i):
                        for j in range(6):
                            wide, src = expert_chunk(layer, i, j)
                            sp.dma_start((slot8 if wide == 8 else slot4)[(b0 + j) % RING], src)\
                                .then_inc(sem(f"m{layer}_more_in"), 16)

                    pair(0)
                    for rnd in range(ROUNDS - 1):
                        with sp.Fori(0 if rnd else 1, PAIRS) as i:
                            sp.wait_ge(sem(f"m{layer}_more_scattered"), i + rnd * PAIRS)
                            pair(i)
                    sp.wait_ge(sem(f"m{layer}_more_scattered"), (ROUNDS - 1) * PAIRS)

            for stage in on:
                if stage in (MOE0, MOE1):
                    experts(stage, stage // 2)
                else:
                    for n, (wide, src) in enumerate(streamed(stage)):
                        load(base[stage] + n, wide, src)
            sp.wait_ge(x_ready, len(on))
            sp.dma_start(out_v, x).then_inc(sem("out_stored"), 16)
            sp.wait_ge(sem("out_stored"), 16)

        @block.gpsimd
        def _(pool):
            pool.wait_ge(const_in, 32)
            for n, stage in enumerate(on):
                if stage <= MOE1:
                    kind = "ffn" if stage % 2 else "mix"
                    if n:
                        pool.wait_ge(x_ready, n)
                    for k, v in enumerate((a[f"ln_{kind}_g"], a[f"ln_{kind}_b"])):
                        pool.dma_start(lnr[:, k, :], v[stage // 2:stage // 2 + 1, :]
                                       .broadcast_to([P, D])).then_inc(ln_in, 16)
                if stage == STICK:
                    for h in range(SB_HEADS):
                        pool.wait_ge(sem("sk_sp"), h + 1)
                        if h >= 2:
                            pool.wait_ge(sem("sk_later"), h - 1)
                        pool.tensor_tensor(sk_spm[:, h % 2, :], sk_sp[:, h % 2, :],
                                           C("stick_mul"), ALU.mult).then_inc(sem("sk_spm"), 1)

        @block.tensor
        def _(pe):
            def transposes(name, src):
                for b in range(4):
                    t, kk = b // 2, b % 2
                    for j in range(4):
                        k = 4 * kk + j
                        ins = pe.transpose(bank(b)[:, j * P:(j + 1) * P],
                                           src[:, t, k * P:(k + 1) * P], ident)
                    ins.then_inc(transposed, 1)

            def wait_T(name):
                pe.wait_ge(moved_T, 4 * (turn[name] + 1))

            def channels(g, b0):
                arrive(pe, g)
                w = slot8[g % RING]
                for m in range(4):
                    o = ps[:, b0 + m // 2, (m % 2) * TOK:(m % 2 + 1) * TOK]
                    for k in range(KT):
                        ins = pe.matmul(o, w[:, k, m * P:(m + 1) * P], xT[:, k, :],
                                        start=(k == 0), stop=(k == KT - 1))
                ins.then_inc(chunk_done, 1)

            def tokens(g, b0):
                arrive(pe, g)
                w = slot8[g % RING]
                for t in range(2):
                    for k in range(KT):
                        ins = pe.matmul(bank(b0 + t), xT[:, k, t * P:(t + 1) * P], w[:, k, :],
                                        start=(k == 0), stop=(k == KT - 1))
                ins.then_inc(chunk_done, 1)

            def residual(scale):
                for t in range(2):
                    for n in range(2):
                        pe.matmul(bank(2 * t + n), scale, x[:, t, n * 512:(n + 1) * 512],
                                  start=True, stop=False, skip_group_check=True)

            def output(g0, n_chunks, mixT, scale):
                residual(scale)
                for c in range(n_chunks):
                    arrive(pe, g0 + c)
                    w = slot4[(g0 + c) % RING]
                    for t in range(2):
                        for n in range(2):
                            for k in range(4):
                                ins = pe.matmul(
                                    bank(2 * t + n), mixT[:, 4 * c + k, t * P:(t + 1) * P],
                                    w[:, k, n * 512:(n + 1) * 512], start=False,
                                    stop=(c == n_chunks - 1 and k == 3), skip_group_check=True)
                    ins.then_inc(chunk_done, 1)

            def conv_mixers():
                g = base[CONV]
                wait_x(pe, CONV)
                transposes("x0", x)
                wait_T("x0")
                channels(g, 4)
                channels(g + 1, 6)
                pe.wait_ge(sem("cv_sig"), 1)
                channels(g + 2, 4)
                pe.wait_ge(sem("cv_gated"), 1)
                channels(g + 3, 6)
                pe.wait_ge(sem("cv_a_out"), 1)
                channels(g + 4, 4)
                pe.wait_ge(sem("cv_convolved"), 1)
                for m in range(4):
                    ins = pe.matmul(ps[:, 0, 0:TOK], C("mean"), cv_g[:, m, :],
                                    start=(m == 0), stop=(m == 3))
                ins.then_inc(sem("cv_mean"), 1)
                pe.wait_ge(sem("cv_squared"), 1)
                for m in range(4):
                    ins = pe.matmul(ps[:, 1, 0:TOK], C("mean"), cv_sq[:, m, :],
                                    start=(m == 0), stop=(m == 3))
                ins.then_inc(sem("cv_var"), 1)
                pe.wait_ge(sem("cv_mixed"), 4)
                pe.wait_ge(sem("cv_ya"), 1)
                output(g + 5, 2, cv_mixT, C("alpha"))

            def moe_round(tag, rnd, first_g, chunk, arrived):
                def s(name):
                    return sem(f"{tag}_{name}")

                def gather(half):
                    for k in range(4):
                        for t in range(2):
                            kk = 4 * half + k
                            ins = pe.matmul(ps[:, 6 + half, k * P:(k + 1) * P],
                                            x[:, t, kk * P:(kk + 1) * P],
                                            pick[:, t].rearrange("p e s -> p (e s)"),
                                            start=(t == 0), stop=(t == 1))
                    ins.then_inc(s("gathered"), 1)

                n1, n2 = (PAIRS + 1) * rnd, PAIRS * rnd
                pe.wait_ge(s("picked"), n1 + 1)
                gather(1)
                gather(0)
                with pe.Fori(0, PAIRS) as i:
                    pe.wait_ge(s("xg_moved"), i * 2 + (2 * n1 + 2))
                    for e in range(2):
                        for half in range(2):
                            j = 2 * e + half
                            arrived(pe, i, j)
                            w = slot8[(first_g + j) % RING]
                            for m in range(4):
                                c = (4 * half + m) * SLOTS
                                for k in range(KT):
                                    ins = pe.matmul(ps[:, 4 + e, c:c + SLOTS],
                                                    w[:, k, m * P:(m + 1) * P],
                                                    xg[:, k, e * SLOTS:(e + 1) * SLOTS],
                                                    start=(k == 0), stop=(k == KT - 1))
                            ins.then_inc(chunk, 1)
                    pe.wait_ge(s("weighted"), i + (n2 + 1))
                    for t in range(2):
                        ins = pe.transpose(ps[:, 6, t * P:(t + 1) * P],
                                           pick_w[:, t].rearrange("p e s -> p (e s)"), ident)
                    ins.then_inc(s("turned"), 1)
                    pe.wait_ge(s("picked"), i + (n1 + 2))
                    gather(1)
                    pe.wait_ge(s("back_moved"), i + (n2 + 1))
                    gather(0)
                    pe.wait_ge(s("hidden"), i * 2 + (2 * n2 + 2))
                    for e in range(2):
                        arrived(pe, i, 4 + e)
                        w = slot4[(first_g + 4 + e) % RING]
                        for n in range(2):
                            for k in range(4):
                                ins = pe.matmul(ps[e * SLOTS:(e + 1) * SLOTS, 4 + n, :],
                                                hid[:, k, e * SLOTS:(e + 1) * SLOTS],
                                                w[:, k, n * 512:(n + 1) * 512],
                                                start=(k == 0), stop=(k == 3))
                        ins.then_inc(chunk, 1)
                    pe.wait_ge(s("yg_moved"), i * 2 + (2 * n2 + 2))
                    for t in range(2):
                        for n in range(2):
                            ins = pe.matmul(bank(2 * t + n), back[:, t * P:(t + 1) * P],
                                            yg[:, n * 512:(n + 1) * 512], start=False,
                                            stop=False, skip_group_check=True)
                    ins.then_inc(s("scattered"), 1)

            def experts(stage, layer):
                wait_x(pe, stage)
                transposes(f"x{stage}", x)
                wait_T(f"x{stage}")
                rw = Q("router_w").rearrange("p (l k n) -> p l k n", l=2, k=KT)
                for t in range(2):
                    for k in range(KT):
                        ins = pe.matmul(ps[:, 4, t * 36:(t + 1) * 36], xT[:, k, t * P:(t + 1) * P],
                                        rw[:, layer, k, :], start=(k == 0), stop=(k == KT - 1))
                ins.then_inc(sem("logits"), 1)
                residual(C("alpha"))
                pe.wait_ge(sem("chosen"), layer_no(stage))
                pe.matmul(ps[:, 5, 0:32], C("before"), s32[:, 0, :], start=True, stop=True)
                pe.matmul(ps[:, 5, 32:64], ones, s32[:, 0, :], start=True, stop=False)
                pe.matmul(ps[:, 5, 32:64], C("before"), s32[:, 1, :], start=False, stop=True)
                pe.matmul(ps[:, 5, 64:96], ones, s32[:, 0, :], start=True, stop=False)
                pe.matmul(ps[:, 5, 64:96], ones, s32[:, 1, :], start=False, stop=True)\
                    .then_inc(sem("ranked"), 1)
                b0 = base[stage]

                def arrived(eng, i, j):
                    g = b0 + j
                    eng.wait_ge(w_in[g % RING], i * 16 + 16 * (g // RING + 1))

                moe_round(f"m{layer}", 0, b0, chunk_done, arrived)
                pe.wait_ge(sem(f"m{layer}_counted"), 1)
                n = pe.value_load(cnt_i[0:1, :], min_val=0, max_val=TOK)
                with pe.If(n > SLOTS):
                    for rnd in range(ROUNDS - 1):
                        def more(eng, i, j):
                            if j == 0:
                                eng.wait_ge(sem(f"m{layer}_more_in"),
                                            i * 96 + 96 * (rnd * PAIRS + 1))
                        moe_round(f"m{layer}_more", rnd, b0, sem(f"m{layer}_more_chunk"), more)

            def stick_breaking():
                g = base[STICK]
                wait_x(pe, STICK)
                transposes("x2", x)
                wait_T("x2")
                for c in range(4):
                    if c >= 2:
                        pe.wait_ge(sem("sk_qk"), c - 1)
                    channels(g + c, 4 + 2 * (c % 2))
                for c in range(2):
                    pe.wait_ge(sem("sk_qk"), 3 + c)
                    tokens(g + 4 + c, 4 + 2 * c)
                pe.wait_ge(sem("sk_v"), 2)

                def z(h):
                    if h >= 2:
                        pe.wait_ge(sem("sk_arg"), h - 1)
                    p0 = 64 * (h % 2)
                    q = sk_qk[p0:p0 + 64, h // 2, :]
                    k = sk_qk[p0:p0 + 64, KT + h // 2, :]
                    pe.matmul(ps[:, h % 2, 0:TOK], k[:, 0:P], q, start=True, stop=True)
                    pe.matmul(ps[:, h % 2, TOK:HEAD_COLS], k[:, P:TOK], q[:, P:TOK],
                              start=True, stop=True).then_inc(sem("sk_z"), 1)

                def later(h):
                    pe.wait_ge(sem("sk_spm"), h + 1)
                    b, m = 2 + h % 2, sk_spm[:, h % 2, :]
                    pe.matmul(ps[:, b, 0:TOK], C("from_on"), m[:, 0:TOK], start=True, stop=False,
                              skip_group_check=True)
                    pe.matmul(ps[:, b, P:TOK], ones, m[:, TOK:HEAD_COLS], start=False, stop=True,
                              skip_group_check=True)
                    pe.matmul(ps[:, b, TOK:HEAD_COLS], C("from_on"), m[:, TOK:HEAD_COLS],
                              start=True, stop=True).then_inc(sem("sk_later"), 1)

                def mix(h):
                    pe.wait_ge(sem("sk_a"), h + 1)
                    if h >= 4 and h % 2 == 0:
                        pe.wait_ge(sem("sk_oT"), h // 2 - 1)
                    p0, b, w = 64 * (h % 2), 4 + (h // 2) % 2, sk_a[:, h % 2, :]
                    pe.matmul(ps[p0:p0 + 64, b, 0:TOK], sk_v[:, 0, h * 64:(h + 1) * 64],
                              w[:, 0:TOK], start=True, stop=False, skip_group_check=True)
                    pe.matmul(ps[p0:p0 + 64, b, P:TOK], sk_v[:, 1, h * 64:(h + 1) * 64],
                              w[:, TOK:HEAD_COLS], start=False, stop=True,
                              skip_group_check=True).then_inc(sem("sk_o"), 1)

                for n in range(SB_HEADS + 3):
                    if n < SB_HEADS:
                        z(n)
                    if 1 <= n <= SB_HEADS:
                        later(n - 1)
                    if n >= 3:
                        mix(n - 3)
                pe.wait_ge(sem("sk_oT"), KT)
                output(g + 6, 2, sk_mixT, C("alpha"))

            def attention(grp, g):
                if grp:
                    pe.wait_ge(sem("at_pT_moved"), 8 * grp)
                tokens(g, 4)
                tokens(g + 1, 2)
                if grp:
                    pe.wait_ge(sem("at_o_moved"), grp)
                tokens(g + 2, 6)
                pe.wait_ge(sem("at_v"), grp + 1)
                pe.wait_ge(sem("at_qk"), grp + 1)
                transposes(qk_turn(grp), at_qk)
                wait_T(qk_turn(grp))

                def scores(pr):
                    n = 4 * grp + pr
                    if pr >= 2:
                        pe.wait_ge(sem("at_masked"), n - 1)
                    for hh in range(2):
                        h = 2 * pr + hh
                        p0, b = 64 * hh, 2 * (pr % 2) + hh
                        q = at_qkT[p0:p0 + 64, h // 2, :]
                        k = at_qkT[p0:p0 + 64, 4 + h // 2, :]
                        pe.matmul(ps[:, b, 0:P], q[:, 0:P], k[:, 0:P], start=True, stop=True)
                        ins = pe.matmul(ps[:, b, P:HEAD_COLS], q[:, P:TOK], k, start=True,
                                        stop=True)
                    ins.then_inc(sem("at_scored"), 1)

                def turn_p(pr):
                    n = 4 * grp + pr
                    pe.wait_ge(sem("at_p"), 4 * (n + 1))
                    if pr:
                        pe.wait_ge(sem("at_pT_moved"), 2 * n)
                    for hh in range(2):
                        for c in range(3):
                            ins = pe.transpose(ps[:, 4 + hh, c * P:(c + 1) * P],
                                               at_p[:, pr % 2, hh, c * P:(c + 1) * P], ident)
                    ins.then_inc(sem("at_turned"), 1)

                def mix(pr):
                    n = 4 * grp + pr
                    pe.wait_ge(sem("at_pT_moved"), 2 * (n + 1))
                    for hh in range(2):
                        h = 2 * pr + hh
                        c = slice(h * 64, (h + 1) * 64)
                        w = at_pT[:, hh, :]
                        pe.matmul(ps[:, 6, c], w[:, 0:P], at_v[:, 0, c], start=True, stop=True)
                        pe.matmul(ps[:, 7, c], w[:, P:TOK], at_v[:, 0, c], start=True,
                                  stop=False)
                        ins = pe.matmul(ps[:, 7, c], w[:, TOK:HEAD_COLS], at_v[:, 1, c],
                                        start=False, stop=True)
                    ins.then_inc(sem("at_mixed"), 1)

                for n in range(6):
                    if n >= 2:
                        mix(n - 2)
                    if n < 4:
                        scores(n)
                    if 1 <= n <= 4:
                        turn_p(n - 1)

            def ssd_dilated():
                g = base[SSD]
                pe.wait_ge(sem("h_ready"), 1)
                transposes("h4", at_h)
                wait_T("h4")
                dw = Q("dt_w").rearrange("p (k n) -> p k n", k=KT)
                for t in range(2):
                    for k in range(KT):
                        ins = pe.matmul(ps[:, 0, t * 16:(t + 1) * 16], xT[:, k, t * P:(t + 1) * P],
                                        dw[:, k, :], start=(k == 0), stop=(k == KT - 1))
                ins.then_inc(sem("ss_dt"), 1)
                for c in range(4):
                    if c >= 2:
                        pe.wait_ge(sem("ss_taken"), 8 * (c - 1))
                    channels(g + c, 4 + 2 * (c % 2))
                pe.wait_ge(sem("ss_a"), 1)
                av = dt_v[5]
                pe.matmul(ps[:, 1, 0:16], C("upto"), av[:, 0, :], start=True, stop=True)
                pe.matmul(ps[:, 1, 16:32], ones, av[:, 0, :], start=True, stop=False)
                pe.matmul(ps[:, 1, 16:32], C("upto"), av[:, 1, :], start=False, stop=True)\
                    .then_inc(sem("ss_cs"), 1)
                for c in range(2):
                    pe.wait_ge(sem("ss_taken"), 8 * (3 + c))
                    tokens(g + 4 + c, 4 + 2 * c)
                for u in range(4):
                    pe.wait_ge(sem("ss_silu"), 4 * (u % 2 + 1))
                    if u >= 2:
                        pe.wait_ge(sem("ss_x"), u - 1)
                    for j in range(4):
                        ins = pe.transpose(bank(2 + u % 2)[:, j * P:(j + 1) * P],
                                           xa[:, 4 * (u % 2) + j, (u // 2) * P:(u // 2 + 1) * P],
                                           ident)
                    ins.then_inc(sem("ss_turned"), 1)
                pe.wait_ge(sem("ss_silu"), 16)
                pe.wait_ge(sem("ss_z"), 2)
                for q in range(4):
                    B, Cc = xa[:, 8 + q, :], xa[:, 12 + q, :]
                    pe.matmul(ps[:, 4 + q, 0:TOK], B[:, 0:P], Cc, start=True, stop=True)
                    pe.matmul(ps[:, 4 + q, TOK:HEAD_COLS], B[:, P:TOK], Cc[:, P:TOK],
                              start=True, stop=True).then_inc(sem("ss_bc"), 1)
                pe.wait_ge(sem("ss_x"), 4)
                pe.wait_ge(sem("ss_xdt"), 1)
                pe.wait_ge(sem("ss_cb"), 4)

                def run_sum(h):
                    if h >= 2:
                        pe.wait_ge(sem("ss_arg"), 2 * (h - 1))
                    o = ps[:, 4 + h % 2, 0:TOK]
                    pe.matmul(o, av[:, 0, h:h + 1].broadcast_to([P, P]),
                              con[:, CONST["upto"][0]:CONST["ones"][1]], start=True, stop=False,
                              skip_group_check=True)
                    pe.matmul(ps[:, 4 + h % 2, P:TOK], av[:, 1, h:h + 1].broadcast_to([P, P]),
                              C("upto"), start=False, stop=True,
                              skip_group_check=True).then_inc(sem("ss_sum"), 1)

                def y(h):
                    pe.wait_ge(sem("ss_m"), h + 1)
                    m, b, c = ss_m[:, h % 2, :], h // 8, (h % 8) * 64
                    xh = [ss_x[:, t, h * 64:(h + 1) * 64] for t in range(2)]
                    pe.matmul(ps[:, b, c:c + 64], m[:, 0:P], xh[0], start=True, stop=True)
                    pe.matmul(ps[:, 2 + b, c:c + 64], m[:, P:TOK], xh[0], start=True, stop=False)
                    pe.matmul(ps[:, 2 + b, c:c + 64], m[:, TOK:HEAD_COLS], xh[1], start=False,
                              stop=True).then_inc(sem("ss_yh"), 1)

                for n in range(SSD_HEADS + 2):
                    if n >= 2:
                        y(n - 2)
                    if n < SSD_HEADS:
                        run_sum(n)
                pe.wait_ge(sem("ss_y"), 1)
                transposes("y4", ss_y)
                wait_T("y4")
                for grp in range(3):
                    attention(grp, g + 6 + 3 * grp)
                pe.wait_ge(sem("at_pT_moved"), 24)
                tokens(g + 15, 4)
                pe.wait_ge(sem("at_gated"), 1)
                for t in range(2):
                    for j in range(4):
                        ins = pe.transpose(bank(t)[:, j * P:(j + 1) * P],
                                           at_o[:, 0, t, j * P:(j + 1) * P], ident)
                    ins.then_inc(sem("at_turned_o"), 1)
                pe.wait_ge(sem("at_mixT"), 2)
                output(g + 16, 3, mixT12, ident)

            def block_attention():
                g = base[MOBA]
                pe.wait_ge(sem("h_ready"), 2 if first <= SSD else 1)
                transposes("h5", at_h)
                wait_T("h5")
                for grp in range(2):
                    attention(g_no(3 + grp), g + 3 * grp)
                pe.wait_ge(sem("at_pT_moved"), 8 * (g_no(4) + 1))
                tokens(g + 6, 4)
                tokens(g + 7, 2)
                pe.wait_ge(sem("at_gated"), 2 if first <= SSD else 1)
                o_turns = 2 if first <= SSD else 0
                for t in range(2):
                    for kk in range(2):
                        for j in range(4):
                            ins = pe.transpose(bank(2 * t + kk)[:, j * P:(j + 1) * P],
                                               at_o[:, kk, t, j * P:(j + 1) * P], ident)
                        ins.then_inc(sem("at_turned_o"), 1)
                pe.wait_ge(sem("at_mixT"), o_turns + 4)
                output(g + 8, 2, mixT12, ident)

            pe.wait_ge(const_in, 32)
            run = {CONV: conv_mixers, MOE0: lambda: experts(MOE0, 0), STICK: stick_breaking,
                   MOE1: lambda: experts(MOE1, 1), SSD: ssd_dilated, MOBA: block_attention}
            for stage in on:
                run[stage]()

        @block.scalar
        def _(act):
            step = Steps(act, "act_step")
            roots = [0]

            def move_T(name, dst, scale=1.0):
                for b in (0, 2):
                    act.wait_ge(transposed, 4 * turn[name] + b + 1)
                    act.activation(dst[:, 0:4, (b // 2) * P:(b // 2 + 1) * P],
                                   bank(b).rearrange("p (k c) -> p k c", k=4), ACT.Copy,
                                   scale=scale).then_inc(moved_T, 1)

            def done(g):
                act.wait_ge(chunk_done, g + 1)

            def root(n):
                roots[0] += 1
                act.wait_ge(sem("squares"), roots[0])
                y = root_w[:, TOK:TOK + n]
                step.run(act.activation(y, root_w[:, 0:n], ACT.Ln))
                act.activation(y, y, ACT.Exp, scale=-0.5).then_inc(sem("roots"), 1)

            def two_banks(b):
                return ps[:, b:b + 2, :]

            def conv_mixers():
                g = base[CONV]
                move_T("x0", xT)
                done(g)
                act.activation(cv_sig.rearrange("p (b c) -> p b c", b=2), two_banks(4),
                               ACT.Sigmoid).then_inc(sem("cv_sig"), 1)
                for c in range(3):
                    done(g + 2 + c)
                    act.activation(cv_a[:, c].rearrange("p (b m) t -> p b (m t)", b=2),
                                   two_banks(4 + 2 * (c % 2)), ACT.Copy)\
                        .then_inc(sem("cv_a_out"), 1)
                root(TOK)
                act.wait_ge(sem("cv_normed"), 1)
                for m in range(4):
                    act.activation(cv_mixT[:, 4 + m, :], cv_g[:, m, :], ACT.Silu,
                                   bias=Q("norm_b")[:, m:m + 1], scale=Q("norm_g")[:, m:m + 1])\
                        .then_inc(sem("cv_mixed"), 1)
                root(2)

            def moe_round(tag, rnd, chunk, first_chunk):
                def s(name):
                    return sem(f"{tag}_{name}")

                n1, n2 = (PAIRS + 1) * rnd, PAIRS * rnd

                def move_xg(count):
                    act.wait_ge(s("gathered"), count)
                    act.activation(xg[:, 4:8, :], ps[:, 7, :].rearrange("p (k s) -> p k s", k=4),
                                   ACT.Copy).then_inc(s("xg_moved"), 1)

                move_xg(2 * n1 + 1)
                with act.Fori(0, PAIRS) as i:
                    for e in range(2):
                        act.wait_ge(chunk, i * 6 + (first_chunk + 2 * e + 2))
                        act.activation(sg[:, e, :], ps[:, 4 + e, 0:4 * SLOTS], ACT.Silu)\
                            .then_inc(s("silu"), 1)
                    act.wait_ge(s("turned"), i + (n2 + 1))
                    act.activation(back, ps[:, 6, 0:TOK], ACT.Copy).then_inc(s("back_moved"), 1)
                    move_xg(i * 2 + (2 * n1 + 3))
                    act.wait_ge(chunk, i * 6 + (first_chunk + 6))
                    act.activation(yg[:, 0:512], bank(4), ACT.Copy).then_inc(s("yg_moved"), 1)

            def experts(stage, layer):
                move_T(f"x{stage}", xT)
                act.wait_ge(sem("shifted"), layer_no(stage))
                act.activation(ge, ge_m, ACT.Exp).then_inc(sem("g_exp"), 1)
                act.wait_ge(sem("gap"), layer_no(stage))
                act.activation(dexp[:, :, 0], gap, ACT.Exp).then_inc(sem("d_exp"), 1)
                moe_round(f"m{layer}", 0, chunk_done, base[stage])
                act.wait_ge(sem(f"m{layer}_counted"), 1)
                n = act.value_load(cnt_i[0:1, :], min_val=0, max_val=TOK)
                with act.If(n > SLOTS):
                    for rnd in range(ROUNDS - 1):
                        moe_round(f"m{layer}_more", rnd, sem(f"m{layer}_more_chunk"),
                                  6 * PAIRS * rnd)
                root(2)

            def stick_breaking():
                g = base[STICK]
                move_T("x2", xT)
                for c in range(4):
                    done(g + c)
                    act.activation(sk_qk[:, 4 * c:4 * c + 4].rearrange("p (b m) t -> p b (m t)", b=2),
                                   two_banks(4 + 2 * (c % 2)), ACT.Copy,
                                   scale=0.125 if c < 2 else 1.0).then_inc(sem("sk_qk"), 1)
                for c in range(2):
                    done(g + 4 + c)
                    act.activation(sk_v[:, :, c * 512:(c + 1) * 512], two_banks(4 + 2 * c),
                                   ACT.Copy).then_inc(sem("sk_v"), 1)

                def soft(h):
                    act.wait_ge(sem("sk_z"), h + 1)
                    step.run(act.activation(sk_az[:, h % 2, :], ps[:, h % 2, 0:HEAD_COLS],
                                            ACT.Abs))
                    step.run(act.activation(sk_e[:, h % 2, :], sk_az[:, h % 2, :], ACT.Exp,
                                            scale=-1.0))
                    if h >= 2:
                        act.wait_ge(sem("sk_sp"), h - 1)
                    act.activation(sk_l[:, h % 2, :], sk_e[:, h % 2, :], ACT.Ln,
                                   bias=ones[:, 0:1]).then_inc(sem("sk_l"), 1)

                def weights(h):
                    act.wait_ge(sem("sk_arg"), h + 1)
                    if h >= 2:
                        act.wait_ge(sem("sk_o"), h - 1)
                    act.activation(sk_a[:, h % 2, :], sk_arg[:, h % 2, :], ACT.Exp)\
                        .then_inc(sem("sk_a"), 1)

                def move_o(pr):
                    act.wait_ge(sem("sk_o"), 2 * pr + 2)
                    act.activation(sk_mixT[:, pr, :], ps[:, 4 + pr % 2, 0:TOK], ACT.Copy)\
                        .then_inc(sem("sk_oT"), 1)

                for n in range(SB_HEADS + 4):
                    if 2 <= n < SB_HEADS + 2:
                        weights(n - 2)
                    if n < SB_HEADS:
                        soft(n)
                    if n >= 4 and n % 2 == 1:
                        move_o((n - 5) // 2)
                root(2)

            def attention(grp, g, lse):
                def squares(n, b):
                    act.wait_ge(chunk_done, n + 1)
                    return act.activation(at_sq[:, :, 512 * (b == 6):512 * (b == 6) + 512],
                                          two_banks(b), ACT.Square).then_inc(sem("at_sq"), 1)

                if grp:
                    act.wait_ge(sem("at_masked"), 4 * grp)
                squares(g, 4)
                act.wait_ge(chunk_done, g + 2)
                act.activation(at_v, two_banks(2), ACT.Copy).then_inc(sem("at_v"), 1)
                squares(g + 2, 6)
                root(32)
                move_T(qk_turn(grp), at_qkT, 0.125)

                def exps(pr):
                    n = 4 * grp + pr
                    act.wait_ge(sem("at_max"), n + 1)
                    for hh in range(2):
                        for t in range(2):
                            h = 2 * pr + hh
                            c = slice(0, P) if t == 0 else slice(P, HEAD_COLS)
                            act.activation(at_p[:, pr % 2, hh, c], at_sm[:, pr % 2, hh, c], ACT.Exp,
                                           bias=at_nmx[:, t, h:h + 1],
                                           accum_out=at_den[:, t, h:h + 1])\
                                .then_inc(sem("at_p"), 1)

                def move_pT(pr):
                    n = 4 * grp + pr
                    act.wait_ge(sem("at_turned"), n + 1)
                    if n:
                        act.wait_ge(sem("at_mixed"), n)
                    act.activation(at_pT[:, 0, :], ps[:, 4, 0:HEAD_COLS], ACT.Copy)\
                        .then_inc(sem("at_pT_moved"), 1)

                for n in range(5):
                    if n < 4:
                        exps(n)
                    if n >= 1:
                        move_pT(n - 1)
                if lse:
                    act.wait_ge(sem("at_p"), 16 * (grp + 1))
                    act.activation(at_lse[:, grp], at_den, ACT.Ln).then_inc(sem("at_lse"), 1)

            def rms(stage):
                wait_x(act, stage)
                for t in range(2):
                    act.activation(junk[:, t, :], x[:, t, :], ACT.Square,
                                   accum_out=mv[:, t, 0:1]).then_inc(sem("h_sq"), 1)
                root(2)

            def ssd_dilated():
                g = base[SSD]
                rms(SSD)
                act.wait_ge(sem("ss_dabs"), 1)
                step.run(act.activation(dt_v[2], dt_v[1], ACT.Exp, scale=-1.0))
                act.activation(dt_v[3], dt_v[2], ACT.Ln, bias=ones[:, 0:1])\
                    .then_inc(sem("ss_soft"), 1)
                act.activation(dt_v[4][:, 0, :], Q("a_log"), ACT.Exp).then_inc(sem("ss_soft"), 1)
                w, b = Q("conv2_w").rearrange("p (m k) -> p m k", k=4), Q("conv2_b")
                for c in range(4):
                    done(g + c)
                    for m in range(4):
                        src = ps[:, 4 + 2 * (c % 2) + m // 2, (m % 2) * TOK:(m % 2 + 1) * TOK]
                        k = 4 * c + m
                        if c >= 2 and m == 0:
                            act.wait_ge(sem("ss_conv"), 4 * (c - 1))
                        act.activation(ss_pad[:, c % 2, m, 3:3 + TOK], src, ACT.Copy)\
                            .then_inc(sem("ss_taken"), 1)
                        act.activation(xa[:, k, :], src, ACT.Identity, bias=b[:, k:k + 1],
                                       scale=w[:, k, 3:4]).then_inc(sem("ss_taken"), 1)
                for m in range(16):
                    act.wait_ge(sem("ss_conv"), m + 1)
                    act.activation(xa[:, m, :], xa[:, m, :], ACT.Silu).then_inc(sem("ss_silu"), 1)
                for c in range(2):
                    done(g + 4 + c)
                    act.activation(ss_z[:, :, c * 512:(c + 1) * 512], two_banks(4 + 2 * c),
                                   ACT.Silu).then_inc(sem("ss_z"), 1)
                for q in range(4):
                    act.wait_ge(sem("ss_bc"), q + 1)
                    act.activation(ss_cb[:, q, :], ps[:, 4 + q, 0:HEAD_COLS], ACT.Copy)\
                        .then_inc(sem("ss_cb"), 1)
                for h in range(SSD_HEADS):
                    act.wait_ge(sem("ss_arg"), 2 * (h + 1))
                    act.activation(ss_arg[:, h % 2, :], ss_arg[:, h % 2, :], ACT.Exp)\
                        .then_inc(sem("ss_e"), 1)
                act.wait_ge(sem("ss_gated"), 2)
                for t in range(2):
                    for q in range(4):
                        act.activation(junk[:, t, q * 256:(q + 1) * 256],
                                       ss_y[:, t, q * 256:(q + 1) * 256], ACT.Square,
                                       accum_out=ss_ss[:, 4 * t + q:4 * t + q + 1])\
                            .then_inc(sem("ss_sq"), 1)
                root(8)
                for grp in range(3):
                    attention(grp, g + 6 + 3 * grp, True)
                act.wait_ge(sem("at_lse_m"), 1)
                act.activation(at_lw, at_lse, ACT.Exp).then_inc(sem("at_lw"), 1)
                done(g + 15)
                act.activation(at_g4, two_banks(4), ACT.Silu)\
                    .then_inc(sem("at_g"), 1)

            def block_attention():
                g = base[MOBA]
                rms(MOBA)
                for grp in range(2):
                    attention(g_no(3 + grp), g + 3 * grp, False)
                for c in range(2):
                    done(g + 6 + c)
                    act.activation(at_g5[:, :, c * 512:(c + 1) * 512], two_banks(4 - 2 * c),
                                   ACT.Silu).then_inc(sem("at_g"), 1)

            act.dma_start(con[:, :], a["constants"]).then_inc(const_in, 16)
            act.dma_start(par[:, :], a["params"]).then_inc(const_in, 16)
            act.wait_ge(const_in, 32)
            run = {CONV: conv_mixers, MOE0: lambda: experts(MOE0, 0), STICK: stick_breaking,
                   MOE1: lambda: experts(MOE1, 1), SSD: ssd_dilated, MOBA: block_attention}
            for stage in on:
                run[stage]()

        @block.vector
        def _(dve):
            step = Steps(dve, "dve_step")
            mul, add, sub, eq = ALU.mult, ALU.add, ALU.subtract, ALU.is_equal
            roots = [0]

            def two_banks(b):
                return ps[:, b:b + 2, :]

            def move_T(name, dst, banks=(1, 3), column=None):
                for b in banks:
                    kk = b % 2
                    dve.wait_ge(transposed, 4 * turn[name] + b + 1)
                    o = dst[:, 4 * kk:4 * kk + 4, (b // 2) * P:(b // 2 + 1) * P]
                    i = bank(b).rearrange("p (k c) -> p k c", k=4)
                    if column is None:
                        ins = dve.tensor_copy(o, i)
                    else:
                        f = column[:, 4 * kk:4 * kk + 4].unsqueeze(2).broadcast_to([P, 4, P])
                        ins = dve.tensor_tensor(o, i, f, mul)
                    ins.then_inc(moved_T, 1)

            def inv_root(o, i, scale, eps):
                n = int(np.prod(o.shape[1:]))
                dims = {2: "p (a) -> p a", 3: "p (a b) -> p a b"}[len(o.shape)]
                size = {} if len(o.shape) == 2 else {"b": o.shape[2]}
                v, y, w = (root_w[:, TOK * q:TOK * q + n].rearrange(dims, **size)
                           for q in range(3))
                dve.tensor_scalar(v, i, scale, eps, mul, add).then_inc(sem("squares"), 1)
                roots[0] += 1
                dve.wait_ge(sem("roots"), roots[0])
                step.run(dve.tensor_tensor(w, v, y, mul))
                step.run(dve.tensor_tensor(w, w, y, mul))
                step.run(dve.tensor_scalar(w, w, -0.5, 1.5, mul, add))
                step.run(dve.tensor_tensor(o, y, w, mul))

            def layer_norm(stage):
                for t in range(2):
                    for n in range(2):
                        step.add(dve.bn_stats(stats[:, t, n, :], bank(2 * t + n)))
                step.settle()
                for t in range(2):
                    step.add(dve.bn_aggr(mv[:, t, :], stats[:, t].rearrange("p n s -> p (n s)")))
                step.settle()
                inv_root(rstd[:, :, 0], mv[:, :, 1], 1.0, LN_EPS)
                for t in range(2):
                    step.add(dve.tensor_scalar(x[:, t].rearrange("p (n c) -> p n c", n=2),
                                               two_banks(2 * t), mv[:, t, 0:1], rstd[:, t, 0:1],
                                               sub, mul))
                step.settle()
                dve.wait_ge(ln_in, 32 * (stage - first + 1))
                step.run(dve.tensor_tensor(x, x, lnr[:, 0:1, :].broadcast_to([P, 2, D]), mul))
                dve.tensor_tensor(x, x, lnr[:, 1:2, :].broadcast_to([P, 2, D]), add)\
                    .then_inc(x_ready, 1)

            def taps(src, dst, w, n, bias=None):
                for k in range(n):
                    for m in range(4):
                        if k:
                            step.settle_but(3)
                            ins = dve.scalar_tensor_tensor(
                                dst[:, m, :], src[:, m, k:k + TOK], w[:, m * n + k:m * n + k + 1],
                                dst[:, m, :], mul, add)
                        elif bias is not None:
                            ins = dve.tensor_scalar(dst[:, m, :], src[:, m, 0:TOK],
                                                    w[:, m * n:m * n + 1], bias[:, m:m + 1],
                                                    mul, add)
                        else:
                            ins = dve.tensor_scalar(dst[:, m, :], src[:, m, 0:TOK],
                                                    w[:, m * n:m * n + 1], None, mul)
                        step.add(ins)

            def conv_mixers():
                g = base[CONV]
                step.add(dve.memset(cv_gpad[:, :, 0:CONV_B - 1], 0.0))
                step.add(dve.memset(cv_apad[:, :, 0:CONV_A - 1], 0.0))
                move_T("x0", xT)
                dve.wait_ge(chunk_done, g + 2)
                dve.wait_ge(sem("cv_sig"), 1)
                dve.tensor_tensor(cv_gpad[:, :, CONV_B - 1:],
                                  two_banks(6).rearrange("p b (m t) -> p (b m) t", m=2),
                                  cv_sig.rearrange("p (m t) -> p m t", m=4), mul)\
                    .then_inc(sem("cv_gated"), 1)
                dve.wait_ge(sem("cv_gated"), 1)
                step.settle()
                taps(cv_gpad, cv_g, Q("conv_b"), CONV_B, Q("conv_bb"))
                step.settle()
                dve.sem_inc(sem("cv_convolved"), 1)
                dve.wait_ge(sem("cv_a_out"), 3)
                step.run(dve.tensor_tensor(cv_apad[:, :, CONV_A - 1:], cv_a[:, 0], cv_a[:, 1], mul))
                taps(cv_apad, cv_y, Q("conv_a"), CONV_A)
                step.settle()
                dve.tensor_tensor(cv_mixT[:, 0:4, :], cv_a[:, 2], cv_y, mul)\
                    .then_inc(sem("cv_ya"), 1)
                dve.wait_ge(sem("cv_mean"), 1)
                step.run(dve.tensor_tensor(
                    cv_g, cv_g, ps[:, 0:1, 0:TOK].broadcast_to([P, 4, TOK]), sub))
                dve.tensor_tensor(cv_sq, cv_g, cv_g, mul).then_inc(sem("cv_squared"), 1)
                dve.wait_ge(sem("cv_var"), 1)
                inv_root(cv_rstd, ps[:, 1, 0:TOK], 1.0, LN_EPS)
                dve.tensor_tensor(cv_g, cv_g, cv_rstd.unsqueeze(1).broadcast_to([P, 4, TOK]), mul)\
                    .then_inc(sem("cv_normed"), 1)
                dve.wait_ge(chunk_done, g + 7)
                layer_norm(CONV)

            def first_max(values, n, rev, vmax, one):
                tie = (tie4 if n == 4 else tie8)
                rv = rev.unsqueeze(1).broadcast_to([P, 2, n])
                step.run(dve.tensor_reduce(vmax, values, AX, ALU.max))
                step.run(dve.tensor_tensor(tie, values, vmax.unsqueeze(2).broadcast_to([P, 2, n]),
                                           eq))
                step.run(dve.tensor_tensor(tie, tie, rv, mul))
                step.run(dve.tensor_reduce(gidx, tie, AX, ALU.max))
                step.run(dve.tensor_tensor(one, rv, gidx.unsqueeze(2).broadcast_to([P, 2, n]), eq))

            def moe_round(tag, rnd, chunk, first_chunk):
                def s(name):
                    return sem(f"{tag}_{name}")

                n1, n2 = (PAIRS + 1) * rnd, PAIRS * rnd
                places = C("iota").unsqueeze(1).unsqueeze(1).broadcast_to([P, 2, 2, SLOTS])

                def choose(pair2):
                    rk = rankm[:, :, pair2].unsqueeze(3).broadcast_to([P, 2, 2, SLOTS])
                    dve.tensor_tensor(pick, places, rk, eq).then_inc(s("picked"), 1)

                def move_xg(count):
                    dve.wait_ge(s("gathered"), count)
                    dve.tensor_copy(xg[:, 0:4, :], ps[:, 6, :].rearrange("p (k s) -> p k s", k=4))\
                        .then_inc(s("xg_moved"), 1)

                choose(slice(0, 2))
                move_xg(2 * n1 + 2)
                with dve.Fori(0, PAIRS) as i:
                    dve.wait_ge(s("gathered"), i * 2 + (2 * n1 + 2))
                    wt = wt32[:, :, bass.ds(i * 2, 2)].unsqueeze(3)\
                        .broadcast_to([P, 2, 2, SLOTS])
                    dve.tensor_tensor(pick_w, pick, wt, mul).then_inc(s("weighted"), 1)
                    dve.wait_ge(s("weighted"), i + (n2 + 1))
                    choose(bass.ds(i * 2 + 2, 2))
                    for e in range(2):
                        dve.wait_ge(s("silu"), i * 2 + (2 * n2 + e + 1))
                        dve.tensor_tensor(hid[:, :, e * SLOTS:(e + 1) * SLOTS],
                                          sg[:, e].rearrange("p (k s) -> p k s", k=4),
                                          ps[:, 4 + e, 4 * SLOTS:].rearrange(
                                              "p (k s) -> p k s", k=4), mul)\
                            .then_inc(s("hidden"), 1)
                    move_xg(i * 2 + (2 * n1 + 4))
                    dve.wait_ge(chunk, i * 6 + (first_chunk + 6))
                    dve.tensor_copy(yg[:, 512:], bank(5)).then_inc(s("yg_moved"), 1)

            def experts(stage, layer):
                no = layer_no(stage)
                move_T(f"x{stage}", xT)
                dve.wait_ge(sem("logits"), no)
                rb = Q("router_b")[:, 36 * layer:36 * layer + 36]
                step.run(dve.tensor_tensor(lg, ps[:, 4, 0:72].rearrange("p (t n) -> p t n", t=2),
                                           rb.unsqueeze(1).broadcast_to([P, 2, 36]), add))
                gmax = gm[:, :, 0]
                first_max(lg[:, :, 0:4], 4, C("rev4"), gmax, g1h)
                dve.tensor_tensor(ge_m, lg[:, :, 0:4], gm.broadcast_to([P, 2, 4]), sub)\
                    .then_inc(sem("shifted"), 1)
                step.run(dve.tensor_tensor(
                    picked, lg[:, :, 4:36].rearrange("p t (g j) -> p t g j", g=4),
                    g1h.unsqueeze(3).broadcast_to([P, 2, 4, 8]), mul))
                step.run(dve.tensor_reduce(el, picked.rearrange("p t g j -> p t j g"), AX, add))
                first_max(el, 8, C("rev8"), top[:, 0, :, 0], one_hot[:, 0])
                step.run(dve.scalar_tensor_tensor(el, one_hot[:, 0], -3e38, el, mul, add))
                first_max(el, 8, C("rev8"), top[:, 1, :, 0], one_hot[:, 1])
                dve.tensor_tensor(gap, top[:, 1, :, 0], top[:, 0, :, 0], sub)\
                    .then_inc(sem("gap"), 1)
                step.run(dve.tensor_tensor(s8, one_hot[:, 0], one_hot[:, 1], add))
                four = [P, 2, 4, 8]

                def spread(o, i):
                    return dve.tensor_tensor(o.rearrange("p t (g j) -> p t g j", g=4),
                                             g1h.unsqueeze(3).broadcast_to(four),
                                             i.unsqueeze(2).broadcast_to(four), mul)

                spread(s32, s8).then_inc(sem("chosen"), 1)
                dve.wait_ge(sem("g_exp"), no)
                gt = gate[:, :, 0]
                step.run(dve.tensor_reduce(gt, ge, AX, add))
                dve.wait_ge(sem("d_exp"), no)
                step.run(dve.tensor_scalar(w12[:, 1, :, 0], dexp[:, :, 0], 1.0, None, add))
                step.run(dve.tensor_tensor(w12[:, 1, :, 0], w12[:, 1, :, 0], gt, mul))
                step.run(dve.reciprocal(w12[:, 0, :, 0], w12[:, 1, :, 0]))
                step.run(dve.tensor_tensor(w12[:, 1, :, 0], w12[:, 0, :, 0], dexp[:, :, 0], mul))
                step.run(dve.tensor_tensor(w8, one_hot[:, 0], w12[:, 0].broadcast_to([P, 2, 8]),
                                           mul))
                step.run(dve.tensor_tensor(tie8, one_hot[:, 1], w12[:, 1].broadcast_to([P, 2, 8]),
                                           mul))
                step.run(dve.tensor_tensor(w8, w8, tie8, add))
                step.run(spread(wt32, w8))
                step.run(dve.memset(rankm, -1.0))
                dve.wait_ge(sem("ranked"), no)
                step.run(dve.scalar_tensor_tensor(
                    rankm[:, :, 0:32], ps[:, 5, 0:64].rearrange("p (t n) -> p t n", t=2), 1.0,
                    s32, add, mul))
                step.run(dve.tensor_scalar(rankm[:, :, 0:32], rankm[:, :, 0:32], -1.0, None, add))
                step.run(dve.tensor_reduce(cnt_f, ps[:, 5, 64:96], AX, ALU.max))
                dve.tensor_copy(cnt_i[:, :], cnt_f).then_inc(sem(f"m{layer}_counted"), 1)
                moe_round(f"m{layer}", 0, chunk_done, base[stage])
                dve.wait_ge(sem(f"m{layer}_counted"), 1)
                n = dve.value_load(cnt_i[0:1, :], min_val=0, max_val=TOK)
                with dve.If(n > SLOTS):
                    dve.wait_ge(sem(f"m{layer}_scattered"), PAIRS)
                    for rnd in range(ROUNDS - 1):
                        dve.tensor_scalar(rankm, rankm, -float(SLOTS), None, add)\
                            .then_inc(sem(f"m{layer}_more_lowered"), 1)
                        dve.wait_ge(sem(f"m{layer}_more_lowered"), rnd + 1)
                        moe_round(f"m{layer}_more", rnd, sem(f"m{layer}_more_chunk"),
                                  6 * PAIRS * rnd)
                    dve.wait_ge(sem(f"m{layer}_more_scattered"), PAIRS * (ROUNDS - 1))
                dve.wait_ge(sem(f"m{layer}_scattered"), PAIRS)
                layer_norm(stage)

            def stick_breaking():
                g = base[STICK]
                move_T("x2", xT)

                def soft(h):
                    dve.wait_ge(sem("sk_l"), h + 1)
                    if h >= 2:
                        dve.wait_ge(sem("sk_spm"), h - 1)
                    dve.scalar_tensor_tensor(
                        sk_sp[:, h % 2, :], ps[:, h % 2, 0:HEAD_COLS], 0.0, sk_l[:, h % 2, :],
                        ALU.max, add).then_inc(sem("sk_sp"), 1)

                def logs(h):
                    dve.wait_ge(sem("sk_later"), h + 1)
                    d = sk_d[:, h % 2, :]
                    step.run(dve.tensor_copy(d, ps[:, 2 + h % 2, 0:HEAD_COLS]))
                    step.run(dve.tensor_tensor(d, ps[:, h % 2, 0:HEAD_COLS], d, sub))
                    if h >= 2:
                        dve.wait_ge(sem("sk_a"), h - 1)
                    dve.scalar_tensor_tensor(sk_arg[:, h % 2, :], sk_d[:, h % 2, :], 0.0,
                                             C("stick_add"), ALU.min, add)\
                        .then_inc(sem("sk_arg"), 1)

                for n in range(SB_HEADS + 2):
                    if n >= 2:
                        logs(n - 2)
                    if 1 <= n <= SB_HEADS:
                        soft(n - 1)
                dve.wait_ge(chunk_done, g + 8)
                layer_norm(STICK)

            def rms_norm(no):
                dve.wait_ge(sem("h_sq"), 2 * no)
                inv_root(rstd[:, :, 0], mv[:, :, 0], 1.0 / D, RMS_EPS)
                dve.tensor_tensor(at_h, x, rstd.broadcast_to([P, 2, D]), mul)\
                    .then_inc(sem("h_ready"), 1)

            def attention(grp, out_g, gains, mask, lse):
                heads = [P, 2, 8, 64]
                dve.wait_ge(sem("at_sq"), 2 * (grp + 1))
                step.run(dve.tensor_reduce(at_ss.rearrange("p t h -> p (t h)"),
                                           at_w.rearrange("p (h d) -> p h d", d=64), AX, add))
                inv_root(at_ss, at_ss, 1.0 / 64, RMS_EPS)
                for w, b in ((0, 4), (1, 6)):
                    v = at_qk[:, :, 512 * w:512 * w + 512].rearrange("p t (h d) -> p t h d", d=64)
                    step.run(dve.tensor_tensor(
                        v, two_banks(b).rearrange("p t (h d) -> p t h d", d=64),
                        at_ss[:, :, 8 * w:8 * w + 8].unsqueeze(3).broadcast_to(heads), mul))
                    gain = gains[:, 64 * w:64 * w + 64].unsqueeze(1).unsqueeze(1)
                    step.run(dve.tensor_tensor(v, v, gain.broadcast_to(heads), mul))
                v = at_qk.rearrange("p t (h d) -> p t h d", d=64)
                x1, x2 = v[:, :, :, 0:8], v[:, :, :, 8:16]
                cos, sin = (C(n).rearrange("p (t j) -> p t j", t=2).unsqueeze(2)
                            .broadcast_to([P, 2, 16, 8]) for n in ("cos", "sin"))
                for n, (u, f) in enumerate(((x1, cos), (x2, sin), (x2, cos), (x1, sin))):
                    step.add(dve.tensor_tensor(at_rope[:, n], u, f, mul))
                step.settle()
                step.add(dve.tensor_tensor(x1, at_rope[:, 0], at_rope[:, 1], sub))
                step.add(dve.tensor_tensor(x2, at_rope[:, 2], at_rope[:, 3], add))
                step.settle()
                dve.sem_inc(sem("at_qk"), 1)
                move_T(qk_turn(grp), at_qkT)

                def masked(pr):
                    n = 4 * grp + pr
                    dve.wait_ge(sem("at_scored"), n + 1)
                    if pr >= 2:
                        dve.wait_ge(sem("at_p"), 4 * (n - 1))
                    o = at_sm[:, pr % 2]
                    dve.tensor_tensor(o, ps[:, 2 * (pr % 2):2 * (pr % 2) + 2, 0:HEAD_COLS],
                                      mask.unsqueeze(1).broadcast_to([P, 2, HEAD_COLS]), add)\
                        .then_inc(sem("at_masked"), 1)
                    dve.wait_ge(sem("at_masked"), n + 1)
                    hs = slice(2 * pr, 2 * pr + 2)
                    step.add(dve.tensor_reduce(at_mx[:, 0, hs], o[:, :, 0:P], AX, ALU.max))
                    step.add(dve.tensor_reduce(at_mx[:, 1, hs], o[:, :, P:], AX, ALU.max))
                    step.settle()
                    dve.tensor_scalar(at_nmx[:, :, hs], at_mx[:, :, hs], -1.0, None, mul)\
                        .then_inc(sem("at_max"), 1)

                def move_pT(pr):
                    n = 4 * grp + pr
                    dve.wait_ge(sem("at_turned"), n + 1)
                    if n:
                        dve.wait_ge(sem("at_mixed"), n)
                    dve.tensor_copy(at_pT[:, 1, :], ps[:, 5, 0:HEAD_COLS])\
                        .then_inc(sem("at_pT_moved"), 1)

                for n in range(5):
                    if n < 4:
                        masked(n)
                    if n >= 1:
                        move_pT(n - 1)
                dve.wait_ge(sem("at_p"), 16 * (grp + 1))
                step.run(dve.reciprocal(at_rden, at_den))
                dve.wait_ge(sem("at_mixed"), 4 * (grp + 1))
                dve.tensor_tensor(at_o[:, out_g].rearrange("p t (h d) -> p t h d", d=64),
                                  two_banks(6).rearrange("p t (h d) -> p t h d", d=64),
                                  at_rden.unsqueeze(3).broadcast_to(heads), mul)\
                    .then_inc(sem("at_o_moved"), 1)
                if lse:
                    dve.wait_ge(sem("at_lse"), grp + 1)
                    step.run(dve.tensor_tensor(at_lse[:, grp], at_lse[:, grp], at_mx, add))

            def ssd_dilated():
                g = base[SSD]
                rms_norm(1)
                move_T("h4", xT, range(4), Q("norm4"))
                pad0 = ss_pad[:, :, :, 0:3].rearrange("p b m t -> p (b m) t")
                step.add(dve.memset(pad0, 0.0))
                d = dt_v
                dve.wait_ge(sem("ss_dt"), 1)
                step.run(dve.tensor_tensor(
                    d[0], ps[:, 0, 0:32].rearrange("p (t h) -> p t h", t=2),
                    Q("dt_b").unsqueeze(1).broadcast_to([P, 2, 16]), add))
                dve.scalar_tensor_tensor(d[1], d[0], -1.0, d[0], mul, ALU.max)\
                    .then_inc(sem("ss_dabs"), 1)
                dve.wait_ge(sem("ss_soft"), 2)
                step.run(dve.scalar_tensor_tensor(d[6], d[0], 0.0, d[3], ALU.max, add))
                dve.scalar_tensor_tensor(d[5], d[6], -1.0,
                                         d[4][:, 0:1, :].broadcast_to([P, 2, 16]), mul, mul)\
                    .then_inc(sem("ss_a"), 1)
                w = Q("conv2_w")
                for c in range(4):
                    for m in range(4):
                        k = 4 * c + m
                        dve.wait_ge(sem("ss_taken"), 2 * k + 2)
                        for j in range(2):
                            step.run(dve.scalar_tensor_tensor(
                                xa[:, k, :], ss_pad[:, c % 2, m, j:j + TOK],
                                w[:, 4 * k + j:4 * k + j + 1], xa[:, k, :], mul, add))
                        dve.scalar_tensor_tensor(
                            xa[:, k, :], ss_pad[:, c % 2, m, 2:2 + TOK],
                            w[:, 4 * k + 2:4 * k + 3], xa[:, k, :], mul, add)\
                            .then_inc(sem("ss_conv"), 1)
                dve.wait_ge(sem("ss_cs"), 1)
                step.run(dve.tensor_scalar(
                    d[7], ps[:, 1, 0:32].rearrange("p (t h) -> p t h", t=2), -1.0, None, mul))
                for u in range(4):
                    dve.wait_ge(sem("ss_turned"), u + 1)
                    dve.tensor_copy(ss_x[:, u // 2, (u % 2) * 512:(u % 2 + 1) * 512],
                                    bank(2 + u % 2)).then_inc(sem("ss_x"), 1)
                dve.wait_ge(sem("ss_x"), 4)
                hd = [P, 16, 64]
                xh = [ss_x[:, t].rearrange("p (h d) -> p h d", d=64) for t in range(2)]
                yh = [ss_y[:, t].rearrange("p (h d) -> p h d", d=64) for t in range(2)]
                for t in range(2):
                    step.add(dve.tensor_tensor(
                        yh[t], xh[t], Q("d_skip").unsqueeze(2).broadcast_to(hd), mul))
                step.settle()
                for t in range(2):
                    step.add(dve.tensor_tensor(
                        xh[t], xh[t], d[6][:, t, :].unsqueeze(2).broadcast_to(hd), mul))
                step.settle()
                dve.sem_inc(sem("ss_xdt"), 1)

                def decay(h):
                    dve.wait_ge(sem("ss_sum"), h + 1)
                    o, p, m = ss_arg[:, h % 2, :], ps[:, 4 + h % 2, :], C("ssd_add")
                    dve.scalar_tensor_tensor(o[:, 0:TOK], p[:, 0:TOK], d[7][:, 0, h:h + 1],
                                             m[:, 0:TOK], add, add).then_inc(sem("ss_arg"), 1)
                    dve.scalar_tensor_tensor(o[:, TOK:], p[:, P:TOK], d[7][:, 1, h:h + 1],
                                             m[:, TOK:], add, add).then_inc(sem("ss_arg"), 1)

                def scan(h):
                    dve.wait_ge(sem("ss_e"), h + 1)
                    if h >= 2:
                        dve.wait_ge(sem("ss_yh"), h - 1)
                    dve.tensor_tensor(ss_m[:, h % 2, :], ss_arg[:, h % 2, :],
                                      ss_cb[:, h // 4, :], mul).then_inc(sem("ss_m"), 1)

                dve.wait_ge(sem("ss_cb"), 4)
                for n in range(SSD_HEADS + 1):
                    if n < SSD_HEADS:
                        if n >= 2:
                            dve.wait_ge(sem("ss_m"), n - 1)
                        decay(n)
                    if n >= 1:
                        scan(n - 1)
                dve.wait_ge(sem("ss_yh"), SSD_HEADS)
                for t in range(2):
                    v = ss_y[:, t].rearrange("p (n c) -> p n c", n=2)
                    step.add(dve.tensor_tensor(v, two_banks(2 * t), v, add))
                step.settle()
                for t in range(2):
                    dve.tensor_tensor(ss_y[:, t], ss_y[:, t], ss_z[:, t], mul)\
                        .then_inc(sem("ss_gated"), 1)
                dve.wait_ge(sem("ss_sq"), 8)
                inv_root(ss_ss, ss_ss, 1.0 / 256, RMS_EPS)
                y4 = ss_y.rearrange("p t (q c) -> p (t q) c", q=4)
                dve.tensor_tensor(y4, y4, ss_ss.unsqueeze(2).broadcast_to([P, 8, 256]), mul)\
                    .then_inc(sem("ss_y"), 1)
                move_T("y4", mixT12, range(4), Q("ssd_norm"))
                add4 = C("att_add").rearrange("p (n c) -> p n c", n=4)
                for grp in range(3):
                    attention(grp, grp, Q("qk4"), add4[:, grp, :], True)
                lse3 = at_lse.rearrange("p g t h -> p g (t h)")
                lm, ls = (v.rearrange("p t h -> p (t h)") for v in (at_lm, at_ls))
                lw3 = at_lw.rearrange("p g t h -> p g (t h)")
                step.run(dve.tensor_reduce(lm, lse3.rearrange("p g n -> p n g"), AX, ALU.max))
                dve.tensor_tensor(lse3, lse3, lm.unsqueeze(1).broadcast_to([P, 3, 16]), sub)\
                    .then_inc(sem("at_lse_m"), 1)
                dve.wait_ge(sem("at_lw"), 1)
                step.run(dve.tensor_reduce(ls, lw3.rearrange("p g n -> p n g"), AX, add))
                step.run(dve.reciprocal(ls, ls))
                step.run(dve.tensor_tensor(lw3, lw3, ls.unsqueeze(1).broadcast_to([P, 3, 16]), mul))
                heads = [P, 16, 64]
                og = [at_o[:, q].rearrange("p t (h d) -> p (t h) d", d=64) for q in range(3)]
                dve.wait_ge(sem("at_o_moved"), 3)
                for q in range(3):
                    step.add(dve.tensor_tensor(
                        og[q], og[q], lw3[:, q, :].unsqueeze(2).broadcast_to(heads), mul))
                step.settle()
                step.run(dve.tensor_tensor(og[0], og[0], og[1], add))
                step.run(dve.tensor_tensor(og[0], og[0], og[2], add))
                dve.wait_ge(sem("at_g"), 1)
                dve.tensor_tensor(at_o[:, 0], at_o[:, 0], at_g4, mul).then_inc(sem("at_gated"), 1)
                for t in range(2):
                    dve.wait_ge(sem("at_turned_o"), t + 1)
                    dve.tensor_copy(mixT12[:, 8:12, t * P:(t + 1) * P],
                                    bank(t).rearrange("p (k c) -> p k c", k=4))\
                        .then_inc(sem("at_mixT"), 1)
                finish(g + 19)

            def finish(chunks):
                dve.wait_ge(chunk_done, chunks)
                dve.tensor_copy(x.rearrange("p t (n c) -> p (t n) c", n=2), ps[:, 0:4, :])\
                    .then_inc(x_ready, 1)

            def block_attention():
                g = base[MOBA]
                two = SSD in on
                rms_norm(2 if two else 1)
                move_T("h5", xT, range(4), Q("norm5"))
                causal = C("att_add")[:, 3 * HEAD_COLS:]
                for grp in range(2):
                    attention(g_no(3 + grp), grp, Q("qk5"), causal, False)
                for c in range(2):
                    dve.wait_ge(sem("at_g"), c + (2 if two else 1))
                    dve.wait_ge(sem("at_o_moved"), g_no(3 + c) + 1)
                    step.add(dve.tensor_tensor(at_o[:, c], at_o[:, c],
                                               at_g5[:, :, c * 512:(c + 1) * 512], mul))
                step.settle()
                dve.sem_inc(sem("at_gated"), 1)
                for t in range(2):
                    for kk in range(2):
                        dve.wait_ge(sem("at_turned_o"), 2 * t + kk + (3 if two else 1))
                        dve.tensor_copy(mixT12[:, 4 * kk:4 * kk + 4, t * P:(t + 1) * P],
                                        bank(2 * t + kk).rearrange("p (k c) -> p k c", k=4))\
                            .then_inc(sem("at_mixT"), 1)
                finish(g + 10)

            dve.wait_ge(const_in, 32)
            run = {CONV: conv_mixers, MOE0: lambda: experts(MOE0, 0), STICK: stick_breaking,
                   MOE1: lambda: experts(MOE1, 1), SSD: ssd_dilated, MOBA: block_attention}
            if first != CONV:
                wait_x(dve, first)
            for stage in on:
                run[stage]()


INPUTS = ["x", "even_w_in", "even_w_out", "odd_w_qkv", "odd_w_o", "ln_mix_g", "ln_mix_b",
          "ln_ffn_g", "ln_ffn_b", "expert_w_up", "expert_w_down", "even_w_in_2", "even_w_out_2",
          "odd_w_in_2", "odd_w_out_2"]


def small_params(a):
    p = np.zeros((P, PARAM_WORDS), np.float32)

    def put(name, value):
        p[:, PARAM[name][0]:PARAM[name][1]] = value.reshape(P, -1)

    def column(v):
        return v.reshape(-1, P).T

    def row(v):
        return np.broadcast_to(v.reshape(1, -1), (P, v.size))

    put("conv_a", a["even_conv_a"][0].reshape(CONV_A, 4, P).transpose(2, 1, 0))
    put("conv_b", a["even_conv_b_w"][0].reshape(CONV_B, 4, P).transpose(2, 1, 0))
    put("conv_bb", column(a["even_conv_b_bias"][0]))
    put("norm_g", column(a["even_norm_b_g"][0]))
    put("norm_b", column(a["even_norm_b_b"][0]))
    w = np.concatenate([a["router_group_w"], a["router_expert_w"]], 2)
    put("router_w", w.reshape(2, KT, P, 36).transpose(2, 0, 1, 3))
    put("router_b", row(np.concatenate([a["router_group_b"], a["router_expert_b"]], 1)))
    put("dt_w", a["even_w_in_2"][0][:, 3072:3088].reshape(KT, P, 16).transpose(1, 0, 2))
    put("conv2_w", a["even_conv_w_2"][0].reshape(16, P, 4).transpose(1, 0, 2))
    put("conv2_b", column(a["even_conv_b_2"][0]))
    put("norm4", column(a["even_norm_w_2"][0]))
    put("norm5", column(a["odd_norm_w_2"][0]))
    put("ssd_norm", column(a["even_ssd_norm_w_2"][0]))
    put("dt_b", row(a["even_dt_bias_2"][0]))
    put("a_log", row(a["even_a_log_2"][0]))
    put("d_skip", row(a["even_d_skip_2"][0]))
    put("qk4", row(np.concatenate([a["even_q_norm_2"][0], a["even_k_norm_2"][0]])))
    put("qk5", row(np.concatenate([a["odd_q_norm_2"][0], a["odd_k_norm_2"][0]])))
    return p


def kernel(**inputs):
    import concourse.bacc as bacc
    from concourse.bass_utils import run_bass_kernel_spmd

    nc = bacc.Bacc("TRN2", target_bir_lowering=False, num_devices=1)
    host = {k: np.asarray(v) for k, v in inputs.items()}
    arrays = {name: np.ascontiguousarray(host[name]) for name in INPUTS}
    arrays["params"] = small_params(host)
    arrays["constants"] = constants()
    dram = {name: nc.dram_tensor(f"in_{name}", v.shape, mybir.dt.from_np(v.dtype),
                                 kind="ExternalInput").ap() for name, v in arrays.items()}
    out = nc.dram_tensor("out_x", (1, TOK, D), F32, kind="ExternalOutput").ap()
    build(nc, dram, out, *STAGES)
    r = run_bass_kernel_spmd(nc, [{f"in_{k}": v for k, v in arrays.items()}], core_ids=[0])
    return r.results[0]["out_x"]


STAGES = (0, 5)
```

```python
from contextlib import ExitStack

import numpy as np

import concourse.bass as bass
from concourse import mybir

F32 = mybir.dt.float32
I32 = mybir.dt.int32
ALU = mybir.AluOpType
ACT = mybir.ActivationFunctionType
AX = mybir.AxisListType.X

P = 128
TOK = 256
D = 1024
KT = D // P
ALPHA = 4 ** 0.25
LN_EPS, RMS_EPS = 1e-5, 1e-6
NEG = -1e30

EXPERTS, GROUPS, PER_GROUP = 32, 4, 8
QUAD = 4
QUADS = EXPERTS // QUAD
SLOTS = P // QUAD
ROUNDS = TOK // SLOTS
FFN = 512
QUAD_CHUNKS = 3 * QUAD

SB_HEADS = 16
SSD_HEADS = 16
CONV_A, CONV_B = 3, 31
HEAD_COLS = 384

RING = 6
SLOT_WORDS = 4096
ARENA = 15800

STAGE_CHUNKS = [7, QUAD_CHUNKS * QUADS, 8, QUAD_CHUNKS * QUADS, 19, 10]
BASE = [sum(STAGE_CHUNKS[:n]) for n in range(len(STAGE_CHUNKS))]
CONV, MOE0, STICK, MOE1, SSD, MOBA = range(6)

TURNS = ["x0", "x1", "x2", "x3", "h4", "qk0", "y4", "qk1", "qk2", "h5", "qk3", "qk4"]
TURN = {name: n for n, name in enumerate(TURNS)}


def layout(items):
    at, out = 0, {}
    for name, n in items:
        out[name] = (at, at + n)
        at += n
    return out, at


CONST, CONST_WORDS = layout([
    ("ident", P), ("alpha", P), ("upto", P), ("ones", P), ("before", P), ("from_on", P),
    ("mean", P), ("iota", SLOTS), ("rev8", 8), ("rev4", 4), ("stick_mul", HEAD_COLS),
    ("stick_add", HEAD_COLS), ("ssd_add", HEAD_COLS), ("att_add", 4 * HEAD_COLS),
    ("cos", 16), ("sin", 16)])
PARAM, PARAM_WORDS = layout([
    ("conv_a", 4 * CONV_A), ("conv_b", 4 * CONV_B), ("conv_bb", 4), ("norm_g", 4), ("norm_b", 4),
    ("router_w", 2 * KT * 36), ("router_b", 72), ("dt_w", KT * 16), ("conv2_w", 64),
    ("conv2_b", 16), ("norm4", 8), ("norm5", 8), ("ssd_norm", 8), ("dt_b", 16), ("a_log", 16),
    ("d_skip", 16), ("qk4", 128), ("qk5", 128)])


def constants():
    r = np.arange(P)
    row, col = r[:, None], r[None, :]
    c = np.zeros((P, CONST_WORDS), np.float32)

    def put(name, value, at=0):
        a, b = CONST[name]
        value = np.asarray(value, np.float32)
        c[:, a + at:a + at + value.shape[-1]] = value

    put("ident", row == col)
    put("alpha", (row == col) * np.float32(ALPHA))
    put("upto", row <= col)
    put("ones", np.ones((P, P)))
    put("before", row < col)
    put("from_on", row >= col)
    put("mean", np.full((P, P), 1.0 / 512))
    put("iota", np.broadcast_to(np.arange(SLOTS), (P, SLOTS)))
    put("rev8", np.broadcast_to(8 - np.arange(8), (P, 8)))
    put("rev4", np.broadcast_to(4 - np.arange(4), (P, 4)))

    def blocks(valid, keys_first):
        out = []
        for t, s in ((0, 0), (1, 0), (1, 1)):
            if keys_first:
                out.append(valid(t * P + col, s * P + row))
            else:
                out.append(valid(t * P + row, s * P + col))
        return np.concatenate(out, 1)

    strict = blocks(lambda t, s: s < t, True)
    put("stick_mul", strict)
    put("stick_add", np.where(strict, 0.0, NEG))
    put("ssd_add", np.where(blocks(lambda t, s: s <= t, True), 0.0, NEG))
    for n, (band, dil) in enumerate(((P, 1), (TOK, 4), (TOK, 16), (TOK, 1))):
        ok = blocks(lambda t, s: (s <= t) & (t - s <= band) & ((t - s) % dil == 0), False)
        put("att_add", np.where(ok, 0.0, NEG), n * HEAD_COLS)
    inv = np.float32(500000.0) ** (-np.arange(8, dtype=np.float32) * 2.0 / 16)
    ang = np.arange(TOK, dtype=np.float32)[:, None] * inv[None, :].astype(np.float32)
    for name, f in (("cos", np.cos), ("sin", np.sin)):
        table = f(ang.astype(np.float32)).reshape(2, P, 8).transpose(1, 0, 2).reshape(P, 16)
        put(name, table)
    return c


def build(nc, a, out, first=0, last=5):
    on = range(first, last + 1)
    turns = [n for n in TURNS if int({"x": n[1:], "h": n[1:], "y": n[1:], "q": "4" if n in
             ("qk0", "qk1", "qk2") else "5"}[n[0]]) in on]
    turn = {n: k for k, n in enumerate(turns)}
    base, at = {}, 0
    for n in on:
        base[n] = at
        at += STAGE_CHUNKS[n]

    ctx = ExitStack()
    with ctx:
        def sb(name, words, dt=F32):
            return ctx.enter_context(nc.sbuf_tensor(name, [P, words], dt))

        sems = {}

        def sem(name):
            if name not in sems:
                sems[name] = ctx.enter_context(nc.semaphore(name))
            return sems[name]

        ring = sb("ring", RING * SLOT_WORDS)
        con = sb("constants_sb", CONST_WORDS)
        par = sb("params_sb", PARAM_WORDS)
        x_w = sb("x_tok", 2 * D)
        xT_w = sb("xT", KT * TOK)
        ln_w = sb("ln_rows", 2 * D)
        arena = sb("arena", ARENA)
        ps = ctx.enter_context(nc.psum_tensor("ps", [P, 8, 512], F32))

        def bank(b):
            return ps[:, b, :]

        def C(name):
            return con[:, CONST[name][0]:CONST[name][1]]

        def Q(name):
            return par[:, PARAM[name][0]:PARAM[name][1]]

        class Region:

            def __init__(self, at=0, whole=None, size=ARENA):
                self.at, self.whole, self.size = at, arena if whole is None else whole, size

            def __call__(self, words, pattern=None, **dims):
                v = self.whole[:, self.at:self.at + words]
                self.at += words
                assert self.at <= self.size, self.at
                return v.rearrange(pattern, **dims) if pattern else v

        ident, ones = C("ident"), C("ones")
        x = x_w[:, :].rearrange("p (t c) -> p t c", t=2)
        xT = xT_w[:, :].rearrange("p (k t) -> p k t", k=KT)
        lnr = ln_w[:, :].rearrange("p (r c) -> p r c", r=2)
        slot8 = [ring[:, s * SLOT_WORDS:(s + 1) * SLOT_WORDS].rearrange("p (k n) -> p k n", k=8)
                 for s in range(RING)]
        slot4 = [ring[:, s * SLOT_WORDS:(s + 1) * SLOT_WORDS].rearrange("p (k n) -> p k n", k=4)
                 for s in range(RING)]

        sm = Region(whole=sb("small", 640), size=640)
        stats = sm(24, "p (t n s) -> p t n s", t=2, n=2)
        mv = sm(4, "p (t s) -> p t s", t=2)
        rstd = sm(2, "p (t s) -> p t s", t=2)
        lg = sm(72, "p (t n) -> p t n", t=2)
        gm = sm(2, "p (t n) -> p t n", t=2)
        ge = sm(8, "p (t n) -> p t n", t=2)
        gate = sm(2, "p (t n) -> p t n", t=2)
        g1h = sm(8, "p (t n) -> p t n", t=2)
        tie4 = sm(8, "p (t n) -> p t n", t=2)
        picked = sm(64, "p (t g j) -> p t g j", t=2, g=4)
        el = sm(16, "p (t n) -> p t n", t=2)
        tie8 = sm(16, "p (t n) -> p t n", t=2)
        top = sm(4, "p (n t o) -> p n t o", n=2, t=2)
        one_hot = sm(32, "p (n t j) -> p n t j", n=2, t=2)
        dexp = sm(2, "p (t n) -> p t n", t=2)
        w12 = sm(4, "p (n t o) -> p n t o", n=2, t=2)
        s8 = sm(16, "p (t n) -> p t n", t=2)
        w8 = sm(16, "p (t n) -> p t n", t=2)
        s32 = sm(64, "p (t n) -> p t n", t=2)
        wt32 = sm(64, "p (t n) -> p t n", t=2)
        rankm = sm(72, "p (t n) -> p t n", t=2)
        cnt_f = sm(1)
        ge_m = sm(8, "p (t n) -> p t n", t=2)
        gap, gidx = sm(2), sm(2)
        cnt_i = sb("cnt_i", 1, I32)
        root_w = sb("root_w", 3 * TOK)

        x_in = sem("x_in")
        const_in = sem("const_in")
        ln_in = sem("ln_in")
        w_in = [sem(f"w_in{s}") for s in range(RING)]
        chunk_done = sem("chunk_done")
        transposed = sem("transposed")
        moved_T = sem("moved_T")
        x_ready = sem("x_ready")
        out_done = sem("out_done")

        def arrive(eng, g):
            eng.wait_ge(w_in[g % RING], 16 * (g // RING + 1))

        def wait_x(eng, stage):
            if stage == first:
                eng.wait_ge(x_in, 16)
            else:
                eng.wait_ge(x_ready, stage - first)

        class Steps:

            def __init__(self, eng, name):
                self.eng, self.sem, self.n = eng, sem(name), 0

            def add(self, ins):
                ins.then_inc(self.sem, 1)
                self.n += 1

            def settle(self):
                if self.n:
                    self.eng.wait_ge(self.sem, self.n)

            def settle_but(self, n):
                self.eng.wait_ge(self.sem, self.n - n)

            def run(self, ins):
                self.add(ins)
                self.settle()

        r = Region()
        cv_mixT = r(KT * TOK, "p (k t) -> p k t", k=KT)
        cv_sig = r(4 * TOK)
        cv_gpad = r(4 * (TOK + CONV_B - 1), "p (m t) -> p m t", m=4)
        cv_g = r(4 * TOK, "p (m t) -> p m t", m=4)
        cv_sq = r(4 * TOK, "p (m t) -> p m t", m=4)
        cv_a = r(3 * 4 * TOK, "p (c m t) -> p c m t", c=3, m=4)
        cv_apad = r(4 * (TOK + CONV_A - 1), "p (m t) -> p m t", m=4)
        cv_y = r(4 * TOK, "p (m t) -> p m t", m=4)
        cv_rstd = r(TOK)

        r = Region()
        pick = r(2 * P, "p (t e s) -> p t e s", t=2, e=QUAD)
        pick_w = r(2 * P, "p (t e s) -> p t e s", t=2, e=QUAD)
        back = r(TOK)
        xg = r(KT * P, "p (k s) -> p k s", k=KT)
        sg = r(2 * P, "p (b c) -> p b c", b=2)
        hid = r(2 * P, "p (b c) -> p b c", b=2)
        hidT = r(QUAD * P, "p (e c) -> p e c", e=QUAD)
        yg = r(D)

        r = Region()
        sk_mixT = r(KT * TOK, "p (k t) -> p k t", k=KT)
        sk_qk = r(2 * KT * TOK, "p (k t) -> p k t", k=2 * KT)
        sk_v = r(2 * D, "p (t c) -> p t c", t=2)
        sk_az = r(2 * HEAD_COLS, "p (b c) -> p b c", b=2)
        sk_e = r(2 * HEAD_COLS, "p (b c) -> p b c", b=2)
        sk_l = r(2 * HEAD_COLS, "p (b c) -> p b c", b=2)
        sk_sp = r(2 * HEAD_COLS, "p (b c) -> p b c", b=2)
        sk_spm = r(2 * HEAD_COLS, "p (b c) -> p b c", b=2)
        sk_arg = r(2 * HEAD_COLS, "p (b c) -> p b c", b=2)
        sk_d = r(2 * HEAD_COLS, "p (b c) -> p b c", b=2)
        sk_a = r(2 * HEAD_COLS, "p (b c) -> p b c", b=2)

        xa = arena[:, 0:16 * TOK].rearrange("p (m t) -> p m t", m=16)
        mixT12 = arena[:, 0:12 * TOK].rearrange("p (k t) -> p k t", k=12)
        r = Region(4096)
        ss_z = r(2 * D, "p (t c) -> p t c", t=2)
        ss_pad = r(2 * 4 * (TOK + 3), "p (b m t) -> p b m t", b=2, m=4)
        ss_x = r(2 * D, "p (t c) -> p t c", t=2)
        ss_cb = r(4 * HEAD_COLS, "p (g c) -> p g c", g=4)
        ss_arg = r(2 * HEAD_COLS, "p (b c) -> p b c", b=2)
        ss_m = r(2 * HEAD_COLS, "p (b c) -> p b c", b=2)
        ss_y = r(2 * D, "p (t c) -> p t c", t=2)
        ss_s = r(400)
        dt_v = [ss_s[:, 32 * n:32 * n + 32].rearrange("p (t h) -> p t h", t=2) for n in range(8)]
        ss_ss = ss_s[:, 256:264]

        at_v = arena[:, 2048:3072].rearrange("p (t c) -> p t c", t=2)
        at_pT = arena[:, 3072:3072 + 2 * HEAD_COLS].rearrange("p (h c) -> p h c", h=2)

        def sq_words(n):
            at = 0 if n == 0 and SSD in on else 4096
            return arena[:, at:at + D]

        def rope_words(n):
            at = D + (0 if n == 0 and SSD in on else 4096)
            return arena[:, at:at + 512].rearrange("p (n t h j) -> p n t h j", n=4, t=2, h=8)

        r = Region(6144)
        at_qk = r(2 * D, "p (t c) -> p t c", t=2)
        r = Region(6144 + 2 * 4 * (TOK + 3))
        at_qkT = r(KT * TOK, "p (k t) -> p k t", k=KT)
        at_o_words = r(4 * D)
        at_oT = at_o_words[:, 0:3 * D].rearrange("p (g k t) -> p g k t", g=3, k=4)
        at_g4 = at_o_words[:, 3 * D:4 * D].rearrange("p (k t) -> p k t", k=4)
        at_g5 = at_o_words[:, 2 * D:4 * D].rearrange("p (k t) -> p k t", k=8)
        at_p = ln_w[:, 0:2 * HEAD_COLS].rearrange("p (h c) -> p h c", h=2)
        at_sm = ln_w[:, 2 * HEAD_COLS:4 * HEAD_COLS].rearrange("p (h c) -> p h c", h=2)
        at_stat = ln_w[:, 4 * HEAD_COLS:]
        at_h = at_qk
        junk = lnr

        def stat(n0, n, **dims):
            return at_stat[:, n0:n0 + n].rearrange(
                "p (g t h) -> p g t h" if "g" in dims else "p (t h) -> p t h", **dims)

        head_v, head_y, head_w = (stat(32 * n, 32, g=2, t=2) for n in range(3))
        at_nmx = stat(96, 16, t=2)
        at_mx, at_den, at_wt = (stat(112 + 48 * n, 48, g=3, t=2) for n in range(3))
        at_em, at_ed = (stat(256 + 48 * n, 48, g=3, t=2) for n in range(2))
        at_lm, at_ls = stat(352, 16, t=2), stat(368, 16, t=2)

        def layer_no(stage):
            return sum(s in on for s in (MOE0, MOE1) if s <= stage)

        def g_no(n):
            return n if SSD in on else n - 3

        def taken(n):
            n = n if SSD in on else n + 3
            return (0, 3, 6, 10, 14)[n] - (0 if SSD in on else 10)

        def qk_turn(n):
            return f"qk{n if SSD in on else n + 3}"

        def cols(w, c0, n=512):
            return w.rearrange("(k p) n -> p k n", p=P)[:, :, c0:c0 + n]

        def rows(w, c):
            return w[c * 512:(c + 1) * 512, :].rearrange("(k p) n -> p k n", p=P)

        up_v = a["expert_w_up"].rearrange("l e (k p) n -> l e p k n", p=P)
        down_v = a["expert_w_down"].rearrange("l e (k p) n -> l e p k n", p=P)
        out_v = out[0].rearrange("(t p) c -> p t c", p=P)

        def streamed(stage):
            if stage == CONV:
                w = a["even_w_in"][0]
                return [(8, cols(w, c)) for c in (2048, 1536, 512, 1024, 0)] + \
                    [(4, rows(a["even_w_out"][0], c)) for c in range(2)]
            if stage == STICK:
                return [(8, cols(a["odd_w_qkv"][0], 512 * c)) for c in range(6)] + \
                    [(4, rows(a["odd_w_o"][0], c)) for c in range(2)]
            if stage == SSD:
                w = a["even_w_in_2"][0]
                xbc = [1024 + 512 * c for c in range(4)]
                qkv = [q0 + 512 * g for g in range(3) for q0 in (3088, 4624, 6160)]
                return [(8, cols(w, c)) for c in xbc + [0, 512] + qkv + [7696]] + \
                    [(4, rows(a["even_w_out_2"][0], c)) for c in range(3)]
            w = a["odd_w_in_2"][0]
            return [(8, cols(w, c)) for c in (0, 1024, 2048, 3072, 512, 1536, 2560, 3584)] + \
                [(4, rows(a["odd_w_out_2"][0], c)) for c in range(2)]

        block = ctx.enter_context(nc.Block())

        @block.sync
        def _(sp):
            sp.dma_start(x, a["x"][0].rearrange("(t p) c -> p t c", p=P)).then_inc(x_in, 16)

            def load(g, wide, src):
                if g >= RING:
                    sp.wait_ge(chunk_done, g - RING + 1)
                dst = (slot8 if wide == 8 else slot4)[g % RING]
                sp.dma_start(dst, src).then_inc(w_in[g % RING], 16)

            def expert_chunk(layer, quad, j):
                if j < 2 * QUAD:
                    return up_v[layer, quad * QUAD + j // 2, :, 4 * (j % 2):4 * (j % 2) + 4, :]
                return down_v[layer, quad * QUAD + (j - 2 * QUAD)]

            def experts(stage, layer):
                b0 = base[stage]
                for j in range(QUAD_CHUNKS):
                    load(b0 + j, 4, expert_chunk(layer, 0, j))
                with sp.Fori(1, QUADS) as i:
                    for j in range(QUAD_CHUNKS):
                        g = b0 + j
                        sp.wait_ge(chunk_done, i * QUAD_CHUNKS + (g - RING + 1))
                        sp.dma_start(slot4[g % RING], expert_chunk(layer, i, j))\
                            .then_inc(w_in[g % RING], 16)
                sp.wait_ge(sem(f"m{layer}_counted"), 1)
                n = sp.value_load(cnt_i[0:1, :], min_val=0, max_val=TOK)
                more_chunk = sem(f"m{layer}_more_chunk")
                with sp.If(n > SLOTS):
                    sp.wait_ge(chunk_done, b0 + QUAD_CHUNKS * QUADS)
                    with sp.Fori(0, ROUNDS - 1) as rnd:
                        with sp.If(n - rnd * SLOTS > SLOTS):
                            with sp.Fori(0, QUADS) as i:
                                for j in range(QUAD_CHUNKS):
                                    if j % RING == 0:
                                        sp.wait_ge(more_chunk, rnd * (QUAD_CHUNKS * QUADS)
                                                   + i * QUAD_CHUNKS + (j + 1))
                                    sp.dma_start(slot4[(b0 + j) % RING], expert_chunk(layer, i, j))\
                                        .then_inc(sem(f"m{layer}_more_in"), 16)
                    sp.wait_ge(sem(f"m{layer}_more_over"), 1)

            for stage in on:
                if stage in (MOE0, MOE1):
                    experts(stage, stage // 2)
                else:
                    for n, (wide, src) in enumerate(streamed(stage)):
                        load(base[stage] + n, wide, src)
            sp.wait_ge(x_ready, len(on))
            sp.dma_start(out_v, x).then_inc(sem("out_stored"), 16)
            sp.wait_ge(sem("out_stored"), 16)

        @block.gpsimd
        def _(pool):
            step = Steps(pool, "pool_step")

            def rotate(grp, gains):
                mul = ALU.mult
                for w in range(2):
                    pool.wait_ge(sem("head_y"), 2 * grp + w + 1)
                    v, y, u = head_v[:, w], head_y[:, w], head_w[:, w]
                    step.run(pool.tensor_tensor(u, v, y, mul))
                    step.run(pool.tensor_tensor(u, u, y, mul))
                    step.run(pool.tensor_scalar(u, u, -0.5, 1.5, mul, ALU.add))
                    step.run(pool.tensor_tensor(u, u, y, mul))
                    heads = [P, 2, 8, 64]
                    qk = at_qk[:, :, 512 * w:512 * w + 512].rearrange("p t (h d) -> p t h d", d=64)
                    gain = gains[:, 64 * w:64 * w + 64].unsqueeze(1).unsqueeze(1)
                    pool.wait_ge(sem("at_proj"), taken(grp) + w + 1)
                    for t in range(2):
                        step.add(pool.tensor_tensor(
                            qk[:, t], qk[:, t], u[:, t].unsqueeze(2).broadcast_to([P, 8, 64]),
                            mul))
                    step.settle()
                    for t in range(2):
                        step.add(pool.tensor_tensor(
                            qk[:, t], qk[:, t], gain[:, 0].broadcast_to([P, 8, 64]), mul))
                    step.settle()
                    x1, x2 = qk[:, :, :, 0:8], qk[:, :, :, 8:16]
                    cos, sin = (C(n).rearrange("p (t j) -> p t j", t=2).unsqueeze(2)
                                .broadcast_to([P, 2, 8, 8]) for n in ("cos", "sin"))
                    part = rope_words(grp)
                    for n, (a_, f) in enumerate(((x1, cos), (x2, sin), (x2, cos), (x1, sin))):
                        step.add(pool.tensor_tensor(part[:, n], a_, f, mul))
                    step.settle()
                    step.add(pool.tensor_tensor(x1, part[:, 0], part[:, 1], ALU.subtract))
                    step.add(pool.tensor_tensor(x2, part[:, 2], part[:, 3], ALU.add))
                    step.settle()
                    pool.sem_inc(sem("at_qk"), 1)

            pool.wait_ge(const_in, 32)
            for n, stage in enumerate(on):
                if stage <= MOE1:
                    kind = "ffn" if stage % 2 else "mix"
                    if n:
                        pool.wait_ge(x_ready, n)
                    for k, v in enumerate((a[f"ln_{kind}_g"], a[f"ln_{kind}_b"])):
                        pool.dma_start(lnr[:, k, :], v[stage // 2:stage // 2 + 1, :]
                                       .broadcast_to([P, D])).then_inc(ln_in, 16)
                if stage == STICK:
                    for h in range(SB_HEADS):
                        pool.wait_ge(sem("sk_sp"), h + 1)
                        if h >= 2:
                            pool.wait_ge(sem("sk_later"), h - 1)
                        pool.tensor_tensor(sk_spm[:, h % 2, :], sk_sp[:, h % 2, :],
                                           C("stick_mul"), ALU.mult).then_inc(sem("sk_spm"), 1)
                gains = Q("qk4") if stage == SSD else Q("qk5")
                if stage == SSD:
                    rotate(0, gains)
                    pool.wait_ge(sem("ss_y_taken"), 1)
                    for t in range(2):
                        pool.tensor_tensor(ss_y[:, t], ss_y[:, t], ss_z[:, t], ALU.mult)\
                            .then_inc(sem("ss_gated"), 1)
                    y4 = ss_y.rearrange("p t (q c) -> p (t q) c", q=4)
                    pool.wait_ge(sem("ss_rstd"), 1)
                    pool.tensor_tensor(y4, y4, ss_ss.unsqueeze(2).broadcast_to([P, 8, 256]),
                                       ALU.mult).then_inc(sem("ss_y"), 1)
                    rotate(1, gains)
                    rotate(2, gains)
                if stage == MOBA:
                    rotate(g_no(3), gains)
                    rotate(g_no(4), gains)

        @block.tensor
        def _(pe):
            def transposes(name, src):
                for b in range(4):
                    t, kk = b // 2, b % 2
                    for j in range(4):
                        k = 4 * kk + j
                        ins = pe.transpose(bank(b)[:, j * P:(j + 1) * P],
                                           src[:, t, k * P:(k + 1) * P], ident)
                    ins.then_inc(transposed, 1)

            def wait_T(name):
                pe.wait_ge(moved_T, 4 * (turn[name] + 1))

            def channels(g, b0):
                arrive(pe, g)
                w = slot8[g % RING]
                for m in range(4):
                    o = ps[:, b0 + m // 2, (m % 2) * TOK:(m % 2 + 1) * TOK]
                    for k in range(KT):
                        ins = pe.matmul(o, w[:, k, m * P:(m + 1) * P], xT[:, k, :],
                                        start=(k == 0), stop=(k == KT - 1))
                ins.then_inc(chunk_done, 1)

            def tokens(g, b0):
                arrive(pe, g)
                w = slot8[g % RING]
                for t in range(2):
                    for k in range(KT):
                        ins = pe.matmul(bank(b0 + t), xT[:, k, t * P:(t + 1) * P], w[:, k, :],
                                        start=(k == 0), stop=(k == KT - 1))
                ins.then_inc(chunk_done, 1)

            def residual(scale):
                for t in range(2):
                    for n in range(2):
                        pe.matmul(bank(2 * t + n), scale, x[:, t, n * 512:(n + 1) * 512],
                                  start=True, stop=False, skip_group_check=True)

            def output(g0, n_chunks, mixT, scale, before=lambda c, t: None):
                residual(scale)
                for c in range(n_chunks):
                    arrive(pe, g0 + c)
                    w = slot4[(g0 + c) % RING]
                    for t in range(2):
                        before(c, t)
                        for n in range(2):
                            for k in range(4):
                                ins = pe.matmul(
                                    bank(2 * t + n), mixT[:, 4 * c + k, t * P:(t + 1) * P],
                                    w[:, k, n * 512:(n + 1) * 512], start=False,
                                    stop=(c == n_chunks - 1 and k == 3), skip_group_check=True)
                    ins.then_inc(chunk_done, 1)

            def conv_mixers():
                g = base[CONV]
                wait_x(pe, CONV)
                transposes("x0", x)
                wait_T("x0")
                channels(g, 4)
                channels(g + 1, 6)
                pe.wait_ge(sem("cv_sig"), 1)
                channels(g + 2, 4)
                pe.wait_ge(sem("cv_gated"), 1)
                channels(g + 3, 6)
                pe.wait_ge(sem("cv_a_out"), 1)
                channels(g + 4, 4)
                pe.wait_ge(sem("cv_convolved"), 1)
                for m in range(4):
                    ins = pe.matmul(ps[:, 0, 0:TOK], C("mean"), cv_g[:, m, :],
                                    start=(m == 0), stop=(m == 3))
                ins.then_inc(sem("cv_mean"), 1)
                pe.wait_ge(sem("cv_squared"), 1)
                for m in range(4):
                    ins = pe.matmul(ps[:, 1, 0:TOK], C("mean"), cv_sq[:, m, :],
                                    start=(m == 0), stop=(m == 3))
                ins.then_inc(sem("cv_var"), 1)
                pe.wait_ge(sem("cv_mixed"), 4)
                pe.wait_ge(sem("cv_ya"), 1)
                output(g + 5, 2, cv_mixT, C("alpha"))

            def moe_round(tag, rnd, first_g, chunk, arrived):
                def s(name):
                    return sem(f"{tag}_{name}")

                def gather(half):
                    for k in range(4):
                        for t in range(2):
                            kk = 4 * half + k
                            ins = pe.matmul(ps[:, 6 + half, k * P:(k + 1) * P],
                                            x[:, t, kk * P:(kk + 1) * P],
                                            pick[:, t].rearrange("p e s -> p (e s)"),
                                            start=(t == 0), stop=(t == 1))
                    ins.then_inc(s("gathered"), 1)

                n1, n2 = rnd * (QUADS + 1), rnd * QUADS
                pe.wait_ge(s("picked"), n1 + 1)
                gather(1)
                gather(0)
                with pe.Fori(0, QUADS) as i:
                    def up(e):
                        if e >= 2:
                            pe.wait_ge(s("hidden_turned"), i * QUAD + (n2 * QUAD + e - 1))
                        for half in range(2):
                            j = 2 * e + half
                            arrived(pe, i, j)
                            w = slot4[(first_g + j) % RING]
                            for k in range(4):
                                for q in range(QUAD):
                                    ins = pe.matmul(
                                        ps[q * SLOTS:(q + 1) * SLOTS, 4 + e % 2, 0:TOK]
                                        .rearrange("p (g n) -> p g n", g=2),
                                        xg[:, 4 * half + k, e * SLOTS:(e + 1) * SLOTS],
                                        w[:, k, :].rearrange("p (g n) -> p g n", g=2)
                                        [:, :, q * P:(q + 1) * P],
                                        start=(j % 2 == 0 and k == 0), stop=(j % 2 == 1 and k == 3),
                                        skip_group_check=True)
                            ins.then_inc(chunk, 1)

                    def turn_hidden(e):
                        pe.wait_ge(s("hidden"), i * QUAD + (n2 * QUAD + e + 1))
                        pe.transpose(ps[:, 4 + e % 2, 0:P], hid[:, e % 2, :],
                                     ident).then_inc(s("turning"), 1)

                    pe.wait_ge(s("xg_moved"), i * 2 + (n1 * 2 + 2))
                    for e in range(QUAD):
                        up(e)
                        if e:
                            turn_hidden(e - 1)
                    pe.wait_ge(s("weighted"), i + (n2 + 1))
                    pe.wait_ge(s("hidden_turned"), i * QUAD + (n2 * QUAD + QUAD - 1))
                    for t in range(2):
                        ins = pe.transpose(ps[:, 4, t * P:(t + 1) * P],
                                           pick_w[:, t].rearrange("p e s -> p (e s)"), ident)
                    ins.then_inc(s("turned"), 1)
                    pe.wait_ge(s("picked"), i + (n1 + 2))
                    gather(1)
                    gather(0)
                    turn_hidden(QUAD - 1)
                    pe.wait_ge(s("xg_moved"), i * 2 + (n1 * 2 + 4))
                    pe.wait_ge(s("hidden_turned"), i * QUAD + (n2 * QUAD + QUAD))
                    for e in range(QUAD):
                        arrived(pe, i, 2 * QUAD + e)
                        w = slot4[(first_g + 2 * QUAD + e) % RING]
                        for n in range(2):
                            for k in range(4):
                                ins = pe.matmul(ps[e * SLOTS:(e + 1) * SLOTS, 6 + n, :],
                                                hidT[:, e, k * SLOTS:(k + 1) * SLOTS],
                                                w[:, k, n * 512:(n + 1) * 512],
                                                start=(k == 0), stop=(k == 3),
                                                skip_group_check=True)
                        ins.then_inc(chunk, 1)
                    pe.wait_ge(s("yg_moved"), i * 2 + (n2 * 2 + 2))
                    pe.wait_ge(s("back_moved"), i + (n2 + 1))
                    for t in range(2):
                        for n in range(2):
                            ins = pe.matmul(bank(2 * t + n), back[:, t * P:(t + 1) * P],
                                            yg[:, n * 512:(n + 1) * 512], start=False,
                                            stop=False, skip_group_check=True)
                    ins.then_inc(s("scattered"), 1)

            def experts(stage, layer):
                wait_x(pe, stage)
                transposes(f"x{stage}", x)
                wait_T(f"x{stage}")
                rw = Q("router_w").rearrange("p (l k n) -> p l k n", l=2, k=KT)
                for t in range(2):
                    for k in range(KT):
                        ins = pe.matmul(ps[:, 4, t * 36:(t + 1) * 36], xT[:, k, t * P:(t + 1) * P],
                                        rw[:, layer, k, :], start=(k == 0), stop=(k == KT - 1))
                ins.then_inc(sem("logits"), 1)
                residual(C("alpha"))
                pe.wait_ge(sem("chosen"), layer_no(stage))
                pe.matmul(ps[:, 5, 0:32], C("before"), s32[:, 0, :], start=True, stop=True)
                pe.matmul(ps[:, 5, 32:64], ones, s32[:, 0, :], start=True, stop=False)
                pe.matmul(ps[:, 5, 32:64], C("before"), s32[:, 1, :], start=False, stop=True)
                pe.matmul(ps[:, 5, 64:96], ones, s32[:, 0, :], start=True, stop=False)
                pe.matmul(ps[:, 5, 64:96], ones, s32[:, 1, :], start=False, stop=True)\
                    .then_inc(sem("ranked"), 1)
                b0 = base[stage]

                def arrived(eng, i, j):
                    g = b0 + j
                    eng.wait_ge(w_in[g % RING], i * (16 * QUAD_CHUNKS // RING)
                                + 16 * (g // RING + 1))

                moe_round(f"m{layer}", 0, b0, chunk_done, arrived)
                pe.wait_ge(sem(f"m{layer}_counted"), 1)
                n = pe.value_load(cnt_i[0:1, :], min_val=0, max_val=TOK)
                with pe.If(n > SLOTS):
                    pe.sem_inc(sem(f"m{layer}_more_chunk"), 1)
                    with pe.Fori(0, ROUNDS - 1) as rnd:
                        with pe.If(n - rnd * SLOTS > SLOTS):
                            def more(eng, i, j):
                                if j % RING == 0:
                                    eng.wait_ge(sem(f"m{layer}_more_in"),
                                                rnd * (16 * QUAD_CHUNKS * QUADS)
                                                + i * (16 * QUAD_CHUNKS) + 16 * (j + RING))
                            moe_round(f"m{layer}_more", rnd, b0, sem(f"m{layer}_more_chunk"), more)
                    pe.sem_inc(sem(f"m{layer}_more_over"), 1)

            def stick_breaking():
                g = base[STICK]
                wait_x(pe, STICK)
                transposes("x2", x)
                wait_T("x2")
                for c in range(4):
                    if c >= 2:
                        pe.wait_ge(sem("sk_qk"), c - 1)
                    channels(g + c, 4 + 2 * (c % 2))
                for c in range(2):
                    pe.wait_ge(sem("sk_qk"), 3 + c)
                    tokens(g + 4 + c, 4 + 2 * c)
                pe.wait_ge(sem("sk_v"), 2)

                def z(h):
                    if h >= 2:
                        pe.wait_ge(sem("sk_arg"), h - 1)
                    p0 = 64 * (h % 2)
                    q = sk_qk[p0:p0 + 64, h // 2, :]
                    k = sk_qk[p0:p0 + 64, KT + h // 2, :]
                    pe.matmul(ps[:, h % 2, 0:TOK], k[:, 0:P], q, start=True, stop=True)
                    pe.matmul(ps[:, h % 2, TOK:HEAD_COLS], k[:, P:TOK], q[:, P:TOK],
                              start=True, stop=True).then_inc(sem("sk_z"), 1)

                def later(h):
                    pe.wait_ge(sem("sk_spm"), h + 1)
                    b, m = 2 + h % 2, sk_spm[:, h % 2, :]
                    pe.matmul(ps[:, b, 0:TOK], C("from_on"), m[:, 0:TOK], start=True, stop=False,
                              skip_group_check=True)
                    pe.matmul(ps[:, b, P:TOK], ones, m[:, TOK:HEAD_COLS], start=False, stop=True,
                              skip_group_check=True)
                    pe.matmul(ps[:, b, TOK:HEAD_COLS], C("from_on"), m[:, TOK:HEAD_COLS],
                              start=True, stop=True).then_inc(sem("sk_later"), 1)

                def mix(h):
                    pe.wait_ge(sem("sk_a"), h + 1)
                    if h >= 4 and h % 2 == 0:
                        pe.wait_ge(sem("sk_oT"), h // 2 - 1)
                    p0, b, w = 64 * (h % 2), 4 + (h // 2) % 2, sk_a[:, h % 2, :]
                    pe.matmul(ps[p0:p0 + 64, b, 0:TOK], sk_v[:, 0, h * 64:(h + 1) * 64],
                              w[:, 0:TOK], start=True, stop=False, skip_group_check=True)
                    pe.matmul(ps[p0:p0 + 64, b, P:TOK], sk_v[:, 1, h * 64:(h + 1) * 64],
                              w[:, TOK:HEAD_COLS], start=False, stop=True,
                              skip_group_check=True).then_inc(sem("sk_o"), 1)

                for n in range(SB_HEADS + 3):
                    if n < SB_HEADS:
                        z(n)
                    if 1 <= n <= SB_HEADS:
                        later(n - 1)
                    if n >= 3:
                        mix(n - 3)
                pe.wait_ge(sem("sk_oT"), KT)
                output(g + 6, 2, sk_mixT, C("alpha"))

            projected = [0]
            holder = {}

            def half(kind, g, part, b):
                if part == 0:
                    if b in holder:
                        pe.wait_ge(sem("at_proj"), holder[b])
                    projected[0] += 1
                    holder[b] = projected[0]
                    arrive(pe, g)
                w = slot8[g % RING]
                if kind == "gate":
                    for m in (2 * part, 2 * part + 1):
                        for k in range(KT):
                            ins = pe.matmul(ps[:, b + part, (m % 2) * TOK:(m % 2 + 1) * TOK],
                                            w[:, k, m * P:(m + 1) * P], xT[:, k, :],
                                            start=(k == 0), stop=(k == KT - 1))
                else:
                    for k in range(KT):
                        ins = pe.matmul(bank(b + part), xT[:, k, part * P:(part + 1) * P],
                                        w[:, k, :], start=(k == 0), stop=(k == KT - 1))
                if part == 1:
                    ins.then_inc(chunk_done, 1)

            def weights_T(grp, b):
                for pr in range(4):
                    for t in range(2):
                        for hh in range(2):
                            h, c = 2 * pr + hh, (pr % 2) * TOK + t * P
                            ins = pe.matmul(ps[64 * hh:64 * hh + 64, b + pr // 2, c:c + P],
                                            at_wt[:, grp, t, h:h + 1].broadcast_to([P, 64]),
                                            ident, start=True, stop=True, skip_group_check=True)
                ins.then_inc(sem("at_wT"), 1)

            def attention(grp, ahead, extra=None):
                pe.wait_ge(sem("at_qk"), 2 * (grp + 1))
                pe.wait_ge(sem("at_proj"), projected[0])
                transposes(qk_turn(grp), at_qk)
                wait_T(qk_turn(grp))
                units = [(kind, g, part) for kind, g in ahead for part in range(2)]

                def fill():
                    if units:
                        half(*units.pop(0), 0)
                    elif extra:
                        extra.pop(0)()

                def scores(pr):
                    n = 4 * grp + pr
                    if pr:
                        pe.wait_ge(sem("at_masked"), n)
                    for hh in range(2):
                        h = 2 * pr + hh
                        p0, b = 64 * hh, 2 + hh
                        q = at_qkT[p0:p0 + 64, h // 2, :]
                        k = at_qkT[p0:p0 + 64, 4 + h // 2, :]
                        pe.matmul(ps[:, b, 0:P], q[:, 0:P], k[:, 0:P], start=True, stop=True)
                        ins = pe.matmul(ps[:, b, P:HEAD_COLS], q[:, P:TOK], k, start=True,
                                        stop=True)
                    ins.then_inc(sem("at_scored"), 1)

                def turn_p(pr):
                    n = 4 * grp + pr
                    pe.wait_ge(sem("at_p"), 4 * (n + 1))
                    if n:
                        pe.wait_ge(sem("at_pT_moved"), 2 * n)
                    for hh in range(2):
                        for c in range(3):
                            ins = pe.transpose(ps[:, 4 + hh, c * P:(c + 1) * P],
                                               at_p[:, hh, c * P:(c + 1) * P], ident)
                    ins.then_inc(sem("at_turned"), 1)

                def mix(pr):
                    n = 4 * grp + pr
                    pe.wait_ge(sem("at_pT_moved"), 2 * (n + 1))
                    if grp and pr % 2 == 0:
                        pe.wait_ge(sem("at_o_moved"), 2 * grp - 1 + pr // 2)
                    b, c = 6 + pr // 2, (pr % 2) * TOK
                    for first_tile in (True, False):
                        for hh in range(2):
                            h, w = 2 * pr + hh, at_pT[:, hh, :]
                            o = ps[64 * hh:64 * hh + 64, b, c:c + TOK]
                            if first_tile:
                                pe.matmul(o, at_v[:, 0, h * 64:(h + 1) * 64], w[:, 0:TOK],
                                          start=True, stop=False, skip_group_check=True)
                            else:
                                ins = pe.matmul(o[:, P:], at_v[:, 1, h * 64:(h + 1) * 64],
                                                w[:, TOK:HEAD_COLS], start=False, stop=True,
                                                skip_group_check=True)
                    ins.then_inc(sem("at_mixed"), 1)

                for pr in range(4):
                    scores(pr)
                    fill()
                    if pr:
                        mix(pr - 1)
                    turn_p(pr)
                fill()
                mix(3)
                fill()

            def ssd_dilated():
                g = base[SSD]
                pe.wait_ge(sem("h_ready"), 1)
                transposes("h4", at_h)
                wait_T("h4")
                dw = Q("dt_w").rearrange("p (k n) -> p k n", k=KT)
                for t in range(2):
                    for k in range(KT):
                        ins = pe.matmul(ps[:, 0, t * 16:(t + 1) * 16], xT[:, k, t * P:(t + 1) * P],
                                        dw[:, k, :], start=(k == 0), stop=(k == KT - 1))
                ins.then_inc(sem("ss_dt"), 1)
                for c in range(4):
                    if c >= 2:
                        pe.wait_ge(sem("ss_taken"), 8 * (c - 1))
                    channels(g + c, 4 + 2 * (c % 2))
                pe.wait_ge(sem("ss_a"), 1)
                av = dt_v[5]
                pe.matmul(ps[:, 1, 0:16], C("upto"), av[:, 0, :], start=True, stop=True)
                pe.matmul(ps[:, 1, 16:32], ones, av[:, 0, :], start=True, stop=False)
                pe.matmul(ps[:, 1, 16:32], C("upto"), av[:, 1, :], start=False, stop=True)\
                    .then_inc(sem("ss_cs"), 1)
                for c in range(2):
                    pe.wait_ge(sem("ss_taken"), 8 * (3 + c))
                    tokens(g + 4 + c, 4 + 2 * c)
                for u in range(4):
                    pe.wait_ge(sem("ss_silu"), 4 * (u % 2 + 1))
                    if u >= 2:
                        pe.wait_ge(sem("ss_x"), u - 1)
                    for j in range(4):
                        ins = pe.transpose(bank(2 + u % 2)[:, j * P:(j + 1) * P],
                                           xa[:, 4 * (u % 2) + j, (u // 2) * P:(u // 2 + 1) * P],
                                           ident)
                    ins.then_inc(sem("ss_turned"), 1)
                pe.wait_ge(sem("ss_silu"), 16)
                pe.wait_ge(sem("ss_z"), 2)
                for q in range(4):
                    B, Cc = xa[:, 8 + q, :], xa[:, 12 + q, :]
                    pe.matmul(ps[:, 4 + q, 0:TOK], B[:, 0:P], Cc, start=True, stop=True)
                    pe.matmul(ps[:, 4 + q, TOK:HEAD_COLS], B[:, P:TOK], Cc[:, P:TOK],
                              start=True, stop=True).then_inc(sem("ss_bc"), 1)
                pe.wait_ge(sem("ss_x"), 4)
                pe.wait_ge(sem("ss_xdt"), 1)
                pe.wait_ge(sem("ss_cb"), 4)

                def run_sum(h):
                    if h >= 2:
                        pe.wait_ge(sem("ss_arg"), 2 * (h - 1))
                    o = ps[:, 4 + h % 2, 0:TOK]
                    pe.matmul(o, av[:, 0, h:h + 1].broadcast_to([P, P]),
                              con[:, CONST["upto"][0]:CONST["ones"][1]], start=True, stop=False,
                              skip_group_check=True)
                    pe.matmul(ps[:, 4 + h % 2, P:TOK], av[:, 1, h:h + 1].broadcast_to([P, P]),
                              C("upto"), start=False, stop=True,
                              skip_group_check=True).then_inc(sem("ss_sum"), 1)

                def y(h):
                    pe.wait_ge(sem("ss_m"), h + 1)
                    m, b, c = ss_m[:, h % 2, :], h // 8, (h % 8) * 64
                    xh = [ss_x[:, t, h * 64:(h + 1) * 64] for t in range(2)]
                    pe.matmul(ps[:, b, c:c + 64], m[:, 0:P], xh[0], start=True, stop=True)
                    pe.matmul(ps[:, 2 + b, c:c + 64], m[:, P:TOK], xh[0], start=True, stop=False)
                    pe.matmul(ps[:, 2 + b, c:c + 64], m[:, TOK:HEAD_COLS], xh[1], start=False,
                              stop=True).then_inc(sem("ss_yh"), 1)

                units = [(kind, g + 6 + n, part) for n, kind in enumerate("qkv")
                         for part in range(2)]
                for n in range(SSD_HEADS + 2):
                    if n >= 2:
                        y(n - 2)
                    if n < SSD_HEADS:
                        run_sum(n)
                    if n in range(2, 14, 2):
                        half(*units.pop(0), 6)
                pe.wait_ge(sem("ss_y_taken"), 1)
                attention(0, [(kind, g + 9 + n) for n, kind in enumerate("qkv")])
                pe.wait_ge(sem("at_proj"), projected[0])
                pe.wait_ge(sem("ss_y"), 1)
                transposes("y4", ss_y)
                wait_T("y4")
                attention(1, [(kind, g + 12 + n) for n, kind in enumerate("qkv")])
                attention(2, [("gate", g + 15)])
                pe.wait_ge(sem("at_proj"), projected[0])

                def before(c, t):
                    if (c, t) == (1, 0):
                        pe.wait_ge(sem("at_weighed"), 1)
                        pe.wait_ge(sem("at_o_moved"), 6)
                        pe.wait_ge(sem("at_pT_moved"), 24)
                        weights_T(0, 4)
                        weights_T(1, 6)
                    elif (c, t) == (1, 1):
                        pe.wait_ge(sem("at_wT_used"), 1)
                        weights_T(2, 4)
                    elif (c, t) == (2, 0):
                        pe.wait_ge(sem("at_mixT"), 1)

                output(g + 16, 3, mixT12, ident, before)

            def block_attention():
                g = base[MOBA]
                pe.wait_ge(sem("h_ready"), 2 if first <= SSD else 1)
                transposes("h5", at_h)
                wait_T("h5")
                for n, kind in enumerate(("q", "k", "v", "gate")):
                    for part in range(2):
                        half(kind, g + n, part, 4 + 2 * (n % 2))
                no = 1 if SSD in on else 0
                attention(g_no(3), [(kind, g + 4 + n) for n, kind in enumerate("qkv")])

                def first_weights():
                    pe.wait_ge(sem("at_weighed"), no + 1)
                    pe.wait_ge(sem("at_proj"), projected[0])
                    weights_T(0, 0)

                attention(g_no(4), [("gate", g + 7)], [first_weights])
                pe.wait_ge(sem("at_weighed"), no + 2)
                pe.wait_ge(sem("at_pT_moved"), 8 * (g_no(4) + 1))
                weights_T(1, 4)
                pe.wait_ge(sem("at_mixT"), no + 1)

                def before(c, t):
                    if (c, t) == (1, 0):
                        pe.wait_ge(sem("at_mixT"), no + 2)

                output(g + 8, 2, mixT12, ident, before)

            pe.wait_ge(const_in, 32)
            run = {CONV: conv_mixers, MOE0: lambda: experts(MOE0, 0), STICK: stick_breaking,
                   MOE1: lambda: experts(MOE1, 1), SSD: ssd_dilated, MOBA: block_attention}
            for stage in on:
                run[stage]()

        @block.scalar
        def _(act):
            step = Steps(act, "act_step")
            roots = [0]

            def move_T(name, dst, scale=1.0):
                for b in (0, 2):
                    act.wait_ge(transposed, 4 * turn[name] + b + 1)
                    act.activation(dst[:, 0:4, (b // 2) * P:(b // 2 + 1) * P],
                                   bank(b).rearrange("p (k c) -> p k c", k=4), ACT.Copy,
                                   scale=scale).then_inc(moved_T, 1)

            def done(g):
                act.wait_ge(chunk_done, g + 1)

            def root(n):
                roots[0] += 1
                act.wait_ge(sem("squares"), roots[0])
                y = root_w[:, TOK:TOK + n]
                step.run(act.activation(y, root_w[:, 0:n], ACT.Ln))
                act.activation(y, y, ACT.Exp, scale=-0.5).then_inc(sem("roots"), 1)

            def two_banks(b):
                return ps[:, b:b + 2, :]

            def conv_mixers():
                g = base[CONV]
                move_T("x0", xT)
                done(g)
                act.activation(cv_sig.rearrange("p (b c) -> p b c", b=2), two_banks(4),
                               ACT.Sigmoid).then_inc(sem("cv_sig"), 1)
                for c in range(3):
                    done(g + 2 + c)
                    act.activation(cv_a[:, c].rearrange("p (b m) t -> p b (m t)", b=2),
                                   two_banks(4 + 2 * (c % 2)), ACT.Copy)\
                        .then_inc(sem("cv_a_out"), 1)
                root(TOK)
                act.wait_ge(sem("cv_normed"), 1)
                for m in range(4):
                    act.activation(cv_mixT[:, 4 + m, :], cv_g[:, m, :], ACT.Silu,
                                   bias=Q("norm_b")[:, m:m + 1], scale=Q("norm_g")[:, m:m + 1])\
                        .then_inc(sem("cv_mixed"), 1)
                root(2)

            def moe_round(tag, rnd, chunk, first_chunk):
                def s(name):
                    return sem(f"{tag}_{name}")

                n1, n2 = rnd * (QUADS + 1), rnd * QUADS

                def move_xg(count):
                    act.wait_ge(s("gathered"), count)
                    act.activation(xg[:, 4:8, :], ps[:, 7, :].rearrange("p (k s) -> p k s", k=4),
                                   ACT.Copy).then_inc(s("xg_moved"), 1)

                move_xg(n1 * 2 + 1)
                with act.Fori(0, QUADS) as i:
                    def move_hidden(e):
                        act.wait_ge(s("turning"), i * QUAD + (n2 * QUAD + e + 1))
                        act.activation(hidT[:, e, :], ps[:, 4 + e % 2, 0:P],
                                       ACT.Copy).then_inc(s("hidden_turned"), 1)

                    for e in range(QUAD):
                        act.wait_ge(chunk, i * QUAD_CHUNKS + (first_chunk + 2 * e + 2))
                        act.activation(sg[:, e % 2, :], ps[:, 4 + e % 2, 0:P],
                                       ACT.Silu).then_inc(s("silu"), 1)
                        if e:
                            move_hidden(e - 1)
                    act.wait_ge(s("turned"), i + (n2 + 1))
                    act.activation(back, ps[:, 4, 0:TOK], ACT.Copy).then_inc(s("back_moved"), 1)
                    move_xg(i * 2 + (n1 * 2 + 3))
                    move_hidden(QUAD - 1)
                    act.wait_ge(chunk, i * QUAD_CHUNKS + (first_chunk + QUAD_CHUNKS))
                    act.activation(yg[:, 0:512], bank(6), ACT.Copy).then_inc(s("yg_moved"), 1)

            def experts(stage, layer):
                move_T(f"x{stage}", xT)
                act.wait_ge(sem("shifted"), layer_no(stage))
                act.activation(ge, ge_m, ACT.Exp).then_inc(sem("g_exp"), 1)
                act.wait_ge(sem("gap"), layer_no(stage))
                act.activation(dexp[:, :, 0], gap, ACT.Exp).then_inc(sem("d_exp"), 1)
                moe_round(f"m{layer}", 0, chunk_done, base[stage])
                act.wait_ge(sem(f"m{layer}_counted"), 1)
                n = act.value_load(cnt_i[0:1, :], min_val=0, max_val=TOK)
                with act.If(n > SLOTS):
                    with act.Fori(0, ROUNDS - 1) as rnd:
                        with act.If(n - rnd * SLOTS > SLOTS):
                            moe_round(f"m{layer}_more", rnd, sem(f"m{layer}_more_chunk"),
                                      rnd * (QUAD_CHUNKS * QUADS) + 1)
                root(2)

            def stick_breaking():
                g = base[STICK]
                move_T("x2", xT)
                for c in range(4):
                    done(g + c)
                    act.activation(sk_qk[:, 4 * c:4 * c + 4].rearrange("p (b m) t -> p b (m t)", b=2),
                                   two_banks(4 + 2 * (c % 2)), ACT.Copy,
                                   scale=0.125 if c < 2 else 1.0).then_inc(sem("sk_qk"), 1)
                for c in range(2):
                    done(g + 4 + c)
                    act.activation(sk_v[:, :, c * 512:(c + 1) * 512], two_banks(4 + 2 * c),
                                   ACT.Copy).then_inc(sem("sk_v"), 1)

                def soft(h):
                    act.wait_ge(sem("sk_z"), h + 1)
                    step.run(act.activation(sk_az[:, h % 2, :], ps[:, h % 2, 0:HEAD_COLS],
                                            ACT.Abs))
                    step.run(act.activation(sk_e[:, h % 2, :], sk_az[:, h % 2, :], ACT.Exp,
                                            scale=-1.0))
                    if h >= 2:
                        act.wait_ge(sem("sk_sp"), h - 1)
                    act.activation(sk_l[:, h % 2, :], sk_e[:, h % 2, :], ACT.Ln,
                                   bias=ones[:, 0:1]).then_inc(sem("sk_l"), 1)

                def weights(h):
                    act.wait_ge(sem("sk_arg"), h + 1)
                    if h >= 2:
                        act.wait_ge(sem("sk_o"), h - 1)
                    act.activation(sk_a[:, h % 2, :], sk_arg[:, h % 2, :], ACT.Exp)\
                        .then_inc(sem("sk_a"), 1)

                def move_o(pr):
                    act.wait_ge(sem("sk_o"), 2 * pr + 2)
                    act.activation(sk_mixT[:, pr, :], ps[:, 4 + pr % 2, 0:TOK], ACT.Copy)\
                        .then_inc(sem("sk_oT"), 1)

                for n in range(SB_HEADS + 4):
                    if 2 <= n < SB_HEADS + 2:
                        weights(n - 2)
                    if n < SB_HEADS:
                        soft(n)
                    if n >= 4 and n % 2 == 1:
                        move_o((n - 5) // 2)
                root(2)

            def take(grp, kind, g, b=0):
                act.wait_ge(chunk_done, g + 1)
                if kind in "qk":
                    if grp or kind == "k":
                        act.wait_ge(sem("head_v"), 2 * grp + (kind == "k"))
                    act.activation(sq_words(grp).rearrange("p (t c) -> p t c", t=2), two_banks(b),
                                   ACT.Square).then_inc(sem("at_sq"), 1)
                    w = 512 * (kind == "k")
                    ins = act.activation(at_qk[:, :, w:w + 512], two_banks(b), ACT.Copy)
                elif kind == "v":
                    if grp:
                        act.wait_ge(sem("at_mixed"), 4 * grp)
                    ins = act.activation(at_v, two_banks(b), ACT.Copy)
                else:
                    ins = act.activation(gate_T(kind).rearrange("p (b m) t -> p b (m t)", b=2),
                                         two_banks(b), ACT.Silu)
                ins.then_inc(sem("at_proj"), 1)

            def gate_T(kind):
                return {"gate4": at_g4, "gate5": at_g5[:, 0:4], "gate6": at_g5[:, 4:8]}[kind]

            def head_root(grp, kind):
                w = int(kind == "k")
                act.wait_ge(sem("head_v"), 2 * grp + w + 1)
                step.run(act.activation(head_y[:, w], head_v[:, w], ACT.Ln))
                act.activation(head_y[:, w], head_y[:, w], ACT.Exp, scale=-0.5)\
                    .then_inc(sem("head_y"), 1)

            def attention(grp, out_g, ahead, between=lambda pr: None):
                move_T(qk_turn(grp), at_qkT, 0.125)

                def exps(pr):
                    n = 4 * grp + pr
                    act.wait_ge(sem("at_max"), n + 1)
                    if n:
                        act.wait_ge(sem("at_turned"), n)
                    for hh in range(2):
                        for t in range(2):
                            h = 2 * pr + hh
                            c = slice(0, P) if t == 0 else slice(P, HEAD_COLS)
                            act.activation(at_p[:, hh, c], at_sm[:, hh, c], ACT.Exp,
                                           bias=at_nmx[:, t, h:h + 1],
                                           accum_out=at_den[:, out_g, t, h:h + 1])\
                                .then_inc(sem("at_p"), 1)

                def move_pT(pr):
                    n = 4 * grp + pr
                    act.wait_ge(sem("at_turned"), n + 1)
                    if n:
                        act.wait_ge(sem("at_mixed"), n)
                    act.activation(at_pT[:, 0, :], ps[:, 4, 0:HEAD_COLS], ACT.Copy)\
                        .then_inc(sem("at_pT_moved"), 1)

                qk_ahead = len(ahead) == 3
                exps(0)
                move_pT(0)
                between(0)
                exps(1)
                take(grp + 1, *ahead[0])
                move_pT(1)
                between(1)
                exps(2)
                if qk_ahead:
                    head_root(grp + 1, "q")
                move_pT(2)
                exps(3)
                if qk_ahead:
                    take(grp + 1, *ahead[1])
                move_pT(3)
                if qk_ahead:
                    head_root(grp + 1, "k")
                    take(grp + 1, *ahead[2])

            def rms(stage):
                wait_x(act, stage)
                for t in range(2):
                    act.activation(junk[:, t, :], x[:, t, :], ACT.Square,
                                   accum_out=mv[:, t, 0:1]).then_inc(sem("h_sq"), 1)
                root(2)

            def ssd_dilated():
                g = base[SSD]
                rms(SSD)
                act.wait_ge(sem("ss_dabs"), 1)
                step.run(act.activation(dt_v[2], dt_v[1], ACT.Exp, scale=-1.0))
                act.activation(dt_v[3], dt_v[2], ACT.Ln, bias=ones[:, 0:1])\
                    .then_inc(sem("ss_soft"), 1)
                act.activation(dt_v[4][:, 0, :], Q("a_log"), ACT.Exp).then_inc(sem("ss_soft"), 1)
                w, b = Q("conv2_w").rearrange("p (m k) -> p m k", k=4), Q("conv2_b")
                for c in range(4):
                    done(g + c)
                    for m in range(4):
                        src = ps[:, 4 + 2 * (c % 2) + m // 2, (m % 2) * TOK:(m % 2 + 1) * TOK]
                        k = 4 * c + m
                        if c >= 2 and m == 0:
                            act.wait_ge(sem("ss_conv"), 4 * (c - 1))
                        act.activation(ss_pad[:, c % 2, m, 3:3 + TOK], src, ACT.Copy)\
                            .then_inc(sem("ss_taken"), 1)
                        act.activation(xa[:, k, :], src, ACT.Identity, bias=b[:, k:k + 1],
                                       scale=w[:, k, 3:4]).then_inc(sem("ss_taken"), 1)
                for m in range(16):
                    act.wait_ge(sem("ss_conv"), m + 1)
                    act.activation(xa[:, m, :], xa[:, m, :], ACT.Silu).then_inc(sem("ss_silu"), 1)
                for c in range(2):
                    done(g + 4 + c)
                    act.activation(ss_z[:, :, c * 512:(c + 1) * 512], two_banks(4 + 2 * c),
                                   ACT.Silu).then_inc(sem("ss_z"), 1)
                for q in range(4):
                    act.wait_ge(sem("ss_bc"), q + 1)
                    act.activation(ss_cb[:, q, :], ps[:, 4 + q, 0:HEAD_COLS], ACT.Copy)\
                        .then_inc(sem("ss_cb"), 1)
                for h in range(SSD_HEADS):
                    act.wait_ge(sem("ss_arg"), 2 * (h + 1))
                    act.activation(ss_arg[:, h % 2, :], ss_arg[:, h % 2, :], ACT.Exp)\
                        .then_inc(sem("ss_e"), 1)
                    if h in (5, 9, 13):
                        take(0, "qkv"[(h - 5) // 4], g + 6 + (h - 5) // 4, 6)
                    if h in (7, 11):
                        head_root(0, "qk"[(h - 7) // 4])

                def between(pr):
                    if pr == 0:
                        act.wait_ge(sem("ss_gated"), 2)
                        for t in range(2):
                            for q in range(4):
                                act.activation(ss_z[:, t, q * 256:(q + 1) * 256], ss_y[:, t, q * 256:(q + 1) * 256],
                                               ACT.Square,
                                               accum_out=ss_ss[:, 4 * t + q:4 * t + q + 1])\
                                    .then_inc(sem("ss_sq"), 1)
                        act.wait_ge(sem("ss_sq"), 8)
                    else:
                        root(8)

                attention(0, 0, [(kind, g + 9 + n) for n, kind in enumerate("qkv")], between)
                attention(1, 1, [(kind, g + 12 + n) for n, kind in enumerate("qkv")])
                attention(2, 2, [("gate4", g + 15)])
                act.wait_ge(sem("at_em"), 1)
                act.activation(at_em, at_em, ACT.Exp).then_inc(sem("at_em_exp"), 1)

            def block_attention():
                g = base[MOBA]
                rms(MOBA)
                n = g_no(3)
                take(n, "q", g, 4)
                take(n, "k", g + 1, 6)
                head_root(n, "q")
                head_root(n, "k")
                take(n, "v", g + 2, 4)
                take(n, "gate5", g + 3, 6)
                attention(n, 0, [(kind, g + 4 + c) for c, kind in enumerate("qkv")])
                attention(n + 1, 1, [("gate6", g + 7)])

            act.dma_start(con[:, :], a["constants"]).then_inc(const_in, 16)
            act.dma_start(par[:, :], a["params"]).then_inc(const_in, 16)
            act.wait_ge(const_in, 32)
            run = {CONV: conv_mixers, MOE0: lambda: experts(MOE0, 0), STICK: stick_breaking,
                   MOE1: lambda: experts(MOE1, 1), SSD: ssd_dilated, MOBA: block_attention}
            for stage in on:
                run[stage]()

        @block.vector
        def _(dve):
            step = Steps(dve, "dve_step")
            mul, add, sub, eq = ALU.mult, ALU.add, ALU.subtract, ALU.is_equal
            roots = [0]

            def two_banks(b):
                return ps[:, b:b + 2, :]

            def move_T(name, dst, banks=(1, 3), column=None):
                for b in banks:
                    kk = b % 2
                    dve.wait_ge(transposed, 4 * turn[name] + b + 1)
                    o = dst[:, 4 * kk:4 * kk + 4, (b // 2) * P:(b // 2 + 1) * P]
                    i = bank(b).rearrange("p (k c) -> p k c", k=4)
                    if column is None:
                        ins = dve.tensor_copy(o, i)
                    else:
                        f = column[:, 4 * kk:4 * kk + 4].unsqueeze(2).broadcast_to([P, 4, P])
                        ins = dve.tensor_tensor(o, i, f, mul)
                    ins.then_inc(moved_T, 1)

            def inv_root(o, i, scale, eps):
                n = int(np.prod(o.shape[1:]))
                dims = {2: "p (a) -> p a", 3: "p (a b) -> p a b"}[len(o.shape)]
                size = {} if len(o.shape) == 2 else {"b": o.shape[2]}
                v, y, w = (root_w[:, TOK * q:TOK * q + n].rearrange(dims, **size)
                           for q in range(3))
                dve.tensor_scalar(v, i, scale, eps, mul, add).then_inc(sem("squares"), 1)
                roots[0] += 1
                dve.wait_ge(sem("roots"), roots[0])
                step.run(dve.tensor_tensor(w, v, y, mul))
                step.run(dve.tensor_tensor(w, w, y, mul))
                step.run(dve.tensor_scalar(w, w, -0.5, 1.5, mul, add))
                step.run(dve.tensor_tensor(o, y, w, mul))

            def layer_norm(stage):
                for t in range(2):
                    for n in range(2):
                        step.add(dve.bn_stats(stats[:, t, n, :], bank(2 * t + n)))
                step.settle()
                for t in range(2):
                    step.add(dve.bn_aggr(mv[:, t, :], stats[:, t].rearrange("p n s -> p (n s)")))
                step.settle()
                inv_root(rstd[:, :, 0], mv[:, :, 1], 1.0, LN_EPS)
                for t in range(2):
                    step.add(dve.tensor_scalar(x[:, t].rearrange("p (n c) -> p n c", n=2),
                                               two_banks(2 * t), mv[:, t, 0:1], rstd[:, t, 0:1],
                                               sub, mul))
                step.settle()
                dve.wait_ge(ln_in, 32 * (stage - first + 1))
                step.run(dve.tensor_tensor(x, x, lnr[:, 0:1, :].broadcast_to([P, 2, D]), mul))
                dve.tensor_tensor(x, x, lnr[:, 1:2, :].broadcast_to([P, 2, D]), add)\
                    .then_inc(x_ready, 1)

            def taps(src, dst, w, n, bias=None):
                for k in range(n):
                    for m in range(4):
                        if k:
                            step.settle_but(3)
                            ins = dve.scalar_tensor_tensor(
                                dst[:, m, :], src[:, m, k:k + TOK], w[:, m * n + k:m * n + k + 1],
                                dst[:, m, :], mul, add)
                        elif bias is not None:
                            ins = dve.tensor_scalar(dst[:, m, :], src[:, m, 0:TOK],
                                                    w[:, m * n:m * n + 1], bias[:, m:m + 1],
                                                    mul, add)
                        else:
                            ins = dve.tensor_scalar(dst[:, m, :], src[:, m, 0:TOK],
                                                    w[:, m * n:m * n + 1], None, mul)
                        step.add(ins)

            def conv_mixers():
                g = base[CONV]
                step.add(dve.memset(cv_gpad[:, :, 0:CONV_B - 1], 0.0))
                step.add(dve.memset(cv_apad[:, :, 0:CONV_A - 1], 0.0))
                move_T("x0", xT)
                dve.wait_ge(chunk_done, g + 2)
                dve.wait_ge(sem("cv_sig"), 1)
                dve.tensor_tensor(cv_gpad[:, :, CONV_B - 1:],
                                  two_banks(6).rearrange("p b (m t) -> p (b m) t", m=2),
                                  cv_sig.rearrange("p (m t) -> p m t", m=4), mul)\
                    .then_inc(sem("cv_gated"), 1)
                dve.wait_ge(sem("cv_gated"), 1)
                step.settle()
                taps(cv_gpad, cv_g, Q("conv_b"), CONV_B, Q("conv_bb"))
                step.settle()
                dve.sem_inc(sem("cv_convolved"), 1)
                dve.wait_ge(sem("cv_a_out"), 3)
                step.run(dve.tensor_tensor(cv_apad[:, :, CONV_A - 1:], cv_a[:, 0], cv_a[:, 1], mul))
                taps(cv_apad, cv_y, Q("conv_a"), CONV_A)
                step.settle()
                dve.tensor_tensor(cv_mixT[:, 0:4, :], cv_a[:, 2], cv_y, mul)\
                    .then_inc(sem("cv_ya"), 1)
                dve.wait_ge(sem("cv_mean"), 1)
                step.run(dve.tensor_tensor(
                    cv_g, cv_g, ps[:, 0:1, 0:TOK].broadcast_to([P, 4, TOK]), sub))
                dve.tensor_tensor(cv_sq, cv_g, cv_g, mul).then_inc(sem("cv_squared"), 1)
                dve.wait_ge(sem("cv_var"), 1)
                inv_root(cv_rstd, ps[:, 1, 0:TOK], 1.0, LN_EPS)
                dve.tensor_tensor(cv_g, cv_g, cv_rstd.unsqueeze(1).broadcast_to([P, 4, TOK]), mul)\
                    .then_inc(sem("cv_normed"), 1)
                dve.wait_ge(chunk_done, g + 7)
                layer_norm(CONV)

            def first_max(values, n, rev, vmax, one):
                tie = (tie4 if n == 4 else tie8)
                rv = rev.unsqueeze(1).broadcast_to([P, 2, n])
                step.run(dve.tensor_reduce(vmax, values, AX, ALU.max))
                step.run(dve.tensor_tensor(tie, values, vmax.unsqueeze(2).broadcast_to([P, 2, n]),
                                           eq))
                step.run(dve.tensor_tensor(tie, tie, rv, mul))
                step.run(dve.tensor_reduce(gidx, tie, AX, ALU.max))
                step.run(dve.tensor_tensor(one, rv, gidx.unsqueeze(2).broadcast_to([P, 2, n]), eq))

            def moe_round(tag, rnd, chunk, first_chunk):
                def s(name):
                    return sem(f"{tag}_{name}")

                n1, n2 = rnd * (QUADS + 1), rnd * QUADS
                dims = [P, 2, QUAD, SLOTS]
                places = C("iota").unsqueeze(1).unsqueeze(1).broadcast_to(dims)

                def choose(four):
                    rk = rankm[:, :, four].unsqueeze(3).broadcast_to(dims)
                    dve.tensor_tensor(pick, places, rk, eq).then_inc(s("picked"), 1)

                def move_xg(count):
                    dve.wait_ge(s("gathered"), count)
                    dve.tensor_copy(xg[:, 0:4, :], ps[:, 6, :].rearrange("p (k s) -> p k s", k=4))\
                        .then_inc(s("xg_moved"), 1)

                choose(slice(0, QUAD))
                move_xg(n1 * 2 + 2)
                with dve.Fori(0, QUADS) as i:
                    dve.wait_ge(s("gathered"), i * 2 + (n1 * 2 + 2))
                    wt = wt32[:, :, bass.ds(i * QUAD, QUAD)].unsqueeze(3).broadcast_to(dims)
                    dve.tensor_tensor(pick_w, pick, wt, mul).then_inc(s("weighted"), 1)
                    dve.wait_ge(s("weighted"), i + (n2 + 1))
                    choose(bass.ds(i * QUAD + QUAD, QUAD))
                    for e in range(QUAD):
                        dve.wait_ge(s("silu"), i * QUAD + (n2 * QUAD + e + 1))
                        if e >= 2:
                            dve.wait_ge(s("turning"), i * QUAD + (n2 * QUAD + e - 1))
                        dve.tensor_tensor(hid[:, e % 2, :], sg[:, e % 2, :],
                                          ps[:, 4 + e % 2, P:TOK], mul)\
                            .then_inc(s("hidden"), 1)
                    move_xg(i * 2 + (n1 * 2 + 4))
                    dve.wait_ge(chunk, i * QUAD_CHUNKS + (first_chunk + QUAD_CHUNKS))
                    dve.tensor_copy(yg[:, 512:], bank(7)).then_inc(s("yg_moved"), 1)

            def experts(stage, layer):
                no = layer_no(stage)
                move_T(f"x{stage}", xT)
                dve.wait_ge(sem("logits"), no)
                rb = Q("router_b")[:, 36 * layer:36 * layer + 36]
                step.run(dve.tensor_tensor(lg, ps[:, 4, 0:72].rearrange("p (t n) -> p t n", t=2),
                                           rb.unsqueeze(1).broadcast_to([P, 2, 36]), add))
                gmax = gm[:, :, 0]
                first_max(lg[:, :, 0:4], 4, C("rev4"), gmax, g1h)
                dve.tensor_tensor(ge_m, lg[:, :, 0:4], gm.broadcast_to([P, 2, 4]), sub)\
                    .then_inc(sem("shifted"), 1)
                step.run(dve.tensor_tensor(
                    picked, lg[:, :, 4:36].rearrange("p t (g j) -> p t g j", g=4),
                    g1h.unsqueeze(3).broadcast_to([P, 2, 4, 8]), mul))
                step.run(dve.tensor_reduce(el, picked.rearrange("p t g j -> p t j g"), AX, add))
                first_max(el, 8, C("rev8"), top[:, 0, :, 0], one_hot[:, 0])
                step.run(dve.scalar_tensor_tensor(el, one_hot[:, 0], -3e38, el, mul, add))
                first_max(el, 8, C("rev8"), top[:, 1, :, 0], one_hot[:, 1])
                dve.tensor_tensor(gap, top[:, 1, :, 0], top[:, 0, :, 0], sub)\
                    .then_inc(sem("gap"), 1)
                step.run(dve.tensor_tensor(s8, one_hot[:, 0], one_hot[:, 1], add))
                four = [P, 2, 4, 8]

                def spread(o, i):
                    return dve.tensor_tensor(o.rearrange("p t (g j) -> p t g j", g=4),
                                             g1h.unsqueeze(3).broadcast_to(four),
                                             i.unsqueeze(2).broadcast_to(four), mul)

                spread(s32, s8).then_inc(sem("chosen"), 1)
                dve.wait_ge(sem("g_exp"), no)
                gt = gate[:, :, 0]
                step.run(dve.tensor_reduce(gt, ge, AX, add))
                dve.wait_ge(sem("d_exp"), no)
                step.run(dve.tensor_scalar(w12[:, 1, :, 0], dexp[:, :, 0], 1.0, None, add))
                step.run(dve.tensor_tensor(w12[:, 1, :, 0], w12[:, 1, :, 0], gt, mul))
                step.run(dve.reciprocal(w12[:, 0, :, 0], w12[:, 1, :, 0]))
                step.run(dve.tensor_tensor(w12[:, 1, :, 0], w12[:, 0, :, 0], dexp[:, :, 0], mul))
                step.run(dve.tensor_tensor(w8, one_hot[:, 0], w12[:, 0].broadcast_to([P, 2, 8]),
                                           mul))
                step.run(dve.tensor_tensor(tie8, one_hot[:, 1], w12[:, 1].broadcast_to([P, 2, 8]),
                                           mul))
                step.run(dve.tensor_tensor(w8, w8, tie8, add))
                step.run(spread(wt32, w8))
                step.run(dve.memset(rankm, -1.0))
                dve.wait_ge(sem("ranked"), no)
                step.run(dve.scalar_tensor_tensor(
                    rankm[:, :, 0:32], ps[:, 5, 0:64].rearrange("p (t n) -> p t n", t=2), 1.0,
                    s32, add, mul))
                step.run(dve.tensor_scalar(rankm[:, :, 0:32], rankm[:, :, 0:32], -1.0, None, add))
                step.run(dve.tensor_reduce(cnt_f, ps[:, 5, 64:96], AX, ALU.max))
                dve.tensor_copy(cnt_i[:, :], cnt_f).then_inc(sem(f"m{layer}_counted"), 1)
                moe_round(f"m{layer}", 0, chunk_done, base[stage])
                dve.wait_ge(sem(f"m{layer}_counted"), 1)
                n = dve.value_load(cnt_i[0:1, :], min_val=0, max_val=TOK)
                with dve.If(n > SLOTS):
                    dve.wait_ge(sem(f"m{layer}_scattered"), QUADS)
                    dve.tensor_scalar(rankm, rankm, -float(SLOTS), None, add)\
                        .then_inc(sem(f"m{layer}_more_lowered"), 1)
                    with dve.Fori(0, ROUNDS - 1) as rnd:
                        with dve.If(n - rnd * SLOTS > SLOTS):
                            dve.wait_ge(sem(f"m{layer}_more_lowered"), rnd + 1)
                            moe_round(f"m{layer}_more", rnd, sem(f"m{layer}_more_chunk"),
                                      rnd * (QUAD_CHUNKS * QUADS) + 1)
                            dve.wait_ge(sem(f"m{layer}_more_scattered"), rnd * QUADS + QUADS)
                            dve.tensor_scalar(rankm, rankm, -float(SLOTS), None, add)\
                                .then_inc(sem(f"m{layer}_more_lowered"), 1)
                dve.wait_ge(sem(f"m{layer}_scattered"), QUADS)
                layer_norm(stage)

            def stick_breaking():
                g = base[STICK]
                move_T("x2", xT)

                def soft(h):
                    dve.wait_ge(sem("sk_l"), h + 1)
                    if h >= 2:
                        dve.wait_ge(sem("sk_spm"), h - 1)
                    dve.scalar_tensor_tensor(
                        sk_sp[:, h % 2, :], ps[:, h % 2, 0:HEAD_COLS], 0.0, sk_l[:, h % 2, :],
                        ALU.max, add).then_inc(sem("sk_sp"), 1)

                def logs(h):
                    dve.wait_ge(sem("sk_later"), h + 1)
                    d = sk_d[:, h % 2, :]
                    step.run(dve.tensor_copy(d, ps[:, 2 + h % 2, 0:HEAD_COLS]))
                    step.run(dve.tensor_tensor(d, ps[:, h % 2, 0:HEAD_COLS], d, sub))
                    if h >= 2:
                        dve.wait_ge(sem("sk_a"), h - 1)
                    dve.scalar_tensor_tensor(sk_arg[:, h % 2, :], sk_d[:, h % 2, :], 0.0,
                                             C("stick_add"), ALU.min, add)\
                        .then_inc(sem("sk_arg"), 1)

                for n in range(SB_HEADS + 2):
                    if n >= 2:
                        logs(n - 2)
                    if 1 <= n <= SB_HEADS:
                        soft(n - 1)
                dve.wait_ge(chunk_done, g + 8)
                layer_norm(STICK)

            def rms_norm(no):
                dve.wait_ge(sem("h_sq"), 2 * no)
                inv_root(rstd[:, :, 0], mv[:, :, 0], 1.0 / D, RMS_EPS)
                dve.tensor_tensor(at_h, x, rstd.broadcast_to([P, 2, D]), mul)\
                    .then_inc(sem("h_ready"), 1)

            def mean_squares(grp, kind):
                w = int(kind == "k")
                dve.wait_ge(sem("at_sq"), 2 * grp + w + 1)
                if grp:
                    dve.wait_ge(sem("at_qk"), 2 * (grp - 1) + w + 1)
                step.run(dve.tensor_reduce(head_w[:, w].rearrange("p t h -> p (t h)"),
                                           sq_words(grp).rearrange("p (h d) -> p h d", d=64),
                                           AX, add))
                dve.tensor_scalar(head_v[:, w], head_w[:, w], 1.0 / 64, RMS_EPS, mul, add)\
                    .then_inc(sem("head_v"), 1)

            def attention(grp, out_g, mask, qk_ahead, between=lambda: None, last=lambda: None):
                move_T(qk_turn(grp), at_qkT)

                def masked(pr):
                    n = 4 * grp + pr
                    dve.wait_ge(sem("at_scored"), n + 1)
                    if n:
                        dve.wait_ge(sem("at_p"), 4 * n)
                    dve.tensor_tensor(at_sm, ps[:, 2:4, 0:HEAD_COLS],
                                      mask.unsqueeze(1).broadcast_to([P, 2, HEAD_COLS]), add)\
                        .then_inc(sem("at_masked"), 1)
                    dve.wait_ge(sem("at_masked"), n + 1)
                    hs = slice(2 * pr, 2 * pr + 2)
                    mx = at_mx[:, out_g]
                    step.add(dve.tensor_reduce(mx[:, 0, hs], at_sm[:, :, 0:P], AX, ALU.max))
                    step.add(dve.tensor_reduce(mx[:, 1, hs], at_sm[:, :, P:], AX, ALU.max))
                    step.settle()
                    dve.tensor_scalar(at_nmx[:, :, hs], mx[:, :, hs], -1.0, None, mul)\
                        .then_inc(sem("at_max"), 1)

                def move_pT(pr):
                    n = 4 * grp + pr
                    dve.wait_ge(sem("at_turned"), n + 1)
                    if n:
                        dve.wait_ge(sem("at_mixed"), n)
                    dve.tensor_copy(at_pT[:, 1, :], ps[:, 5, 0:HEAD_COLS])\
                        .then_inc(sem("at_pT_moved"), 1)

                def move_o(b):
                    dve.wait_ge(sem("at_mixed"), 4 * grp + 2 * b + 2)
                    dve.tensor_copy(at_oT[:, out_g, 2 * b:2 * b + 2, :],
                                    bank(6 + b).rearrange("p (k t) -> p k t", k=2))\
                        .then_inc(sem("at_o_moved"), 1)

                masked(0)
                move_pT(0)
                masked(1)
                move_pT(1)
                between()
                masked(2)
                if qk_ahead:
                    mean_squares(grp + 1, "q")
                move_pT(2)
                masked(3)
                move_o(0)
                move_pT(3)
                if qk_ahead:
                    mean_squares(grp + 1, "k")
                last()
                move_o(1)

            def ssd_dilated():
                g = base[SSD]
                rms_norm(1)
                move_T("h4", xT, range(4), Q("norm4"))
                pad0 = ss_pad[:, :, :, 0:3].rearrange("p b m t -> p (b m) t")
                step.add(dve.memset(pad0, 0.0))
                d = dt_v
                dve.wait_ge(sem("ss_dt"), 1)
                step.run(dve.tensor_tensor(
                    d[0], ps[:, 0, 0:32].rearrange("p (t h) -> p t h", t=2),
                    Q("dt_b").unsqueeze(1).broadcast_to([P, 2, 16]), add))
                dve.scalar_tensor_tensor(d[1], d[0], -1.0, d[0], mul, ALU.max)\
                    .then_inc(sem("ss_dabs"), 1)
                dve.wait_ge(sem("ss_soft"), 2)
                step.run(dve.scalar_tensor_tensor(d[6], d[0], 0.0, d[3], ALU.max, add))
                dve.scalar_tensor_tensor(d[5], d[6], -1.0,
                                         d[4][:, 0:1, :].broadcast_to([P, 2, 16]), mul, mul)\
                    .then_inc(sem("ss_a"), 1)
                w = Q("conv2_w")
                for c in range(4):
                    for m in range(4):
                        k = 4 * c + m
                        dve.wait_ge(sem("ss_taken"), 2 * k + 2)
                        for j in range(2):
                            step.run(dve.scalar_tensor_tensor(
                                xa[:, k, :], ss_pad[:, c % 2, m, j:j + TOK],
                                w[:, 4 * k + j:4 * k + j + 1], xa[:, k, :], mul, add))
                        dve.scalar_tensor_tensor(
                            xa[:, k, :], ss_pad[:, c % 2, m, 2:2 + TOK],
                            w[:, 4 * k + 2:4 * k + 3], xa[:, k, :], mul, add)\
                            .then_inc(sem("ss_conv"), 1)
                dve.wait_ge(sem("ss_cs"), 1)
                step.run(dve.tensor_scalar(
                    d[7], ps[:, 1, 0:32].rearrange("p (t h) -> p t h", t=2), -1.0, None, mul))
                for u in range(4):
                    dve.wait_ge(sem("ss_turned"), u + 1)
                    dve.tensor_copy(ss_x[:, u // 2, (u % 2) * 512:(u % 2 + 1) * 512],
                                    bank(2 + u % 2)).then_inc(sem("ss_x"), 1)
                dve.wait_ge(sem("ss_x"), 4)
                hd = [P, 16, 64]
                xh = [ss_x[:, t].rearrange("p (h d) -> p h d", d=64) for t in range(2)]
                yh = [ss_y[:, t].rearrange("p (h d) -> p h d", d=64) for t in range(2)]
                for t in range(2):
                    step.add(dve.tensor_tensor(
                        yh[t], xh[t], Q("d_skip").unsqueeze(2).broadcast_to(hd), mul))
                step.settle()
                for t in range(2):
                    step.add(dve.tensor_tensor(
                        xh[t], xh[t], d[6][:, t, :].unsqueeze(2).broadcast_to(hd), mul))
                step.settle()
                dve.sem_inc(sem("ss_xdt"), 1)

                def decay(h):
                    dve.wait_ge(sem("ss_sum"), h + 1)
                    o, p, m = ss_arg[:, h % 2, :], ps[:, 4 + h % 2, :], C("ssd_add")
                    dve.scalar_tensor_tensor(o[:, 0:TOK], p[:, 0:TOK], d[7][:, 0, h:h + 1],
                                             m[:, 0:TOK], add, add).then_inc(sem("ss_arg"), 1)
                    dve.scalar_tensor_tensor(o[:, TOK:], p[:, P:TOK], d[7][:, 1, h:h + 1],
                                             m[:, TOK:], add, add).then_inc(sem("ss_arg"), 1)

                def scan(h):
                    dve.wait_ge(sem("ss_e"), h + 1)
                    if h >= 2:
                        dve.wait_ge(sem("ss_yh"), h - 1)
                    dve.tensor_tensor(ss_m[:, h % 2, :], ss_arg[:, h % 2, :],
                                      ss_cb[:, h // 4, :], mul).then_inc(sem("ss_m"), 1)

                dve.wait_ge(sem("ss_cb"), 4)
                for n in range(SSD_HEADS + 1):
                    if n < SSD_HEADS:
                        if n >= 2:
                            dve.wait_ge(sem("ss_m"), n - 1)
                        decay(n)
                    if n >= 1:
                        scan(n - 1)
                    if n in (6, 10):
                        mean_squares(0, "qk"[(n - 6) // 4])
                dve.wait_ge(sem("ss_yh"), SSD_HEADS)
                for t in range(2):
                    v = ss_y[:, t].rearrange("p (n c) -> p n c", n=2)
                    step.add(dve.tensor_tensor(v, two_banks(2 * t), v, add))
                step.settle()
                dve.sem_inc(sem("ss_y_taken"), 1)

                def between():
                    dve.wait_ge(sem("ss_sq"), 8)
                    inv_root(ss_ss, ss_ss, 1.0 / 256, RMS_EPS)
                    dve.sem_inc(sem("ss_rstd"), 1)

                add4 = C("att_add").rearrange("p (n c) -> p n c", n=4)
                attention(0, 0, add4[:, 0, :], True, between)
                dve.wait_ge(sem("at_qk"), 2)
                move_T("y4", mixT12, range(4), Q("ssd_norm"))
                attention(1, 1, add4[:, 1, :], True)
                attention(2, 2, add4[:, 2, :], False)
                mx3, den3, em3, ed3, wt3 = (v.rearrange("p g t h -> p g (t h)") for v in
                                            (at_mx, at_den, at_em, at_ed, at_wt))
                lm, ls = (v.rearrange("p t h -> p (t h)") for v in (at_lm, at_ls))
                step.run(dve.tensor_reduce(lm, mx3.rearrange("p g n -> p n g"), AX, ALU.max))
                dve.tensor_tensor(em3, mx3, lm.unsqueeze(1).broadcast_to([P, 3, 16]), sub)\
                    .then_inc(sem("at_em"), 1)
                dve.wait_ge(sem("at_em_exp"), 1)
                step.run(dve.tensor_tensor(ed3, em3, den3, mul))
                step.run(dve.tensor_reduce(ls, ed3.rearrange("p g n -> p n g"), AX, add))
                step.run(dve.reciprocal(ls, ls))
                dve.tensor_tensor(wt3, em3, ls.unsqueeze(1).broadcast_to([P, 3, 16]), mul)\
                    .then_inc(sem("at_weighed"), 1)
                dve.wait_ge(sem("at_o_moved"), 6)
                for q in range(3):
                    o = at_oT[:, q].rearrange("p (b k) t -> p b (k t)", b=2)
                    dve.wait_ge(sem("at_wT"), q + 1)
                    dve.tensor_tensor(o, o, two_banks(6 if q == 1 else 4), mul)\
                        .then_inc(sem("at_wT_used"), 1)
                    dve.wait_ge(sem("at_wT_used"), q + 1)
                    if q:
                        step.run(dve.tensor_tensor(at_oT[:, 0], at_oT[:, 0], at_oT[:, q], add))
                dve.wait_ge(sem("at_proj"), 10)
                dve.tensor_tensor(mixT12[:, 8:12, :], at_oT[:, 0], at_g4, mul)\
                    .then_inc(sem("at_mixT"), 1)
                finish(g + 19)

            def finish(chunks):
                dve.wait_ge(chunk_done, chunks)
                dve.tensor_copy(x.rearrange("p t (n c) -> p (t n) c", n=2), ps[:, 0:4, :])\
                    .then_inc(x_ready, 1)

            def block_attention():
                g = base[MOBA]
                two = SSD in on
                rms_norm(2 if two else 1)
                move_T("h5", xT, range(4), Q("norm5"))
                causal = C("att_add")[:, 3 * HEAD_COLS:]
                n, no = g_no(3), (1 if two else 0)
                mean_squares(n, "q")
                mean_squares(n, "k")

                def reciprocals(grp):
                    dve.wait_ge(sem("at_p"), 16 * (n + grp + 1))
                    dve.reciprocal(at_wt[:, grp], at_den[:, grp]).then_inc(sem("at_weighed"), 1)

                def mixed(grp):
                    o = at_oT[:, grp].rearrange("p (b k) t -> p b (k t)", b=2)
                    wT = (3 if two else 0) + grp + 1
                    dve.wait_ge(sem("at_o_moved"), 2 * (n + grp + 1))
                    dve.wait_ge(sem("at_wT"), wT)
                    dve.tensor_tensor(o, o, two_banks(4 * grp), mul).then_inc(sem("at_wT_used"), 1)
                    dve.wait_ge(sem("at_wT_used"), wT)
                    dve.wait_ge(sem("at_proj"), (10 if two else 0) + 4 * (grp + 1))
                    dve.tensor_tensor(mixT12[:, 4 * grp:4 * grp + 4, :], at_oT[:, grp],
                                      at_g5[:, 4 * grp:4 * grp + 4], mul)\
                        .then_inc(sem("at_mixT"), 1)

                attention(n, 0, causal, True, last=lambda: reciprocals(0))
                attention(n + 1, 1, causal, False, last=lambda: (mixed(0), reciprocals(1)))
                mixed(1)
                finish(g + 10)

            dve.wait_ge(const_in, 32)
            run = {CONV: conv_mixers, MOE0: lambda: experts(MOE0, 0), STICK: stick_breaking,
                   MOE1: lambda: experts(MOE1, 1), SSD: ssd_dilated, MOBA: block_attention}
            if first != CONV:
                wait_x(dve, first)
            for stage in on:
                run[stage]()


INPUTS = ["x", "even_w_in", "even_w_out", "odd_w_qkv", "odd_w_o", "ln_mix_g", "ln_mix_b",
          "ln_ffn_g", "ln_ffn_b", "expert_w_up", "expert_w_down", "even_w_in_2", "even_w_out_2",
          "odd_w_in_2", "odd_w_out_2"]


def small_params(a):
    p = np.zeros((P, PARAM_WORDS), np.float32)

    def put(name, value):
        p[:, PARAM[name][0]:PARAM[name][1]] = value.reshape(P, -1)

    def column(v):
        return v.reshape(-1, P).T

    def row(v):
        return np.broadcast_to(v.reshape(1, -1), (P, v.size))

    put("conv_a", a["even_conv_a"][0].reshape(CONV_A, 4, P).transpose(2, 1, 0))
    put("conv_b", a["even_conv_b_w"][0].reshape(CONV_B, 4, P).transpose(2, 1, 0))
    put("conv_bb", column(a["even_conv_b_bias"][0]))
    put("norm_g", column(a["even_norm_b_g"][0]))
    put("norm_b", column(a["even_norm_b_b"][0]))
    w = np.concatenate([a["router_group_w"], a["router_expert_w"]], 2)
    put("router_w", w.reshape(2, KT, P, 36).transpose(2, 0, 1, 3))
    put("router_b", row(np.concatenate([a["router_group_b"], a["router_expert_b"]], 1)))
    put("dt_w", a["even_w_in_2"][0][:, 3072:3088].reshape(KT, P, 16).transpose(1, 0, 2))
    put("conv2_w", a["even_conv_w_2"][0].reshape(16, P, 4).transpose(1, 0, 2))
    put("conv2_b", column(a["even_conv_b_2"][0]))
    put("norm4", column(a["even_norm_w_2"][0]))
    put("norm5", column(a["odd_norm_w_2"][0]))
    put("ssd_norm", column(a["even_ssd_norm_w_2"][0]))
    put("dt_b", row(a["even_dt_bias_2"][0]))
    put("a_log", row(a["even_a_log_2"][0]))
    put("d_skip", row(a["even_d_skip_2"][0]))
    put("qk4", row(np.concatenate([a["even_q_norm_2"][0], a["even_k_norm_2"][0]])))
    put("qk5", row(np.concatenate([a["odd_q_norm_2"][0], a["odd_k_norm_2"][0]])))
    return p


def kernel(**inputs):
    import concourse.bacc as bacc
    from concourse.bass_utils import run_bass_kernel_spmd

    nc = bacc.Bacc("TRN2", target_bir_lowering=False, num_devices=1)
    host = {k: np.asarray(v) for k, v in inputs.items()}
    arrays = {name: np.ascontiguousarray(host[name]) for name in INPUTS}
    arrays["params"] = small_params(host)
    arrays["constants"] = constants()
    dram = {name: nc.dram_tensor(f"in_{name}", v.shape, mybir.dt.from_np(v.dtype),
                                 kind="ExternalInput").ap() for name, v in arrays.items()}
    out = nc.dram_tensor("out_x", (1, TOK, D), F32, kind="ExternalOutput").ap()
    build(nc, dram, out, *STAGES)
    r = run_bass_kernel_spmd(nc, [{f"in_{k}": v for k, v in arrays.items()}], core_ids=[0])
    return r.results[0]["out_x"]


STAGES = (0, 5)
```

```python
from contextlib import ExitStack

import numpy as np

import concourse.bass as bass
from concourse import mybir

F32 = mybir.dt.float32
I32 = mybir.dt.int32
ALU = mybir.AluOpType
ACT = mybir.ActivationFunctionType
AX = mybir.AxisListType.X

P = 128
TOK = 256
D = 1024
KT = D // P
ALPHA = 4 ** 0.25
LN_EPS, RMS_EPS = 1e-5, 1e-6
NEG = -1e30

EXPERTS, GROUPS, PER_GROUP = 32, 4, 8
QUAD = 4
QUADS = EXPERTS // QUAD
SLOTS = P // QUAD
ROUNDS = TOK // SLOTS
FFN = 512
QUAD_CHUNKS = 3 * QUAD

SB_HEADS = 16
SB_PAIRS = SB_HEADS // 2
SSD_HEADS = 16
CONV_A, CONV_B = 3, 31
HEAD_COLS = 384

RING = 6
SLOT_WORDS = 4096
EXTRA = (6, 7, 8)
ARENA = 15800

STAGE_CHUNKS = [7, QUAD_CHUNKS * QUADS, 8, QUAD_CHUNKS * QUADS, 19, 10]
BASE = [sum(STAGE_CHUNKS[:n]) for n in range(len(STAGE_CHUNKS))]
CONV, MOE0, STICK, MOE1, SSD, MOBA = range(6)

TURNS = ["x0", "x1", "x2", "x3", "h4", "qk0", "y4", "qk1", "qk2", "h5", "qk3", "qk4"]
TURN = {name: n for n, name in enumerate(TURNS)}


def layout(items):
    at, out = 0, {}
    for name, n in items:
        out[name] = (at, at + n)
        at += n
    return out, at


CONST, CONST_WORDS = layout([
    ("ident", P), ("alpha", P), ("upto", P), ("ones", P), ("before", P), ("from_on", P),
    ("mean", P), ("iota", SLOTS), ("rev8", 8), ("rev4", 4), ("stick_mul", HEAD_COLS),
    ("stick_add", HEAD_COLS), ("ssd_add", HEAD_COLS), ("att_add", 4 * HEAD_COLS),
    ("cos", 16), ("sin", 16)])
PARAM, PARAM_WORDS = layout([
    ("conv_a", 4 * CONV_A), ("conv_b", 4 * CONV_B), ("conv_bb", 4), ("norm_g", 4), ("norm_b", 4),
    ("router_w", 2 * KT * 36), ("router_b", 72), ("dt_w", KT * 16), ("conv2_w", 64),
    ("conv2_b", 16), ("norm4", 8), ("norm5", 8), ("ssd_norm", 8), ("dt_b", 16), ("a_log", 16),
    ("d_skip", 16), ("qk4", 128), ("qk5", 128)])


def constants():
    r = np.arange(P)
    row, col = r[:, None], r[None, :]
    c = np.zeros((P, CONST_WORDS), np.float32)

    def put(name, value, at=0):
        a, b = CONST[name]
        value = np.asarray(value, np.float32)
        c[:, a + at:a + at + value.shape[-1]] = value

    put("ident", row == col)
    put("alpha", (row == col) * np.float32(ALPHA))
    put("upto", row <= col)
    put("ones", np.ones((P, P)))
    put("before", row < col)
    put("from_on", row >= col)
    put("mean", np.full((P, P), 1.0 / 512))
    put("iota", np.broadcast_to(np.arange(SLOTS), (P, SLOTS)))
    put("rev8", np.broadcast_to(8 - np.arange(8), (P, 8)))
    put("rev4", np.broadcast_to(4 - np.arange(4), (P, 4)))

    def blocks(valid, keys_first):
        out = []
        for t, s in ((0, 0), (1, 0), (1, 1)):
            if keys_first:
                out.append(valid(t * P + col, s * P + row))
            else:
                out.append(valid(t * P + row, s * P + col))
        return np.concatenate(out, 1)

    strict = blocks(lambda t, s: s < t, True)
    put("stick_mul", strict)
    put("stick_add", np.where(strict, 0.0, NEG))
    put("ssd_add", np.where(blocks(lambda t, s: s <= t, True), 0.0, NEG))
    for n, (band, dil) in enumerate(((P, 1), (TOK, 4), (TOK, 16), (TOK, 1))):
        ok = blocks(lambda t, s: (s <= t) & (t - s <= band) & ((t - s) % dil == 0), False)
        put("att_add", np.where(ok, 0.0, NEG), n * HEAD_COLS)
    inv = np.float32(500000.0) ** (-np.arange(8, dtype=np.float32) * 2.0 / 16)
    ang = np.arange(TOK, dtype=np.float32)[:, None] * inv[None, :].astype(np.float32)
    for name, f in (("cos", np.cos), ("sin", np.sin)):
        table = f(ang.astype(np.float32)).reshape(2, P, 8).transpose(1, 0, 2).reshape(P, 16)
        put(name, table)
    return c


def build(nc, a, out, first=0, last=5):
    on = range(first, last + 1)
    turns = [n for n in TURNS if int({"x": n[1:], "h": n[1:], "y": n[1:], "q": "4" if n in
             ("qk0", "qk1", "qk2") else "5"}[n[0]]) in on]
    turn = {n: k for k, n in enumerate(turns)}
    base, at = {}, 0
    for n in on:
        base[n] = at
        at += STAGE_CHUNKS[n]
    in_ring = [g for g in range(at) if not any(g - base[n] in EXTRA for n in (MOE0, MOE1)
                                               if n in base)]
    seq = {g: n for n, g in enumerate(in_ring)}

    ctx = ExitStack()
    with ctx:
        def sb(name, words, dt=F32):
            return ctx.enter_context(nc.sbuf_tensor(name, [P, words], dt))

        sems = {}

        def sem(name):
            if name not in sems:
                sems[name] = ctx.enter_context(nc.semaphore(name))
            return sems[name]

        ring = sb("ring", RING * SLOT_WORDS)
        con = sb("constants_sb", CONST_WORDS)
        par = sb("params_sb", PARAM_WORDS)
        x_w = sb("x_tok", 2 * D)
        xT_w = sb("xT", KT * TOK)
        ln_w = sb("ln_rows", 2 * D)
        arena = sb("arena", ARENA)
        ps = ctx.enter_context(nc.psum_tensor("ps", [P, 8, 512], F32))

        def bank(b):
            return ps[:, b, :]

        def C(name):
            return con[:, CONST[name][0]:CONST[name][1]]

        def Q(name):
            return par[:, PARAM[name][0]:PARAM[name][1]]

        class Region:

            def __init__(self, at=0, whole=None, size=ARENA):
                self.at, self.whole, self.size = at, arena if whole is None else whole, size

            def __call__(self, words, pattern=None, **dims):
                v = self.whole[:, self.at:self.at + words]
                self.at += words
                assert self.at <= self.size, self.at
                return v.rearrange(pattern, **dims) if pattern else v

        ident, ones = C("ident"), C("ones")
        x = x_w[:, :].rearrange("p (t c) -> p t c", t=2)
        xT = xT_w[:, :].rearrange("p (k t) -> p k t", k=KT)
        lnr = ln_w[:, :].rearrange("p (r c) -> p r c", r=2)
        slot8 = [ring[:, s * SLOT_WORDS:(s + 1) * SLOT_WORDS].rearrange("p (k n) -> p k n", k=8)
                 for s in range(RING)]
        slot4 = [ring[:, s * SLOT_WORDS:(s + 1) * SLOT_WORDS].rearrange("p (k n) -> p k n", k=4)
                 for s in range(RING)]

        sm = Region(whole=sb("small", 640), size=640)
        stats = sm(24, "p (t n s) -> p t n s", t=2, n=2)
        mv = sm(4, "p (t s) -> p t s", t=2)
        rstd = sm(2, "p (t s) -> p t s", t=2)
        lg = sm(72, "p (t n) -> p t n", t=2)
        gm = sm(2, "p (t n) -> p t n", t=2)
        ge = sm(8, "p (t n) -> p t n", t=2)
        gate = sm(2, "p (t n) -> p t n", t=2)
        g1h = sm(8, "p (t n) -> p t n", t=2)
        tie4 = sm(8, "p (t n) -> p t n", t=2)
        picked = sm(64, "p (t g j) -> p t g j", t=2, g=4)
        el = sm(16, "p (t n) -> p t n", t=2)
        tie8 = sm(16, "p (t n) -> p t n", t=2)
        top = sm(4, "p (n t o) -> p n t o", n=2, t=2)
        one_hot = sm(32, "p (n t j) -> p n t j", n=2, t=2)
        dexp = sm(2, "p (t n) -> p t n", t=2)
        w12 = sm(4, "p (n t o) -> p n t o", n=2, t=2)
        s8 = sm(16, "p (t n) -> p t n", t=2)
        w8 = sm(16, "p (t n) -> p t n", t=2)
        s32 = sm(64, "p (t n) -> p t n", t=2)
        wt32 = sm(64, "p (t n) -> p t n", t=2)
        rankm = sm(72, "p (t n) -> p t n", t=2)
        cnt_f = sm(1)
        ge_m = sm(8, "p (t n) -> p t n", t=2)
        gap, gidx = sm(2), sm(2)
        cnt_i = sb("cnt_i", 1, I32)
        root_w = sb("root_w", 3 * TOK)

        x_in = sem("x_in")
        const_in = sem("const_in")
        ln_in = sem("ln_in")
        w_in = [sem(f"w_in{s}") for s in range(RING)]
        chunk_done = sem("chunk_done")
        transposed = sem("transposed")
        moved_T = sem("moved_T")
        x_ready = [sem(f"x_ready{t}") for t in range(2)]
        tile_out = sem("tile_out")

        def slot(g):
            return seq[g] % RING

        def arrive(eng, g):
            eng.wait_ge(w_in[slot(g)], 16 * (seq[g] // RING + 1))

        def wait_x(eng, stage, tiles=(0, 1)):
            for t in tiles:
                if stage == first:
                    eng.wait_ge(x_in, 32)
                else:
                    eng.wait_ge(x_ready[t], stage - first)

        def out_no(stage):
            return sum(n not in (MOE0, MOE1) for n in on if n <= stage)

        class Steps:

            def __init__(self, eng, name):
                self.eng, self.sem, self.n = eng, sem(name), 0

            def add(self, ins):
                ins.then_inc(self.sem, 1)
                self.n += 1

            def settle(self):
                if self.n:
                    self.eng.wait_ge(self.sem, self.n)

            def settle_but(self, n):
                self.eng.wait_ge(self.sem, self.n - n)

            def run(self, ins):
                self.add(ins)
                self.settle()

        r = Region()
        cv_mixT = r(KT * TOK, "p (k t) -> p k t", k=KT)
        cv_sig = r(4 * TOK)
        cv_gpad = r(4 * (TOK + CONV_B - 1), "p (m t) -> p m t", m=4)
        cv_g = r(4 * TOK, "p (m t) -> p m t", m=4)
        cv_sq = r(4 * TOK, "p (m t) -> p m t", m=4)
        cv_a = r(3 * 4 * TOK, "p (c m t) -> p c m t", c=3, m=4)
        cv_apad = r(4 * (TOK + CONV_A - 1), "p (m t) -> p m t", m=4)
        cv_y = r(4 * TOK, "p (m t) -> p m t", m=4)
        cv_rstd = r(TOK)

        r = Region()
        pick = r(2 * P, "p (t e s) -> p t e s", t=2, e=QUAD)
        xg = r(KT * P, "p (k s) -> p k s", k=KT)
        sg = r(2 * P, "p (b c) -> p b c", b=2)
        hid = r(2 * P, "p (b c) -> p b c", b=2)
        hidT = r(QUAD * P, "p (e c) -> p e c", e=QUAD)
        yg = r(D)
        extra = [r(SLOT_WORDS, "p (k n) -> p k n", k=4) for _ in EXTRA]
        pick_w = root_w[:, 0:2 * P].rearrange("p (t e s) -> p t e s", t=2, e=QUAD)
        back = root_w[:, 2 * P:2 * P + TOK]

        r = Region()
        sk_mixT = r(KT * TOK, "p (k t) -> p k t", k=KT)
        sk_qk = r(2 * KT * TOK, "p (k t) -> p k t", k=2 * KT)
        sk_v = r(2 * D, "p (t c) -> p t c", t=2)
        sk_z, sk_l, sk_sp, sk_a = (
            r(4 * HEAD_COLS, "p (b h c) -> p b h c", b=2, h=2) for _ in range(4))

        xa = arena[:, 0:16 * TOK].rearrange("p (m t) -> p m t", m=16)
        mixT12 = arena[:, 0:12 * TOK].rearrange("p (k t) -> p k t", k=12)
        r = Region(4096)
        ss_z = r(2 * D, "p (t c) -> p t c", t=2)
        ss_pad = r(2 * 4 * (TOK + 3), "p (b m t) -> p b m t", b=2, m=4)
        ss_x = r(2 * D, "p (t c) -> p t c", t=2)
        ss_cb = r(4 * HEAD_COLS, "p (g c) -> p g c", g=4)
        ss_arg = r(2 * HEAD_COLS, "p (b c) -> p b c", b=2)
        ss_m = r(2 * HEAD_COLS, "p (b c) -> p b c", b=2)
        ss_y = r(2 * D, "p (t c) -> p t c", t=2)
        ss_s = r(400)
        dt_v = [ss_s[:, 32 * n:32 * n + 32].rearrange("p (t h) -> p t h", t=2) for n in range(8)]
        ss_ss = ss_s[:, 256:264]

        at_v = arena[:, 2048:3072].rearrange("p (t c) -> p t c", t=2)
        at_pT = arena[:, 3072:3072 + 2 * HEAD_COLS].rearrange("p (h c) -> p h c", h=2)

        def sq_words(n):
            at = 0 if n == 0 and SSD in on else 4096
            return arena[:, at:at + D]

        def rope_words(n):
            at = D + (0 if n == 0 and SSD in on else 4096)
            return arena[:, at:at + 512].rearrange("p (n t h j) -> p n t h j", n=4, t=2, h=8)

        r = Region(6144)
        at_qk = r(2 * D, "p (t c) -> p t c", t=2)
        r = Region(6144 + 2 * 4 * (TOK + 3))
        at_qkT = r(KT * TOK, "p (k t) -> p k t", k=KT)
        at_o_words = r(4 * D)
        at_oT = at_o_words[:, 0:3 * D].rearrange("p (g k t) -> p g k t", g=3, k=4)
        at_g4 = at_o_words[:, 3 * D:4 * D].rearrange("p (k t) -> p k t", k=4)
        at_g5 = at_o_words[:, 2 * D:4 * D].rearrange("p (k t) -> p k t", k=8)
        at_p = ln_w[:, 0:2 * HEAD_COLS].rearrange("p (h c) -> p h c", h=2)
        at_sm = ln_w[:, 2 * HEAD_COLS:4 * HEAD_COLS].rearrange("p (h c) -> p h c", h=2)
        at_stat = ln_w[:, 4 * HEAD_COLS:]
        at_h = at_qk
        junk = at_qkT.rearrange("p k t -> p (k t)").rearrange("p (t c) -> p t c", t=2)

        def stat(n0, n, **dims):
            return at_stat[:, n0:n0 + n].rearrange(
                "p (g t h) -> p g t h" if "g" in dims else "p (t h) -> p t h", **dims)

        head_v, head_y, head_w = (stat(32 * n, 32, g=2, t=2) for n in range(3))
        at_nmx = stat(96, 16, t=2)
        at_mx, at_den, at_wt = (stat(112 + 48 * n, 48, g=3, t=2) for n in range(3))
        at_em, at_ed = (stat(256 + 48 * n, 48, g=3, t=2) for n in range(2))
        at_lm, at_ls = stat(352, 16, t=2), stat(368, 16, t=2)

        def layer_no(stage):
            return sum(s in on for s in (MOE0, MOE1) if s <= stage)

        def g_no(n):
            return n if SSD in on else n - 3

        def taken(n):
            n = n if SSD in on else n + 3
            return (0, 3, 6, 10, 14)[n] - (0 if SSD in on else 10)

        def qk_turn(n):
            return f"qk{n if SSD in on else n + 3}"

        def cols(w, c0, n=512):
            return w.rearrange("(k p) n -> p k n", p=P)[:, :, c0:c0 + n]

        def rows(w, c):
            return w[c * 512:(c + 1) * 512, :].rearrange("(k p) n -> p k n", p=P)

        up_v = a["expert_w_up"].rearrange("l e (k p) n -> l e p k n", p=P)
        down_v = a["expert_w_down"].rearrange("l e (k p) n -> l e p k n", p=P)
        out_v = out[0].rearrange("(t p) c -> p t c", p=P)

        def streamed(stage):
            if stage == CONV:
                w = a["even_w_in"][0]
                return [(8, cols(w, c)) for c in (2048, 1536, 512, 1024, 0)] + \
                    [(4, rows(a["even_w_out"][0], c)) for c in range(2)]
            if stage == STICK:
                return [(8, cols(a["odd_w_qkv"][0], 512 * c)) for c in (0, 2, 4, 1, 3, 5)] + \
                    [(4, rows(a["odd_w_o"][0], c)) for c in range(2)]
            if stage == SSD:
                w = a["even_w_in_2"][0]
                xbc = [1024 + 512 * c for c in range(4)]
                qkv = [q0 + 512 * g for g in range(3) for q0 in (3088, 4624, 6160)]
                return [(8, cols(w, c)) for c in xbc + [0, 512] + qkv + [7696]] + \
                    [(4, rows(a["even_w_out_2"][0], c)) for c in range(3)]
            w = a["odd_w_in_2"][0]
            return [(8, cols(w, c)) for c in (0, 1024, 2048, 3072, 512, 1536, 2560, 3584)] + \
                [(4, rows(a["odd_w_out_2"][0], c)) for c in range(2)]

        block = ctx.enter_context(nc.Block())

        @block.sync
        def _(sp):
            sp.dma_start(con[:, 0:P], a["constants"][:, 0:P]).then_inc(x_in, 16)
            sp.dma_start(x, a["x"][0].rearrange("(t p) c -> p t c", p=P)).then_inc(x_in, 16)

            def load(g, wide, src):
                if seq[g] >= RING:
                    sp.wait_ge(chunk_done, in_ring[seq[g] - RING] + 1)
                dst = (slot8 if wide == 8 else slot4)[slot(g)]
                sp.dma_start(dst, src).then_inc(w_in[slot(g)], 16)

            def expert_chunk(layer, quad, j):
                if j < 2 * QUAD:
                    return up_v[layer, quad * QUAD + j // 2, :, 4 * (j % 2):4 * (j % 2) + 4, :]
                return down_v[layer, quad * QUAD + (j - 2 * QUAD)]

            def experts(stage, layer):
                b0 = base[stage]
                for j in range(QUAD_CHUNKS):
                    if j not in EXTRA:
                        load(b0 + j, 4, expert_chunk(layer, 0, j))
                        continue
                    if j == EXTRA[0] and stage != first:
                        for t in range(2):
                            sp.wait_ge(x_ready[t], stage - first)
                    sp.dma_start(extra[j - EXTRA[0]], expert_chunk(layer, 0, j))\
                        .then_inc(sem(f"m{layer}_extra_in"), 16)
                with sp.Fori(1, QUADS) as i:
                    for j in range(QUAD_CHUNKS):
                        b = slot(b0 + QUAD_CHUNKS + j)
                        sp.wait_ge(chunk_done, i * QUAD_CHUNKS + (b0 + j - RING + 1))
                        sp.dma_start(slot4[b], expert_chunk(layer, i, j))\
                            .then_inc(w_in[b], 16)
                sp.wait_ge(sem(f"m{layer}_counted"), 1)
                n = sp.value_load(cnt_i[0:1, :], min_val=0, max_val=TOK)
                more_chunk = sem(f"m{layer}_more_chunk")
                with sp.If(n > SLOTS):
                    sp.wait_ge(chunk_done, b0 + QUAD_CHUNKS * QUADS)
                    with sp.Fori(0, ROUNDS - 1) as rnd:
                        with sp.If(n - rnd * SLOTS > SLOTS):
                            with sp.Fori(0, QUADS) as i:
                                for j in range(QUAD_CHUNKS):
                                    if j % RING == 0:
                                        sp.wait_ge(more_chunk, rnd * (QUAD_CHUNKS * QUADS)
                                                   + i * QUAD_CHUNKS + (j + 1))
                                    sp.dma_start(slot4[j % RING], expert_chunk(layer, i, j))\
                                        .then_inc(sem(f"m{layer}_more_in"), 16)
                    sp.wait_ge(sem(f"m{layer}_more_over"), 1)

            def small_loads():
                sp.dma_start(con[:, P:], a["constants"][:, P:]).then_inc(const_in, 16)
                sp.dma_start(par[:, :], a["params"]).then_inc(const_in, 16)

            if first != CONV:
                small_loads()
            for stage in on:
                if stage in (MOE0, MOE1):
                    experts(stage, stage // 2)
                else:
                    for n, (wide, src) in enumerate(streamed(stage)):
                        if stage == CONV and n == 2:
                            small_loads()
                        load(base[stage] + n, wide, src)
            for t in range(2):
                sp.wait_ge(x_ready[t], len(on))
                sp.dma_start(out_v[:, t, :], x[:, t, :]).then_inc(sem("out_stored"), 16)
            sp.wait_ge(sem("out_stored"), 32)

        @block.gpsimd
        def _(pool):
            step = Steps(pool, "pool_step")

            def rotate(grp, gains):
                mul = ALU.mult
                for w in range(2):
                    pool.wait_ge(sem("head_y"), 2 * grp + w + 1)
                    v, y, u = head_v[:, w], head_y[:, w], head_w[:, w]
                    step.run(pool.tensor_tensor(u, v, y, mul))
                    step.run(pool.tensor_tensor(u, u, y, mul))
                    step.run(pool.tensor_scalar(u, u, -0.5, 1.5, mul, ALU.add))
                    step.run(pool.tensor_tensor(u, u, y, mul))
                    heads = [P, 2, 8, 64]
                    qk = at_qk[:, :, 512 * w:512 * w + 512].rearrange("p t (h d) -> p t h d", d=64)
                    gain = gains[:, 64 * w:64 * w + 64].unsqueeze(1).unsqueeze(1)
                    pool.wait_ge(sem("at_proj"), taken(grp) + w + 1)
                    for t in range(2):
                        step.add(pool.tensor_tensor(
                            qk[:, t], qk[:, t], u[:, t].unsqueeze(2).broadcast_to([P, 8, 64]),
                            mul))
                    step.settle()
                    for t in range(2):
                        step.add(pool.tensor_tensor(
                            qk[:, t], qk[:, t], gain[:, 0].broadcast_to([P, 8, 64]), mul))
                    step.settle()
                    x1, x2 = qk[:, :, :, 0:8], qk[:, :, :, 8:16]
                    cos, sin = (C(n).rearrange("p (t j) -> p t j", t=2).unsqueeze(2)
                                .broadcast_to([P, 2, 8, 8]) for n in ("cos", "sin"))
                    part = rope_words(grp)
                    for n, (a_, f) in enumerate(((x1, cos), (x2, sin), (x2, cos), (x1, sin))):
                        step.add(pool.tensor_tensor(part[:, n], a_, f, mul))
                    step.settle()
                    step.add(pool.tensor_tensor(x1, part[:, 0], part[:, 1], ALU.subtract))
                    step.add(pool.tensor_tensor(x2, part[:, 2], part[:, 3], ALU.add))
                    step.settle()
                    pool.sem_inc(sem("at_qk"), 1)

            pool.wait_ge(const_in, 32)
            for n, stage in enumerate(on):
                if stage <= MOE1:
                    kind = "ffn" if stage % 2 else "mix"
                    if n:
                        for t in range(2):
                            pool.wait_ge(x_ready[t], n)
                    for k, v in enumerate((a[f"ln_{kind}_g"], a[f"ln_{kind}_b"])):
                        pool.dma_start(lnr[:, k, :], v[stage // 2:stage // 2 + 1, :]
                                       .broadcast_to([P, D])).then_inc(ln_in, 16)
                if stage == CONV:
                    four, mul = [P, 4, TOK], ALU.mult
                    wa = Q("conv_a").rearrange("p (m k) -> p m k", k=CONV_A)
                    step.run(pool.memset(cv_apad[:, :, 0:CONV_A - 1], 0.0))
                    pool.wait_ge(sem("cv_a_out"), 2)
                    step.run(pool.tensor_tensor(cv_apad[:, :, CONV_A - 1:], cv_a[:, 0], cv_a[:, 1],
                                                mul))
                    for k in range(CONV_A):
                        tap = wa[:, :, k:k + 1].broadcast_to(four)
                        src = cv_apad[:, :, k:k + TOK]
                        step.run(pool.tensor_tensor(cv_a[:, 0] if k else cv_y, src, tap, mul))
                        if k:
                            step.run(pool.tensor_tensor(cv_y, cv_y, cv_a[:, 0], ALU.add))
                    pool.wait_ge(sem("cv_a_out"), 3)
                    pool.tensor_tensor(cv_mixT[:, 0:4, :], cv_a[:, 2], cv_y, mul)\
                        .then_inc(sem("cv_ya"), 1)
                if stage == STICK:
                    for pr in range(SB_PAIRS):
                        sp = sk_sp[:, pr % 2]
                        pool.wait_ge(sem("sk_sp"), pr + 1)
                        pool.tensor_tensor(sp, sp, C("stick_mul").unsqueeze(1)
                                           .broadcast_to([P, 2, HEAD_COLS]), ALU.mult)\
                            .then_inc(sem("sk_spm"), 1)
                if stage in (MOE0, MOE1):
                    pool.wait_ge(ln_in, 32 * (n + 1))
                    pool.wait_ge(sem("normed"), layer_no(stage))
                    step.run(pool.tensor_tensor(x[:, 0], x[:, 0], lnr[:, 0, :], ALU.mult))
                    pool.tensor_tensor(x[:, 0], x[:, 0], lnr[:, 1, :], ALU.add)\
                        .then_inc(x_ready[0], 1)
                gains = Q("qk4") if stage == SSD else Q("qk5")
                if stage == SSD:
                    rotate(0, gains)
                    pool.wait_ge(sem("ss_y_taken"), 1)
                    for t in range(2):
                        pool.tensor_tensor(ss_y[:, t], ss_y[:, t], ss_z[:, t], ALU.mult)\
                            .then_inc(sem("ss_gated"), 1)
                    y4 = ss_y.rearrange("p t (q c) -> p (t q) c", q=4)
                    pool.wait_ge(sem("ss_rstd"), 1)
                    pool.tensor_tensor(y4, y4, ss_ss.unsqueeze(2).broadcast_to([P, 8, 256]),
                                       ALU.mult).then_inc(sem("ss_y"), 1)
                    rotate(1, gains)
                    rotate(2, gains)
                if stage == MOBA:
                    rotate(g_no(3), gains)
                    rotate(g_no(4), gains)

        @block.tensor
        def _(pe):
            def transposes(name, src, ready=lambda t: None):
                for b in range(4):
                    t, kk = b // 2, b % 2
                    if kk == 0:
                        ready(t)
                    for j in range(4):
                        k = 4 * kk + j
                        ins = pe.transpose(bank(b)[:, j * P:(j + 1) * P],
                                           src[:, t, k * P:(k + 1) * P], ident)
                    ins.then_inc(transposed, 1)

            def wait_T(name):
                pe.wait_ge(moved_T, 4 * (turn[name] + 1))

            def channels(g, b0):
                arrive(pe, g)
                w = slot8[slot(g)]
                for m in range(4):
                    o = ps[:, b0 + m // 2, (m % 2) * TOK:(m % 2 + 1) * TOK]
                    for k in range(KT):
                        ins = pe.matmul(o, w[:, k, m * P:(m + 1) * P], xT[:, k, :],
                                        start=(k == 0), stop=(k == KT - 1))
                ins.then_inc(chunk_done, 1)

            def tokens(g, b0):
                arrive(pe, g)
                w = slot8[slot(g)]
                for t in range(2):
                    for k in range(KT):
                        ins = pe.matmul(bank(b0 + t), xT[:, k, t * P:(t + 1) * P], w[:, k, :],
                                        start=(k == 0), stop=(k == KT - 1))
                ins.then_inc(chunk_done, 1)

            def residual(scale, tiles=(0, 1)):
                for t in tiles:
                    for n in range(2):
                        pe.matmul(bank(2 * t + n), scale, x[:, t, n * 512:(n + 1) * 512],
                                  start=True, stop=False, skip_group_check=True)

            def output_tile(g0, n_chunks, mixT, scale, c, t):
                if c == 0 and scale is not None:
                    residual(scale, (t,))
                if t == 0:
                    arrive(pe, g0 + c)
                w = slot4[slot(g0 + c)]
                for n in range(2):
                    for k in range(4):
                        ins = pe.matmul(bank(2 * t + n), mixT[:, 4 * c + k, t * P:(t + 1) * P],
                                        w[:, k, n * 512:(n + 1) * 512],
                                        start=(scale is None and c == 0 and k == 0),
                                        stop=(c == n_chunks - 1 and k == 3),
                                        skip_group_check=True)
                if t == 1:
                    ins.then_inc(chunk_done, 1)
                elif c == n_chunks - 1:
                    ins.then_inc(tile_out, 1)

            def output(g0, n_chunks, mixT, scale, first_chunk=0, before=lambda c, t: None):
                for c in range(first_chunk, n_chunks):
                    for t in range(2):
                        before(c, t)
                        output_tile(g0, n_chunks, mixT, scale, c, t)

            def conv_mixers():
                g = base[CONV]
                transposes("x0", x, lambda t: wait_x(pe, CONV, (t,)))
                wait_T("x0")
                channels(g, 4)
                channels(g + 1, 6)
                pe.wait_ge(const_in, 32)
                pe.wait_ge(sem("cv_sig"), 1)
                channels(g + 2, 4)
                pe.wait_ge(sem("cv_gated"), 1)
                channels(g + 3, 6)
                pe.wait_ge(sem("cv_a_out"), 1)
                channels(g + 4, 4)
                pe.wait_ge(sem("cv_ya"), 1)
                output_tile(g + 5, 2, cv_mixT, C("alpha"), 0, 0)
                pe.wait_ge(sem("cv_a_out"), 2)
                pe.wait_ge(sem("cv_convolved"), 1)
                for m in range(4):
                    ins = pe.matmul(ps[:, 6, 0:TOK], C("mean"), cv_g[:, m, :],
                                    start=(m == 0), stop=(m == 3))
                ins.then_inc(sem("cv_mean"), 1)
                output_tile(g + 5, 2, cv_mixT, C("alpha"), 0, 1)
                pe.wait_ge(sem("cv_squared"), 1)
                for m in range(4):
                    ins = pe.matmul(ps[:, 7, 0:TOK], C("mean"), cv_sq[:, m, :],
                                    start=(m == 0), stop=(m == 3))
                ins.then_inc(sem("cv_var"), 1)
                pe.wait_ge(sem("cv_mixed"), 4)
                output(g + 5, 2, cv_mixT, C("alpha"), 1)

            def moe_round(tag, rnd, chunk, arrived, peeled, place):
                def s(name):
                    return sem(f"{tag}_{name}")

                def gather(half):
                    for k in range(4):
                        for t in range(2):
                            kk = 4 * half + k
                            ins = pe.matmul(ps[:, 6 + half, k * P:(k + 1) * P],
                                            x[:, t, kk * P:(kk + 1) * P],
                                            pick[:, t].rearrange("p e s -> p (e s)"),
                                            start=(t == 0), stop=(t == 1))
                    ins.then_inc(s("gathered"), 1)

                n1, n2 = rnd * (QUADS + 1), rnd * QUADS
                pe.wait_ge(s("picked"), n1 + 1)
                gather(1)
                gather(0)

                def quad(i, chunk_at):
                    def up(e):
                        if e >= 2:
                            pe.wait_ge(s("hidden_turned"), i * QUAD + (n2 * QUAD + e - 1))
                        for half in range(2):
                            j = 2 * e + half
                            arrived(pe, i, j)
                            w = chunk_at(j)
                            for k in range(4):
                                for q in range(QUAD):
                                    ins = pe.matmul(
                                        ps[q * SLOTS:(q + 1) * SLOTS, 4 + e % 2, 0:TOK]
                                        .rearrange("p (g n) -> p g n", g=2),
                                        xg[:, 4 * half + k, e * SLOTS:(e + 1) * SLOTS],
                                        w[:, k, :].rearrange("p (g n) -> p g n", g=2)
                                        [:, :, q * P:(q + 1) * P],
                                        start=(j % 2 == 0 and k == 0), stop=(j % 2 == 1 and k == 3),
                                        skip_group_check=True)
                            ins.then_inc(chunk, 1)

                    def turn_hidden(e):
                        pe.wait_ge(s("hidden"), i * QUAD + (n2 * QUAD + e + 1))
                        pe.transpose(ps[:, 4 + e % 2, 0:P], hid[:, e % 2, :],
                                     ident).then_inc(s("turning"), 1)

                    pe.wait_ge(s("xg_moved"), i * 2 + (n1 * 2 + 2))
                    for e in range(QUAD):
                        up(e)
                        if e:
                            turn_hidden(e - 1)
                    pe.wait_ge(s("weighted"), i + (n2 + 1))
                    pe.wait_ge(s("hidden_turned"), i * QUAD + (n2 * QUAD + QUAD - 1))
                    for t in range(2):
                        ins = pe.transpose(ps[:, 4, t * P:(t + 1) * P],
                                           pick_w[:, t].rearrange("p e s -> p (e s)"), ident)
                    ins.then_inc(s("turned"), 1)
                    pe.wait_ge(s("picked"), i + (n1 + 2))
                    gather(1)
                    gather(0)
                    turn_hidden(QUAD - 1)
                    pe.wait_ge(s("xg_moved"), i * 2 + (n1 * 2 + 4))
                    pe.wait_ge(s("hidden_turned"), i * QUAD + (n2 * QUAD + QUAD))
                    for e in range(QUAD):
                        arrived(pe, i, 2 * QUAD + e)
                        w = chunk_at(2 * QUAD + e)
                        for n in range(2):
                            for k in range(4):
                                ins = pe.matmul(ps[e * SLOTS:(e + 1) * SLOTS, 6 + n, :],
                                                hidT[:, e, k * SLOTS:(k + 1) * SLOTS],
                                                w[:, k, n * 512:(n + 1) * 512],
                                                start=(k == 0), stop=(k == 3),
                                                skip_group_check=True)
                        ins.then_inc(chunk, 1)
                    pe.wait_ge(s("yg_moved"), i * 2 + (n2 * 2 + 2))
                    pe.wait_ge(s("back_moved"), i + (n2 + 1))
                    for t in range(2):
                        for n in range(2):
                            ins = pe.matmul(bank(2 * t + n), back[:, t * P:(t + 1) * P],
                                            yg[:, n * 512:(n + 1) * 512], start=False,
                                            stop=False, skip_group_check=True)
                    ins.then_inc(s("scattered"), 1)

                if peeled:
                    quad(0, peeled)
                with pe.Fori(1 if peeled else 0, QUADS) as i:
                    quad(i, place)

            def experts(stage, layer):
                transposes(f"x{stage}", x, lambda t: wait_x(pe, stage, (t,)))
                wait_T(f"x{stage}")
                rw = Q("router_w").rearrange("p (l k n) -> p l k n", l=2, k=KT)
                for t in range(2):
                    for k in range(KT):
                        ins = pe.matmul(ps[:, 4, t * 36:(t + 1) * 36], xT[:, k, t * P:(t + 1) * P],
                                        rw[:, layer, k, :], start=(k == 0), stop=(k == KT - 1))
                ins.then_inc(sem("logits"), 1)
                residual(C("alpha"))
                pe.wait_ge(sem("chosen"), layer_no(stage))
                pe.matmul(ps[:, 5, 0:32], C("before"), s32[:, 0, :], start=True, stop=True)
                pe.matmul(ps[:, 5, 32:64], ones, s32[:, 0, :], start=True, stop=False)
                pe.matmul(ps[:, 5, 32:64], C("before"), s32[:, 1, :], start=False, stop=True)
                pe.matmul(ps[:, 5, 64:96], ones, s32[:, 0, :], start=True, stop=False)
                pe.matmul(ps[:, 5, 64:96], ones, s32[:, 1, :], start=False, stop=True)\
                    .then_inc(sem("ranked"), 1)
                b0 = base[stage]

                def arrived(eng, i, j):
                    if not isinstance(i, int):
                        g = b0 + QUAD_CHUNKS + j
                        eng.wait_ge(w_in[slot(g)], i * (16 * QUAD_CHUNKS // RING)
                                    + 16 * (seq[g] // RING + 1 - QUAD_CHUNKS // RING))
                    elif j in EXTRA:
                        if j == EXTRA[0]:
                            eng.wait_ge(sem(f"m{layer}_extra_in"), 16 * len(EXTRA))
                    else:
                        arrive(eng, b0 + j)

                moe_round(f"m{layer}", 0, chunk_done, arrived,
                          lambda j: extra[j - EXTRA[0]] if j in EXTRA else slot4[slot(b0 + j)],
                          lambda j: slot4[slot(b0 + QUAD_CHUNKS + j)])
                pe.wait_ge(sem(f"m{layer}_counted"), 1)
                n = pe.value_load(cnt_i[0:1, :], min_val=0, max_val=TOK)
                with pe.If(n > SLOTS):
                    pe.sem_inc(sem(f"m{layer}_more_chunk"), 1)
                    with pe.Fori(0, ROUNDS - 1) as rnd:
                        with pe.If(n - rnd * SLOTS > SLOTS):
                            def more(eng, i, j):
                                if j % RING == 0:
                                    eng.wait_ge(sem(f"m{layer}_more_in"),
                                                rnd * (16 * QUAD_CHUNKS * QUADS)
                                                + i * (16 * QUAD_CHUNKS) + 16 * (j + RING))
                            moe_round(f"m{layer}_more", rnd, sem(f"m{layer}_more_chunk"), more,
                                      None, lambda j: slot4[j % RING])
                    pe.sem_inc(sem(f"m{layer}_more_over"), 1)

            def stick_breaking():
                g = base[STICK]
                transposes("x2", x, lambda t: wait_x(pe, STICK, (t,)))
                wait_T("x2")
                channels(g, 4)
                channels(g + 1, 6)
                pe.wait_ge(sem("sk_taken"), 1)
                tokens(g + 2, 4)
                units = [(c, part) for c in (3, 4, 5) for part in range(2)]

                def fill():
                    c, part = units.pop(0)
                    if part == 0:
                        pe.wait_ge(sem("sk_taken"), 2 if c == 3 else c)
                        arrive(pe, g + c)
                    w = slot8[slot(g + c)]
                    if c < 5:
                        for m in (2 * part, 2 * part + 1):
                            for k in range(KT):
                                ins = pe.matmul(ps[:, 6 + part, (m % 2) * TOK:(m % 2 + 1) * TOK],
                                                w[:, k, m * P:(m + 1) * P], xT[:, k, :],
                                                start=(k == 0), stop=(k == KT - 1))
                    else:
                        for k in range(KT):
                            ins = pe.matmul(bank(6 + part), xT[:, k, part * P:(part + 1) * P],
                                            w[:, k, :], start=(k == 0), stop=(k == KT - 1))
                    if part == 1:
                        ins.then_inc(chunk_done, 1)

                def z(pr):
                    if pr:
                        pe.wait_ge(sem("sk_z"), pr)
                    pe.wait_ge(sem("sk_taken"), 2 if pr < 4 else 5)
                    for hh in range(2):
                        p0 = 64 * hh
                        q = sk_qk[p0:p0 + 64, pr, :]
                        k = sk_qk[p0:p0 + 64, KT + pr, :]
                        pe.matmul(ps[:, hh, 0:TOK], k[:, 0:P], q, start=True, stop=True)
                        ins = pe.matmul(ps[:, hh, TOK:HEAD_COLS], k[:, P:TOK], q[:, P:TOK],
                                        start=True, stop=True)
                    ins.then_inc(sem("sk_scored"), 1)

                def later(pr):
                    pe.wait_ge(sem("sk_spm"), pr + 1)
                    if pr:
                        pe.wait_ge(sem("sk_d"), pr)
                    for hh in range(2):
                        b, m = 2 + hh, sk_sp[:, pr % 2, hh, :]
                        pe.matmul(ps[:, b, 0:TOK], C("from_on"), m[:, 0:TOK], start=True,
                                  stop=False, skip_group_check=True)
                        pe.matmul(ps[:, b, P:TOK], ones, m[:, TOK:HEAD_COLS], start=False,
                                  stop=True, skip_group_check=True)
                        ins = pe.matmul(ps[:, b, TOK:HEAD_COLS], C("from_on"),
                                        m[:, TOK:HEAD_COLS], start=True, stop=True)
                    ins.then_inc(sem("sk_later"), 1)

                def mix(pr):
                    pe.wait_ge(sem("sk_a"), pr + 1)
                    pe.wait_ge(sem("sk_taken"), 3 if pr < 4 else 6)
                    if pr >= 2:
                        pe.wait_ge(sem("sk_oT"), pr - 1)
                    for first_tile in (True, False):
                        for hh in range(2):
                            h, w = 2 * pr + hh, sk_a[:, pr % 2, hh, :]
                            o = ps[64 * hh:64 * hh + 64, 4 + pr % 2, 0:TOK]
                            if first_tile:
                                pe.matmul(o, sk_v[:, 0, h * 64:(h + 1) * 64], w[:, 0:TOK],
                                          start=True, stop=False, skip_group_check=True)
                            else:
                                ins = pe.matmul(o[:, P:], sk_v[:, 1, h * 64:(h + 1) * 64],
                                                w[:, TOK:HEAD_COLS], start=False, stop=True,
                                                skip_group_check=True)
                    ins.then_inc(sem("sk_o"), 1)

                z(0)
                for n in range(SB_PAIRS + 2):
                    if n + 1 < SB_PAIRS:
                        z(n + 1)
                    if n < 5:
                        fill()
                    if n == 0:
                        fill()
                    if n == SB_PAIRS:
                        pe.wait_ge(sem("sk_z"), SB_PAIRS)
                        pe.wait_ge(sem("sk_oT"), 4)
                        output_tile(g + 6, 2, sk_mixT, C("alpha"), 0, 0)
                    if n == SB_PAIRS + 1:
                        pe.wait_ge(sem("sk_d"), SB_PAIRS)
                        output_tile(g + 6, 2, sk_mixT, C("alpha"), 0, 1)
                    if 1 <= n <= SB_PAIRS:
                        later(n - 1)
                    if n >= 2:
                        mix(n - 2)
                pe.wait_ge(sem("sk_oT"), KT)
                output(g + 6, 2, sk_mixT, C("alpha"), 1)

            projected = [0]
            holder = {}

            def half(kind, g, part, b):
                if part == 0:
                    if b in holder:
                        pe.wait_ge(sem("at_proj"), holder[b])
                    projected[0] += 1
                    holder[b] = projected[0]
                    arrive(pe, g)
                w = slot8[slot(g)]
                if kind == "gate":
                    for m in (2 * part, 2 * part + 1):
                        for k in range(KT):
                            ins = pe.matmul(ps[:, b + part, (m % 2) * TOK:(m % 2 + 1) * TOK],
                                            w[:, k, m * P:(m + 1) * P], xT[:, k, :],
                                            start=(k == 0), stop=(k == KT - 1))
                else:
                    for k in range(KT):
                        ins = pe.matmul(bank(b + part), xT[:, k, part * P:(part + 1) * P],
                                        w[:, k, :], start=(k == 0), stop=(k == KT - 1))
                if part == 1:
                    ins.then_inc(chunk_done, 1)

            def weights_T(grp, b):
                for pr in range(4):
                    for t in range(2):
                        for hh in range(2):
                            h, c = 2 * pr + hh, (pr % 2) * TOK + t * P
                            ins = pe.matmul(ps[64 * hh:64 * hh + 64, b + pr // 2, c:c + P],
                                            at_wt[:, grp, t, h:h + 1].broadcast_to([P, 64]),
                                            ident, start=True, stop=True, skip_group_check=True)
                ins.then_inc(sem("at_wT"), 1)

            def attention(grp, ahead, extra=None):
                pe.wait_ge(sem("at_qk"), 2 * (grp + 1))
                pe.wait_ge(sem("at_proj"), projected[0])
                transposes(qk_turn(grp), at_qk)
                wait_T(qk_turn(grp))
                units = [(kind, g, part) for kind, g in ahead for part in range(2)]

                def fill():
                    if units:
                        half(*units.pop(0), 0)
                    elif extra:
                        extra.pop(0)()

                def scores(pr):
                    n = 4 * grp + pr
                    if pr:
                        pe.wait_ge(sem("at_masked"), n)
                    for hh in range(2):
                        h = 2 * pr + hh
                        p0, b = 64 * hh, 2 + hh
                        q = at_qkT[p0:p0 + 64, h // 2, :]
                        k = at_qkT[p0:p0 + 64, 4 + h // 2, :]
                        pe.matmul(ps[:, b, 0:P], q[:, 0:P], k[:, 0:P], start=True, stop=True)
                        ins = pe.matmul(ps[:, b, P:HEAD_COLS], q[:, P:TOK], k, start=True,
                                        stop=True)
                    ins.then_inc(sem("at_scored"), 1)

                def turn_p(pr):
                    n = 4 * grp + pr
                    pe.wait_ge(sem("at_p"), 4 * (n + 1))
                    if n:
                        pe.wait_ge(sem("at_pT_moved"), 2 * n)
                    for hh in range(2):
                        for c in range(3):
                            ins = pe.transpose(ps[:, 4 + hh, c * P:(c + 1) * P],
                                               at_p[:, hh, c * P:(c + 1) * P], ident)
                    ins.then_inc(sem("at_turned"), 1)

                def mix(pr):
                    n = 4 * grp + pr
                    pe.wait_ge(sem("at_pT_moved"), 2 * (n + 1))
                    if grp and pr % 2 == 0:
                        pe.wait_ge(sem("at_o_moved"), 2 * grp - 1 + pr // 2)
                    b, c = 6 + pr // 2, (pr % 2) * TOK
                    for first_tile in (True, False):
                        for hh in range(2):
                            h, w = 2 * pr + hh, at_pT[:, hh, :]
                            o = ps[64 * hh:64 * hh + 64, b, c:c + TOK]
                            if first_tile:
                                pe.matmul(o, at_v[:, 0, h * 64:(h + 1) * 64], w[:, 0:TOK],
                                          start=True, stop=False, skip_group_check=True)
                            else:
                                ins = pe.matmul(o[:, P:], at_v[:, 1, h * 64:(h + 1) * 64],
                                                w[:, TOK:HEAD_COLS], start=False, stop=True,
                                                skip_group_check=True)
                    ins.then_inc(sem("at_mixed"), 1)

                for pr in range(4):
                    scores(pr)
                    fill()
                    if pr:
                        mix(pr - 1)
                    turn_p(pr)
                fill()
                mix(3)
                fill()

            def ssd_dilated():
                g = base[SSD]
                transposes("h4", at_h, lambda t: pe.wait_ge(sem(f"h_ready{t}"), 1))
                wait_T("h4")
                dw = Q("dt_w").rearrange("p (k n) -> p k n", k=KT)
                for t in range(2):
                    for k in range(KT):
                        ins = pe.matmul(ps[:, 0, t * 16:(t + 1) * 16], xT[:, k, t * P:(t + 1) * P],
                                        dw[:, k, :], start=(k == 0), stop=(k == KT - 1))
                ins.then_inc(sem("ss_dt"), 1)
                for c in range(4):
                    if c >= 2:
                        pe.wait_ge(sem("ss_taken"), 8 * (c - 1))
                    channels(g + c, 4 + 2 * (c % 2))
                pe.wait_ge(sem("ss_a"), 1)
                av = dt_v[5]
                pe.matmul(ps[:, 1, 0:16], C("upto"), av[:, 0, :], start=True, stop=True)
                pe.matmul(ps[:, 1, 16:32], ones, av[:, 0, :], start=True, stop=False)
                pe.matmul(ps[:, 1, 16:32], C("upto"), av[:, 1, :], start=False, stop=True)\
                    .then_inc(sem("ss_cs"), 1)
                for c in range(2):
                    pe.wait_ge(sem("ss_taken"), 8 * (3 + c))
                    tokens(g + 4 + c, 4 + 2 * c)
                for u in range(4):
                    pe.wait_ge(sem("ss_silu"), 4 * (u % 2 + 1))
                    if u >= 2:
                        pe.wait_ge(sem("ss_x"), u - 1)
                    for j in range(4):
                        ins = pe.transpose(bank(2 + u % 2)[:, j * P:(j + 1) * P],
                                           xa[:, 4 * (u % 2) + j, (u // 2) * P:(u // 2 + 1) * P],
                                           ident)
                    ins.then_inc(sem("ss_turned"), 1)
                pe.wait_ge(sem("ss_silu"), 16)
                pe.wait_ge(sem("ss_z"), 2)
                for q in range(4):
                    B, Cc = xa[:, 8 + q, :], xa[:, 12 + q, :]
                    pe.matmul(ps[:, 4 + q, 0:TOK], B[:, 0:P], Cc, start=True, stop=True)
                    pe.matmul(ps[:, 4 + q, TOK:HEAD_COLS], B[:, P:TOK], Cc[:, P:TOK],
                              start=True, stop=True).then_inc(sem("ss_bc"), 1)
                pe.wait_ge(sem("ss_x"), 4)
                pe.wait_ge(sem("ss_xdt"), 1)
                pe.wait_ge(sem("ss_cb"), 4)

                def run_sum(h):
                    if h >= 2:
                        pe.wait_ge(sem("ss_arg"), 2 * (h - 1))
                    o = ps[:, 4 + h % 2, 0:TOK]
                    pe.matmul(o, av[:, 0, h:h + 1].broadcast_to([P, P]),
                              con[:, CONST["upto"][0]:CONST["ones"][1]], start=True, stop=False,
                              skip_group_check=True)
                    pe.matmul(ps[:, 4 + h % 2, P:TOK], av[:, 1, h:h + 1].broadcast_to([P, P]),
                              C("upto"), start=False, stop=True,
                              skip_group_check=True).then_inc(sem("ss_sum"), 1)

                def y(h):
                    pe.wait_ge(sem("ss_m"), h + 1)
                    m, b, c = ss_m[:, h % 2, :], h // 8, (h % 8) * 64
                    xh = [ss_x[:, t, h * 64:(h + 1) * 64] for t in range(2)]
                    pe.matmul(ps[:, b, c:c + 64], m[:, 0:P], xh[0], start=True, stop=True)
                    pe.matmul(ps[:, 2 + b, c:c + 64], m[:, P:TOK], xh[0], start=True, stop=False)
                    pe.matmul(ps[:, 2 + b, c:c + 64], m[:, TOK:HEAD_COLS], xh[1], start=False,
                              stop=True).then_inc(sem("ss_yh"), 1)

                units = [(kind, g + 6 + n, part) for n, kind in enumerate("qkv")
                         for part in range(2)]
                for n in range(SSD_HEADS + 2):
                    if n >= 2:
                        y(n - 2)
                    if n < SSD_HEADS:
                        run_sum(n)
                    if n in range(2, 14, 2):
                        half(*units.pop(0), 6)
                pe.wait_ge(sem("ss_y_taken"), 1)
                attention(0, [(kind, g + 9 + n) for n, kind in enumerate("qkv")])
                pe.wait_ge(sem("at_proj"), projected[0])
                pe.wait_ge(sem("ss_y"), 1)
                transposes("y4", ss_y)
                wait_T("y4")
                attention(1, [(kind, g + 12 + n) for n, kind in enumerate("qkv")])
                attention(2, [("gate", g + 15)])
                pe.wait_ge(sem("at_proj"), projected[0])

                def before(c, t):
                    if (c, t) == (1, 0):
                        pe.wait_ge(sem("at_weighed"), 1)
                        pe.wait_ge(sem("at_o_moved"), 6)
                        pe.wait_ge(sem("at_pT_moved"), 24)
                        weights_T(0, 4)
                        weights_T(1, 6)
                    elif (c, t) == (1, 1):
                        pe.wait_ge(sem("at_wT_used"), 1)
                        weights_T(2, 4)
                    elif (c, t) == (2, 0):
                        pe.wait_ge(sem("at_mixT"), 1)

                output(g + 16, 3, mixT12, None, before=before)

            def block_attention():
                g = base[MOBA]
                transposes("h5", at_h,
                           lambda t: pe.wait_ge(sem(f"h_ready{t}"), 2 if first <= SSD else 1))
                wait_T("h5")
                for n, kind in enumerate(("q", "k", "v", "gate")):
                    for part in range(2):
                        half(kind, g + n, part, 4 + 2 * (n % 2))
                no = 1 if SSD in on else 0
                attention(g_no(3), [(kind, g + 4 + n) for n, kind in enumerate("qkv")])

                def first_weights():
                    pe.wait_ge(sem("at_weighed"), no + 1)
                    pe.wait_ge(sem("at_proj"), projected[0])
                    weights_T(0, 0)

                attention(g_no(4), [("gate", g + 7)], [first_weights])
                pe.wait_ge(sem("at_weighed"), no + 2)
                pe.wait_ge(sem("at_pT_moved"), 8 * (g_no(4) + 1))
                weights_T(1, 4)
                pe.wait_ge(sem("at_mixT"), no + 1)

                def before(c, t):
                    if (c, t) == (1, 0):
                        pe.wait_ge(sem("at_mixT"), no + 2)

                output(g + 8, 2, mixT12, None, before=before)

            if first != CONV:
                pe.wait_ge(const_in, 32)
            run = {CONV: conv_mixers, MOE0: lambda: experts(MOE0, 0), STICK: stick_breaking,
                   MOE1: lambda: experts(MOE1, 1), SSD: ssd_dilated, MOBA: block_attention}
            for stage in on:
                run[stage]()

        @block.scalar
        def _(act):
            step = Steps(act, "act_step")
            roots = [0]

            def move_T(name, dst, scale=1.0):
                for b in (0, 2) if name[0] == "q" else (0, 1):
                    act.wait_ge(transposed, 4 * turn[name] + b + 1)
                    kk = b % 2
                    act.activation(dst[:, 4 * kk:4 * kk + 4, (b // 2) * P:(b // 2 + 1) * P],
                                   bank(b).rearrange("p (k c) -> p k c", k=4), ACT.Copy,
                                   scale=scale).then_inc(moved_T, 1)

            def done(g):
                act.wait_ge(chunk_done, g + 1)

            def root(n):
                roots[0] += 1
                act.wait_ge(sem("squares"), roots[0])
                y = root_w[:, TOK:TOK + n]
                step.run(act.activation(y, root_w[:, 0:n], ACT.Ln))
                act.activation(y, y, ACT.Exp, scale=-0.5).then_inc(sem("roots"), 1)

            def two_banks(b):
                return ps[:, b:b + 2, :]

            def conv_mixers():
                g = base[CONV]
                move_T("x0", xT)
                act.wait_ge(const_in, 32)
                done(g)
                act.activation(cv_sig.rearrange("p (b c) -> p b c", b=2), two_banks(4),
                               ACT.Sigmoid).then_inc(sem("cv_sig"), 1)
                for c in range(3):
                    done(g + 2 + c)
                    act.activation(cv_a[:, c].rearrange("p (b m) t -> p b (m t)", b=2),
                                   two_banks(4 + 2 * (c % 2)), ACT.Copy)\
                        .then_inc(sem("cv_a_out"), 1)
                root(TOK)
                act.wait_ge(sem("cv_normed"), 1)
                for m in range(4):
                    act.activation(cv_mixT[:, 4 + m, :], cv_g[:, m, :], ACT.Silu,
                                   bias=Q("norm_b")[:, m:m + 1], scale=Q("norm_g")[:, m:m + 1])\
                        .then_inc(sem("cv_mixed"), 1)
                root(1)
                root(1)

            def moe_round(tag, rnd, chunk, first_chunk):
                def s(name):
                    return sem(f"{tag}_{name}")

                n1, n2 = rnd * (QUADS + 1), rnd * QUADS

                def move_xg(count):
                    act.wait_ge(s("gathered"), count)
                    act.activation(xg[:, 4:8, :], ps[:, 7, :].rearrange("p (k s) -> p k s", k=4),
                                   ACT.Copy).then_inc(s("xg_moved"), 1)

                move_xg(n1 * 2 + 1)
                with act.Fori(0, QUADS) as i:
                    def move_hidden(e):
                        act.wait_ge(s("turning"), i * QUAD + (n2 * QUAD + e + 1))
                        act.activation(hidT[:, e, :], ps[:, 4 + e % 2, 0:P],
                                       ACT.Copy).then_inc(s("hidden_turned"), 1)

                    for e in range(QUAD):
                        act.wait_ge(chunk, i * QUAD_CHUNKS + (first_chunk + 2 * e + 2))
                        act.activation(sg[:, e % 2, :], ps[:, 4 + e % 2, 0:P],
                                       ACT.Silu).then_inc(s("silu"), 1)
                        if e:
                            move_hidden(e - 1)
                    act.wait_ge(s("turned"), i + (n2 + 1))
                    act.activation(back, ps[:, 4, 0:TOK], ACT.Copy).then_inc(s("back_moved"), 1)
                    move_xg(i * 2 + (n1 * 2 + 3))
                    move_hidden(QUAD - 1)
                    act.wait_ge(chunk, i * QUAD_CHUNKS + (first_chunk + QUAD_CHUNKS))
                    act.activation(yg[:, 0:512], bank(6), ACT.Copy).then_inc(s("yg_moved"), 1)

            def experts(stage, layer):
                move_T(f"x{stage}", xT)
                act.wait_ge(sem("exp_arg"), 2 * layer_no(stage) - 1)
                act.activation(ge, ge_m, ACT.Exp).then_inc(sem("exp_out"), 1)
                act.wait_ge(sem("exp_arg"), 2 * layer_no(stage))
                act.activation(dexp[:, :, 0], gap, ACT.Exp).then_inc(sem("exp_out"), 1)
                moe_round(f"m{layer}", 0, chunk_done, base[stage])
                act.wait_ge(sem(f"m{layer}_counted"), 1)
                n = act.value_load(cnt_i[0:1, :], min_val=0, max_val=TOK)
                with act.If(n > SLOTS):
                    with act.Fori(0, ROUNDS - 1) as rnd:
                        with act.If(n - rnd * SLOTS > SLOTS):
                            moe_round(f"m{layer}_more", rnd, sem(f"m{layer}_more_chunk"),
                                      rnd * (QUAD_CHUNKS * QUADS) + 1)
                root(2)

            def stick_breaking():
                g = base[STICK]
                move_T("x2", xT)
                def take(c):
                    done(g + c)
                    kind, half = c % 3, c // 3
                    b = (4, 6, 4, 6, 6, 6)[c]
                    if kind == 2:
                        ins = act.activation(sk_v[:, :, half * 512:(half + 1) * 512],
                                             two_banks(b), ACT.Copy)
                    else:
                        m = KT * kind + 4 * half
                        ins = act.activation(
                            sk_qk[:, m:m + 4].rearrange("p (b m) t -> p b (m t)", b=2),
                            two_banks(b), ACT.Copy, scale=1.0 if kind else 0.125)
                    ins.then_inc(sem("sk_taken"), 1)

                def copy_z(pr):
                    act.wait_ge(sem("sk_scored"), pr + 1)
                    if pr >= 2:
                        act.wait_ge(sem("sk_d"), pr - 1)
                    act.activation(sk_z[:, pr % 2], ps[:, 0:2, 0:HEAD_COLS], ACT.Copy)\
                        .then_inc(sem("sk_z"), 1)

                take(0)
                take(1)
                copy_z(0)
                take(2)
                for n in range(SB_PAIRS + 2):
                    if n < SB_PAIRS:
                        act.wait_ge(sem("sk_az"), n + 1)
                        step.run(act.activation(sk_l[:, n % 2], sk_l[:, n % 2], ACT.Exp,
                                                scale=-1.0))
                    if n >= 2:
                        act.wait_ge(sem("sk_arg"), n - 1)
                        act.activation(sk_a[:, n % 2], sk_a[:, n % 2], ACT.Exp)\
                            .then_inc(sem("sk_a"), 1)
                    if n < SB_PAIRS:
                        act.activation(sk_l[:, n % 2], sk_l[:, n % 2], ACT.Ln, bias=ones[:, 0:1])\
                            .then_inc(sem("sk_l"), 1)
                    if n + 1 < SB_PAIRS:
                        copy_z(n + 1)
                    if n in (0, 2, 4):
                        take(3 + n // 2)
                    if n >= 2:
                        act.wait_ge(sem("sk_o"), n - 1)
                        act.activation(sk_mixT[:, n - 2, :], ps[:, 4 + n % 2, 0:TOK], ACT.Copy)\
                            .then_inc(sem("sk_oT"), 1)
                root(1)
                root(1)

            def take(grp, kind, g, b=0):
                act.wait_ge(chunk_done, g + 1)
                if kind in "qk":
                    if grp or kind == "k":
                        act.wait_ge(sem("head_v"), 2 * grp + (kind == "k"))
                    act.activation(sq_words(grp).rearrange("p (t c) -> p t c", t=2), two_banks(b),
                                   ACT.Square).then_inc(sem("at_sq"), 1)
                    w = 512 * (kind == "k")
                    ins = act.activation(at_qk[:, :, w:w + 512], two_banks(b), ACT.Copy)
                elif kind == "v":
                    if grp:
                        act.wait_ge(sem("at_mixed"), 4 * grp)
                    ins = act.activation(at_v, two_banks(b), ACT.Copy)
                else:
                    ins = act.activation(gate_T(kind).rearrange("p (b m) t -> p b (m t)", b=2),
                                         two_banks(b), ACT.Silu)
                ins.then_inc(sem("at_proj"), 1)

            def gate_T(kind):
                return {"gate4": at_g4, "gate5": at_g5[:, 0:4], "gate6": at_g5[:, 4:8]}[kind]

            def head_root(grp, kind):
                w = int(kind == "k")
                act.wait_ge(sem("head_v"), 2 * grp + w + 1)
                step.run(act.activation(head_y[:, w], head_v[:, w], ACT.Ln))
                act.activation(head_y[:, w], head_y[:, w], ACT.Exp, scale=-0.5)\
                    .then_inc(sem("head_y"), 1)

            def attention(grp, out_g, ahead, between=lambda pr: None):
                move_T(qk_turn(grp), at_qkT, 0.125)

                def exps(pr):
                    n = 4 * grp + pr
                    act.wait_ge(sem("at_max"), n + 1)
                    if n:
                        act.wait_ge(sem("at_turned"), n)
                    for hh in range(2):
                        for t in range(2):
                            h = 2 * pr + hh
                            c = slice(0, P) if t == 0 else slice(P, HEAD_COLS)
                            act.activation(at_p[:, hh, c], at_sm[:, hh, c], ACT.Exp,
                                           bias=at_nmx[:, t, h:h + 1],
                                           accum_out=at_den[:, out_g, t, h:h + 1])\
                                .then_inc(sem("at_p"), 1)

                def move_pT(pr):
                    n = 4 * grp + pr
                    act.wait_ge(sem("at_turned"), n + 1)
                    if n:
                        act.wait_ge(sem("at_mixed"), n)
                    act.activation(at_pT[:, 0, :], ps[:, 4, 0:HEAD_COLS], ACT.Copy)\
                        .then_inc(sem("at_pT_moved"), 1)

                qk_ahead = len(ahead) == 3
                exps(0)
                move_pT(0)
                between(0)
                exps(1)
                take(grp + 1, *ahead[0])
                move_pT(1)
                between(1)
                exps(2)
                if qk_ahead:
                    head_root(grp + 1, "q")
                move_pT(2)
                exps(3)
                if qk_ahead:
                    take(grp + 1, *ahead[1])
                move_pT(3)
                if qk_ahead:
                    head_root(grp + 1, "k")
                    take(grp + 1, *ahead[2])

            def rms(stage):
                for t in range(2):
                    wait_x(act, stage, (t,))
                    act.activation(junk[:, t, :], x[:, t, :], ACT.Square,
                                   accum_out=mv[:, t, 0:1]).then_inc(sem("h_sq"), 1)
                root(2)

            def ssd_dilated():
                g = base[SSD]
                rms(SSD)
                act.wait_ge(sem("ss_dabs"), 1)
                step.run(act.activation(dt_v[2], dt_v[1], ACT.Exp, scale=-1.0))
                act.activation(dt_v[3], dt_v[2], ACT.Ln, bias=ones[:, 0:1])\
                    .then_inc(sem("ss_soft"), 1)
                act.activation(dt_v[4][:, 0, :], Q("a_log"), ACT.Exp).then_inc(sem("ss_soft"), 1)
                w, b = Q("conv2_w").rearrange("p (m k) -> p m k", k=4), Q("conv2_b")
                for c in range(4):
                    done(g + c)
                    for m in range(4):
                        src = ps[:, 4 + 2 * (c % 2) + m // 2, (m % 2) * TOK:(m % 2 + 1) * TOK]
                        k = 4 * c + m
                        if c >= 2 and m == 0:
                            act.wait_ge(sem("ss_conv"), 4 * (c - 1))
                        act.activation(ss_pad[:, c % 2, m, 3:3 + TOK], src, ACT.Copy)\
                            .then_inc(sem("ss_taken"), 1)
                        act.activation(xa[:, k, :], src, ACT.Identity, bias=b[:, k:k + 1],
                                       scale=w[:, k, 3:4]).then_inc(sem("ss_taken"), 1)
                for m in range(16):
                    act.wait_ge(sem("ss_conv"), m + 1)
                    act.activation(xa[:, m, :], xa[:, m, :], ACT.Silu).then_inc(sem("ss_silu"), 1)
                for c in range(2):
                    done(g + 4 + c)
                    act.activation(ss_z[:, :, c * 512:(c + 1) * 512], two_banks(4 + 2 * c),
                                   ACT.Silu).then_inc(sem("ss_z"), 1)
                for q in range(4):
                    act.wait_ge(sem("ss_bc"), q + 1)
                    act.activation(ss_cb[:, q, :], ps[:, 4 + q, 0:HEAD_COLS], ACT.Copy)\
                        .then_inc(sem("ss_cb"), 1)
                for h in range(SSD_HEADS):
                    act.wait_ge(sem("ss_arg"), 2 * (h + 1))
                    act.activation(ss_arg[:, h % 2, :], ss_arg[:, h % 2, :], ACT.Exp)\
                        .then_inc(sem("ss_e"), 1)
                    if h in (5, 9, 13):
                        take(0, "qkv"[(h - 5) // 4], g + 6 + (h - 5) // 4, 6)
                    if h in (7, 11):
                        head_root(0, "qk"[(h - 7) // 4])

                def between(pr):
                    if pr == 0:
                        act.wait_ge(sem("ss_gated"), 2)
                        for t in range(2):
                            for q in range(4):
                                act.activation(ss_z[:, t, q * 256:(q + 1) * 256], ss_y[:, t, q * 256:(q + 1) * 256],
                                               ACT.Square,
                                               accum_out=ss_ss[:, 4 * t + q:4 * t + q + 1])\
                                    .then_inc(sem("ss_sq"), 1)
                        act.wait_ge(sem("ss_sq"), 8)
                    else:
                        root(8)

                attention(0, 0, [(kind, g + 9 + n) for n, kind in enumerate("qkv")], between)
                attention(1, 1, [(kind, g + 12 + n) for n, kind in enumerate("qkv")])
                attention(2, 2, [("gate4", g + 15)])
                act.wait_ge(sem("at_em"), 1)
                act.activation(at_em, at_em, ACT.Exp).then_inc(sem("at_em_exp"), 1)

            def block_attention():
                g = base[MOBA]
                rms(MOBA)
                n = g_no(3)
                take(n, "q", g, 4)
                take(n, "k", g + 1, 6)
                head_root(n, "q")
                head_root(n, "k")
                take(n, "v", g + 2, 4)
                take(n, "gate5", g + 3, 6)
                attention(n, 0, [(kind, g + 4 + c) for c, kind in enumerate("qkv")])
                attention(n + 1, 1, [("gate6", g + 7)])

            if first != CONV:
                act.wait_ge(const_in, 32)
            run = {CONV: conv_mixers, MOE0: lambda: experts(MOE0, 0), STICK: stick_breaking,
                   MOE1: lambda: experts(MOE1, 1), SSD: ssd_dilated, MOBA: block_attention}
            for stage in on:
                run[stage]()

        @block.vector
        def _(dve):
            step = Steps(dve, "dve_step")
            mul, add, sub, eq = ALU.mult, ALU.add, ALU.subtract, ALU.is_equal
            roots = [0]

            def two_banks(b):
                return ps[:, b:b + 2, :]

            def move_T(name, dst, banks=None, column=None):
                if banks is None:
                    banks = (1, 3) if name[0] == "q" else (2, 3)
                for b in banks:
                    kk = b % 2
                    dve.wait_ge(transposed, 4 * turn[name] + b + 1)
                    o = dst[:, 4 * kk:4 * kk + 4, (b // 2) * P:(b // 2 + 1) * P]
                    i = bank(b).rearrange("p (k c) -> p k c", k=4)
                    if column is None:
                        ins = dve.tensor_copy(o, i)
                    else:
                        f = column[:, 4 * kk:4 * kk + 4].unsqueeze(2).broadcast_to([P, 4, P])
                        ins = dve.tensor_tensor(o, i, f, mul)
                    ins.then_inc(moved_T, 1)

            def inv_root(o, i, scale, eps):
                n = int(np.prod(o.shape[1:]))
                dims = {2: "p (a) -> p a", 3: "p (a b) -> p a b"}[len(o.shape)]
                size = {} if len(o.shape) == 2 else {"b": o.shape[2]}
                v, y, w = (root_w[:, TOK * q:TOK * q + n].rearrange(dims, **size)
                           for q in range(3))
                dve.tensor_scalar(v, i, scale, eps, mul, add).then_inc(sem("squares"), 1)
                roots[0] += 1
                dve.wait_ge(sem("roots"), roots[0])
                step.run(dve.tensor_tensor(w, v, y, mul))
                step.run(dve.tensor_tensor(w, w, y, mul))
                step.run(dve.tensor_scalar(w, w, -0.5, 1.5, mul, add))
                step.run(dve.tensor_tensor(o, y, w, mul))

            def layer_norm(stage):
                split = stage in (CONV, STICK)

                def statistics(t):
                    for n in range(2):
                        step.add(dve.bn_stats(stats[:, t, n, :], bank(2 * t + n)))
                    step.settle()
                    step.run(dve.bn_aggr(mv[:, t, :], stats[:, t].rearrange("p n s -> p (n s)")))

                def scaled(t):
                    return dve.tensor_scalar(x[:, t].rearrange("p (n c) -> p n c", n=2),
                                             two_banks(2 * t), mv[:, t, 0:1], rstd[:, t, 0:1],
                                             sub, mul)

                def gained(t):
                    dve.wait_ge(ln_in, 32 * (stage - first + 1))
                    step.run(dve.tensor_tensor(x[:, t], x[:, t], lnr[:, 0, :], mul))
                    dve.tensor_tensor(x[:, t], x[:, t], lnr[:, 1, :], add)\
                        .then_inc(x_ready[t], 1)

                if split:
                    for t in range(2):
                        if t == 0:
                            dve.wait_ge(tile_out, out_no(stage))
                        else:
                            dve.wait_ge(chunk_done, base[stage] + STAGE_CHUNKS[stage])
                        statistics(t)
                        inv_root(rstd[:, t], mv[:, t, 1:2], 1.0, LN_EPS)
                        step.run(scaled(t))
                        gained(t)
                else:
                    statistics(0)
                    statistics(1)
                    inv_root(rstd[:, :, 0], mv[:, :, 1], 1.0, LN_EPS)
                    scaled(0).then_inc(sem("normed"), 1)
                    step.run(scaled(1))
                    gained(1)

            def taps(src, dst, w, n, bias=None):
                for k in range(n):
                    for m in range(4):
                        if k:
                            step.settle_but(3)
                            ins = dve.scalar_tensor_tensor(
                                dst[:, m, :], src[:, m, k:k + TOK], w[:, m * n + k:m * n + k + 1],
                                dst[:, m, :], mul, add)
                        elif bias is not None:
                            ins = dve.tensor_scalar(dst[:, m, :], src[:, m, 0:TOK],
                                                    w[:, m * n:m * n + 1], bias[:, m:m + 1],
                                                    mul, add)
                        else:
                            ins = dve.tensor_scalar(dst[:, m, :], src[:, m, 0:TOK],
                                                    w[:, m * n:m * n + 1], None, mul)
                        step.add(ins)

            def conv_mixers():
                g = base[CONV]
                step.add(dve.memset(cv_gpad[:, :, 0:CONV_B - 1], 0.0))
                move_T("x0", xT)
                dve.wait_ge(const_in, 32)
                dve.wait_ge(chunk_done, g + 2)
                dve.wait_ge(sem("cv_sig"), 1)
                dve.tensor_tensor(cv_gpad[:, :, CONV_B - 1:],
                                  two_banks(6).rearrange("p b (m t) -> p (b m) t", m=2),
                                  cv_sig.rearrange("p (m t) -> p m t", m=4), mul)\
                    .then_inc(sem("cv_gated"), 1)
                dve.wait_ge(sem("cv_gated"), 1)
                step.settle()
                taps(cv_gpad, cv_g, Q("conv_b"), CONV_B, Q("conv_bb"))
                step.settle()
                dve.sem_inc(sem("cv_convolved"), 1)
                dve.wait_ge(sem("cv_mean"), 1)
                step.run(dve.tensor_tensor(
                    cv_g, cv_g, ps[:, 6:7, 0:TOK].broadcast_to([P, 4, TOK]), sub))
                dve.tensor_tensor(cv_sq, cv_g, cv_g, mul).then_inc(sem("cv_squared"), 1)
                dve.wait_ge(sem("cv_var"), 1)
                inv_root(cv_rstd, ps[:, 7, 0:TOK], 1.0, LN_EPS)
                dve.tensor_tensor(cv_g, cv_g, cv_rstd.unsqueeze(1).broadcast_to([P, 4, TOK]), mul)\
                    .then_inc(sem("cv_normed"), 1)
                layer_norm(CONV)

            def first_max(values, n, rev, vmax, one):
                tie = (tie4 if n == 4 else tie8)
                rv = rev.unsqueeze(1).broadcast_to([P, 2, n])
                step.run(dve.tensor_reduce(vmax, values, AX, ALU.max))
                step.run(dve.tensor_tensor(tie, values, vmax.unsqueeze(2).broadcast_to([P, 2, n]),
                                           eq))
                step.run(dve.tensor_tensor(tie, tie, rv, mul))
                step.run(dve.tensor_reduce(gidx, tie, AX, ALU.max))
                step.run(dve.tensor_tensor(one, rv, gidx.unsqueeze(2).broadcast_to([P, 2, n]), eq))

            def moe_round(tag, rnd, chunk, first_chunk):
                def s(name):
                    return sem(f"{tag}_{name}")

                n1, n2 = rnd * (QUADS + 1), rnd * QUADS
                dims = [P, 2, QUAD, SLOTS]
                places = C("iota").unsqueeze(1).unsqueeze(1).broadcast_to(dims)

                def choose(four):
                    rk = rankm[:, :, four].unsqueeze(3).broadcast_to(dims)
                    dve.tensor_tensor(pick, places, rk, eq).then_inc(s("picked"), 1)

                def move_xg(count):
                    dve.wait_ge(s("gathered"), count)
                    dve.tensor_copy(xg[:, 0:4, :], ps[:, 6, :].rearrange("p (k s) -> p k s", k=4))\
                        .then_inc(s("xg_moved"), 1)

                choose(slice(0, QUAD))
                move_xg(n1 * 2 + 2)
                with dve.Fori(0, QUADS) as i:
                    dve.wait_ge(s("gathered"), i * 2 + (n1 * 2 + 2))
                    wt = wt32[:, :, bass.ds(i * QUAD, QUAD)].unsqueeze(3).broadcast_to(dims)
                    dve.tensor_tensor(pick_w, pick, wt, mul).then_inc(s("weighted"), 1)
                    dve.wait_ge(s("weighted"), i + (n2 + 1))
                    choose(bass.ds(i * QUAD + QUAD, QUAD))
                    for e in range(QUAD):
                        dve.wait_ge(s("silu"), i * QUAD + (n2 * QUAD + e + 1))
                        if e >= 2:
                            dve.wait_ge(s("turning"), i * QUAD + (n2 * QUAD + e - 1))
                        dve.tensor_tensor(hid[:, e % 2, :], sg[:, e % 2, :],
                                          ps[:, 4 + e % 2, P:TOK], mul)\
                            .then_inc(s("hidden"), 1)
                    move_xg(i * 2 + (n1 * 2 + 4))
                    dve.wait_ge(chunk, i * QUAD_CHUNKS + (first_chunk + QUAD_CHUNKS))
                    dve.tensor_copy(yg[:, 512:], bank(7)).then_inc(s("yg_moved"), 1)

            def experts(stage, layer):
                no = layer_no(stage)
                move_T(f"x{stage}", xT)
                dve.wait_ge(sem("logits"), no)
                rb = Q("router_b")[:, 36 * layer:36 * layer + 36]
                step.run(dve.tensor_tensor(lg, ps[:, 4, 0:72].rearrange("p (t n) -> p t n", t=2),
                                           rb.unsqueeze(1).broadcast_to([P, 2, 36]), add))
                gmax = gm[:, :, 0]
                first_max(lg[:, :, 0:4], 4, C("rev4"), gmax, g1h)
                dve.tensor_tensor(ge_m, lg[:, :, 0:4], gm.broadcast_to([P, 2, 4]), sub)\
                    .then_inc(sem("exp_arg"), 1)
                step.run(dve.tensor_tensor(
                    picked, lg[:, :, 4:36].rearrange("p t (g j) -> p t g j", g=4),
                    g1h.unsqueeze(3).broadcast_to([P, 2, 4, 8]), mul))
                step.run(dve.tensor_reduce(el, picked.rearrange("p t g j -> p t j g"), AX, add))
                first_max(el, 8, C("rev8"), top[:, 0, :, 0], one_hot[:, 0])
                step.run(dve.scalar_tensor_tensor(el, one_hot[:, 0], -3e38, el, mul, add))
                first_max(el, 8, C("rev8"), top[:, 1, :, 0], one_hot[:, 1])
                dve.tensor_tensor(gap, top[:, 1, :, 0], top[:, 0, :, 0], sub)\
                    .then_inc(sem("exp_arg"), 1)
                step.run(dve.tensor_tensor(s8, one_hot[:, 0], one_hot[:, 1], add))
                four = [P, 2, 4, 8]

                def spread(o, i):
                    return dve.tensor_tensor(o.rearrange("p t (g j) -> p t g j", g=4),
                                             g1h.unsqueeze(3).broadcast_to(four),
                                             i.unsqueeze(2).broadcast_to(four), mul)

                spread(s32, s8).then_inc(sem("chosen"), 1)
                dve.wait_ge(sem("exp_out"), 2 * no - 1)
                gt = gate[:, :, 0]
                step.run(dve.tensor_reduce(gt, ge, AX, add))
                dve.wait_ge(sem("exp_out"), 2 * no)
                step.run(dve.tensor_scalar(w12[:, 1, :, 0], dexp[:, :, 0], 1.0, None, add))
                step.run(dve.tensor_tensor(w12[:, 1, :, 0], w12[:, 1, :, 0], gt, mul))
                step.run(dve.reciprocal(w12[:, 0, :, 0], w12[:, 1, :, 0]))
                step.run(dve.tensor_tensor(w12[:, 1, :, 0], w12[:, 0, :, 0], dexp[:, :, 0], mul))
                step.run(dve.tensor_tensor(w8, one_hot[:, 0], w12[:, 0].broadcast_to([P, 2, 8]),
                                           mul))
                step.run(dve.tensor_tensor(tie8, one_hot[:, 1], w12[:, 1].broadcast_to([P, 2, 8]),
                                           mul))
                step.run(dve.tensor_tensor(w8, w8, tie8, add))
                step.run(spread(wt32, w8))
                step.run(dve.memset(rankm, -1.0))
                dve.wait_ge(sem("ranked"), no)
                step.run(dve.scalar_tensor_tensor(
                    rankm[:, :, 0:32], ps[:, 5, 0:64].rearrange("p (t n) -> p t n", t=2), 1.0,
                    s32, add, mul))
                step.run(dve.tensor_scalar(rankm[:, :, 0:32], rankm[:, :, 0:32], -1.0, None, add))
                step.run(dve.tensor_reduce(cnt_f, ps[:, 5, 64:96], AX, ALU.max))
                dve.tensor_copy(cnt_i[:, :], cnt_f).then_inc(sem(f"m{layer}_counted"), 1)
                moe_round(f"m{layer}", 0, chunk_done, base[stage])
                dve.wait_ge(sem(f"m{layer}_counted"), 1)
                n = dve.value_load(cnt_i[0:1, :], min_val=0, max_val=TOK)
                with dve.If(n > SLOTS):
                    dve.wait_ge(sem(f"m{layer}_scattered"), QUADS)
                    dve.tensor_scalar(rankm, rankm, -float(SLOTS), None, add)\
                        .then_inc(sem(f"m{layer}_more_lowered"), 1)
                    with dve.Fori(0, ROUNDS - 1) as rnd:
                        with dve.If(n - rnd * SLOTS > SLOTS):
                            dve.wait_ge(sem(f"m{layer}_more_lowered"), rnd + 1)
                            moe_round(f"m{layer}_more", rnd, sem(f"m{layer}_more_chunk"),
                                      rnd * (QUAD_CHUNKS * QUADS) + 1)
                            dve.wait_ge(sem(f"m{layer}_more_scattered"), rnd * QUADS + QUADS)
                            dve.tensor_scalar(rankm, rankm, -float(SLOTS), None, add)\
                                .then_inc(sem(f"m{layer}_more_lowered"), 1)
                dve.wait_ge(sem(f"m{layer}_scattered"), QUADS)
                layer_norm(stage)

            def stick_breaking():
                g = base[STICK]
                move_T("x2", xT)

                def magnitude(pr):
                    dve.wait_ge(sem("sk_z"), pr + 1)
                    if pr >= 2:
                        dve.wait_ge(sem("sk_sp"), pr - 1)
                    z = sk_z[:, pr % 2]
                    dve.scalar_tensor_tensor(sk_l[:, pr % 2], z, -1.0, z, mul, ALU.max)\
                        .then_inc(sem("sk_az"), 1)

                def soft(pr):
                    dve.wait_ge(sem("sk_l"), pr + 1)
                    if pr >= 2:
                        dve.wait_ge(sem("sk_later"), pr - 1)
                    dve.scalar_tensor_tensor(sk_sp[:, pr % 2], sk_z[:, pr % 2], 0.0,
                                             sk_l[:, pr % 2], ALU.max, add)\
                        .then_inc(sem("sk_sp"), 1)

                def logs(pr):
                    dve.wait_ge(sem("sk_later"), pr + 1)
                    if pr >= 2:
                        dve.wait_ge(sem("sk_o"), pr - 1)
                    w = sk_a[:, pr % 2]
                    dve.tensor_tensor(w, sk_z[:, pr % 2], ps[:, 2:4, 0:HEAD_COLS], sub)\
                        .then_inc(sem("sk_d"), 1)
                    dve.wait_ge(sem("sk_d"), pr + 1)
                    dve.scalar_tensor_tensor(w, w, 0.0, C("stick_add").unsqueeze(1)
                                             .broadcast_to([P, 2, HEAD_COLS]), ALU.min, add)\
                        .then_inc(sem("sk_arg"), 1)

                magnitude(0)
                for n in range(SB_PAIRS + 1):
                    if n >= 1:
                        logs(n - 1)
                    if n < SB_PAIRS:
                        soft(n)
                    if n + 1 < SB_PAIRS:
                        magnitude(n + 1)
                layer_norm(STICK)

            def rms_norm(no):
                dve.wait_ge(sem("h_sq"), 2 * no)
                inv_root(rstd[:, :, 0], mv[:, :, 0], 1.0 / D, RMS_EPS)
                for t in range(2):
                    dve.tensor_scalar(at_h[:, t], x[:, t], rstd[:, t, 0:1], None, mul)\
                        .then_inc(sem(f"h_ready{t}"), 1)

            def mean_squares(grp, kind):
                w = int(kind == "k")
                dve.wait_ge(sem("at_sq"), 2 * grp + w + 1)
                if grp:
                    dve.wait_ge(sem("at_qk"), 2 * (grp - 1) + w + 1)
                step.run(dve.tensor_reduce(head_w[:, w].rearrange("p t h -> p (t h)"),
                                           sq_words(grp).rearrange("p (h d) -> p h d", d=64),
                                           AX, add))
                dve.tensor_scalar(head_v[:, w], head_w[:, w], 1.0 / 64, RMS_EPS, mul, add)\
                    .then_inc(sem("head_v"), 1)

            def attention(grp, out_g, mask, qk_ahead, between=lambda: None, last=lambda: None):
                move_T(qk_turn(grp), at_qkT)

                def masked(pr):
                    n = 4 * grp + pr
                    dve.wait_ge(sem("at_scored"), n + 1)
                    if n:
                        dve.wait_ge(sem("at_p"), 4 * n)
                    dve.tensor_tensor(at_sm, ps[:, 2:4, 0:HEAD_COLS],
                                      mask.unsqueeze(1).broadcast_to([P, 2, HEAD_COLS]), add)\
                        .then_inc(sem("at_masked"), 1)
                    dve.wait_ge(sem("at_masked"), n + 1)
                    hs = slice(2 * pr, 2 * pr + 2)
                    mx = at_mx[:, out_g]
                    step.add(dve.tensor_reduce(mx[:, 0, hs], at_sm[:, :, 0:P], AX, ALU.max))
                    step.add(dve.tensor_reduce(mx[:, 1, hs], at_sm[:, :, P:], AX, ALU.max))
                    step.settle()
                    dve.tensor_scalar(at_nmx[:, :, hs], mx[:, :, hs], -1.0, None, mul)\
                        .then_inc(sem("at_max"), 1)

                def move_pT(pr):
                    n = 4 * grp + pr
                    dve.wait_ge(sem("at_turned"), n + 1)
                    if n:
                        dve.wait_ge(sem("at_mixed"), n)
                    dve.tensor_copy(at_pT[:, 1, :], ps[:, 5, 0:HEAD_COLS])\
                        .then_inc(sem("at_pT_moved"), 1)

                def move_o(b):
                    dve.wait_ge(sem("at_mixed"), 4 * grp + 2 * b + 2)
                    dve.tensor_copy(at_oT[:, out_g, 2 * b:2 * b + 2, :],
                                    bank(6 + b).rearrange("p (k t) -> p k t", k=2))\
                        .then_inc(sem("at_o_moved"), 1)

                masked(0)
                move_pT(0)
                masked(1)
                move_pT(1)
                between()
                masked(2)
                if qk_ahead:
                    mean_squares(grp + 1, "q")
                move_pT(2)
                masked(3)
                move_o(0)
                move_pT(3)
                if qk_ahead:
                    mean_squares(grp + 1, "k")
                last()
                move_o(1)

            def ssd_dilated():
                g = base[SSD]
                rms_norm(1)
                move_T("h4", xT, range(4), Q("norm4"))
                pad0 = ss_pad[:, :, :, 0:3].rearrange("p b m t -> p (b m) t")
                step.add(dve.memset(pad0, 0.0))
                d = dt_v
                dve.wait_ge(sem("ss_dt"), 1)
                step.run(dve.tensor_tensor(
                    d[0], ps[:, 0, 0:32].rearrange("p (t h) -> p t h", t=2),
                    Q("dt_b").unsqueeze(1).broadcast_to([P, 2, 16]), add))
                dve.scalar_tensor_tensor(d[1], d[0], -1.0, d[0], mul, ALU.max)\
                    .then_inc(sem("ss_dabs"), 1)
                dve.wait_ge(sem("ss_soft"), 2)
                step.run(dve.scalar_tensor_tensor(d[6], d[0], 0.0, d[3], ALU.max, add))
                dve.scalar_tensor_tensor(d[5], d[6], -1.0,
                                         d[4][:, 0:1, :].broadcast_to([P, 2, 16]), mul, mul)\
                    .then_inc(sem("ss_a"), 1)
                w = Q("conv2_w")
                for c in range(4):
                    for m in range(4):
                        k = 4 * c + m
                        dve.wait_ge(sem("ss_taken"), 2 * k + 2)
                        for j in range(2):
                            step.run(dve.scalar_tensor_tensor(
                                xa[:, k, :], ss_pad[:, c % 2, m, j:j + TOK],
                                w[:, 4 * k + j:4 * k + j + 1], xa[:, k, :], mul, add))
                        dve.scalar_tensor_tensor(
                            xa[:, k, :], ss_pad[:, c % 2, m, 2:2 + TOK],
                            w[:, 4 * k + 2:4 * k + 3], xa[:, k, :], mul, add)\
                            .then_inc(sem("ss_conv"), 1)
                dve.wait_ge(sem("ss_cs"), 1)
                step.run(dve.tensor_scalar(
                    d[7], ps[:, 1, 0:32].rearrange("p (t h) -> p t h", t=2), -1.0, None, mul))
                for u in range(4):
                    dve.wait_ge(sem("ss_turned"), u + 1)
                    dve.tensor_copy(ss_x[:, u // 2, (u % 2) * 512:(u % 2 + 1) * 512],
                                    bank(2 + u % 2)).then_inc(sem("ss_x"), 1)
                dve.wait_ge(sem("ss_x"), 4)
                hd = [P, 16, 64]
                xh = [ss_x[:, t].rearrange("p (h d) -> p h d", d=64) for t in range(2)]
                yh = [ss_y[:, t].rearrange("p (h d) -> p h d", d=64) for t in range(2)]
                for t in range(2):
                    step.add(dve.tensor_tensor(
                        yh[t], xh[t], Q("d_skip").unsqueeze(2).broadcast_to(hd), mul))
                step.settle()
                for t in range(2):
                    step.add(dve.tensor_tensor(
                        xh[t], xh[t], d[6][:, t, :].unsqueeze(2).broadcast_to(hd), mul))
                step.settle()
                dve.sem_inc(sem("ss_xdt"), 1)

                def decay(h):
                    dve.wait_ge(sem("ss_sum"), h + 1)
                    o, p, m = ss_arg[:, h % 2, :], ps[:, 4 + h % 2, :], C("ssd_add")
                    dve.scalar_tensor_tensor(o[:, 0:TOK], p[:, 0:TOK], d[7][:, 0, h:h + 1],
                                             m[:, 0:TOK], add, add).then_inc(sem("ss_arg"), 1)
                    dve.scalar_tensor_tensor(o[:, TOK:], p[:, P:TOK], d[7][:, 1, h:h + 1],
                                             m[:, TOK:], add, add).then_inc(sem("ss_arg"), 1)

                def scan(h):
                    dve.wait_ge(sem("ss_e"), h + 1)
                    if h >= 2:
                        dve.wait_ge(sem("ss_yh"), h - 1)
                    dve.tensor_tensor(ss_m[:, h % 2, :], ss_arg[:, h % 2, :],
                                      ss_cb[:, h // 4, :], mul).then_inc(sem("ss_m"), 1)

                dve.wait_ge(sem("ss_cb"), 4)
                for n in range(SSD_HEADS + 1):
                    if n < SSD_HEADS:
                        if n >= 2:
                            dve.wait_ge(sem("ss_m"), n - 1)
                        decay(n)
                    if n >= 1:
                        scan(n - 1)
                    if n in (6, 10):
                        mean_squares(0, "qk"[(n - 6) // 4])
                dve.wait_ge(sem("ss_yh"), SSD_HEADS)
                for t in range(2):
                    v = ss_y[:, t].rearrange("p (n c) -> p n c", n=2)
                    step.add(dve.tensor_tensor(v, two_banks(2 * t), v, add))
                step.settle()
                dve.sem_inc(sem("ss_y_taken"), 1)

                def between():
                    dve.wait_ge(sem("ss_sq"), 8)
                    inv_root(ss_ss, ss_ss, 1.0 / 256, RMS_EPS)
                    dve.sem_inc(sem("ss_rstd"), 1)

                add4 = C("att_add").rearrange("p (n c) -> p n c", n=4)
                attention(0, 0, add4[:, 0, :], True, between)
                dve.wait_ge(sem("at_qk"), 2)
                move_T("y4", mixT12, range(4), Q("ssd_norm"))
                attention(1, 1, add4[:, 1, :], True)
                attention(2, 2, add4[:, 2, :], False)
                mx3, den3, em3, ed3, wt3 = (v.rearrange("p g t h -> p g (t h)") for v in
                                            (at_mx, at_den, at_em, at_ed, at_wt))
                lm, ls = (v.rearrange("p t h -> p (t h)") for v in (at_lm, at_ls))
                step.run(dve.tensor_reduce(lm, mx3.rearrange("p g n -> p n g"), AX, ALU.max))
                dve.tensor_tensor(em3, mx3, lm.unsqueeze(1).broadcast_to([P, 3, 16]), sub)\
                    .then_inc(sem("at_em"), 1)
                dve.wait_ge(sem("at_em_exp"), 1)
                step.run(dve.tensor_tensor(ed3, em3, den3, mul))
                step.run(dve.tensor_reduce(ls, ed3.rearrange("p g n -> p n g"), AX, add))
                step.run(dve.reciprocal(ls, ls))
                dve.tensor_tensor(wt3, em3, ls.unsqueeze(1).broadcast_to([P, 3, 16]), mul)\
                    .then_inc(sem("at_weighed"), 1)
                dve.wait_ge(sem("at_o_moved"), 6)
                for q in range(3):
                    o = at_oT[:, q].rearrange("p (b k) t -> p b (k t)", b=2)
                    dve.wait_ge(sem("at_wT"), q + 1)
                    dve.tensor_tensor(o, o, two_banks(6 if q == 1 else 4), mul)\
                        .then_inc(sem("at_wT_used"), 1)
                    dve.wait_ge(sem("at_wT_used"), q + 1)
                    if q:
                        step.run(dve.tensor_tensor(at_oT[:, 0], at_oT[:, 0], at_oT[:, q], add))
                dve.wait_ge(sem("at_proj"), 10)
                dve.tensor_tensor(mixT12[:, 8:12, :], at_oT[:, 0], at_g4, mul)\
                    .then_inc(sem("at_mixT"), 1)
                finish(SSD)

            def finish(stage):
                for t in range(2):
                    if t == 0:
                        dve.wait_ge(tile_out, out_no(stage))
                    else:
                        dve.wait_ge(chunk_done, base[stage] + STAGE_CHUNKS[stage])
                    xt = x[:, t].rearrange("p (n c) -> p n c", n=2)
                    dve.tensor_tensor(xt, two_banks(2 * t), xt, add).then_inc(x_ready[t], 1)

            def block_attention():
                g = base[MOBA]
                two = SSD in on
                rms_norm(2 if two else 1)
                move_T("h5", xT, range(4), Q("norm5"))
                causal = C("att_add")[:, 3 * HEAD_COLS:]
                n, no = g_no(3), (1 if two else 0)
                mean_squares(n, "q")
                mean_squares(n, "k")

                def reciprocals(grp):
                    dve.wait_ge(sem("at_p"), 16 * (n + grp + 1))
                    dve.reciprocal(at_wt[:, grp], at_den[:, grp]).then_inc(sem("at_weighed"), 1)

                def mixed(grp):
                    o = at_oT[:, grp].rearrange("p (b k) t -> p b (k t)", b=2)
                    wT = (3 if two else 0) + grp + 1
                    dve.wait_ge(sem("at_o_moved"), 2 * (n + grp + 1))
                    dve.wait_ge(sem("at_wT"), wT)
                    dve.tensor_tensor(o, o, two_banks(4 * grp), mul).then_inc(sem("at_wT_used"), 1)
                    dve.wait_ge(sem("at_wT_used"), wT)
                    dve.wait_ge(sem("at_proj"), (10 if two else 0) + 4 * (grp + 1))
                    dve.tensor_tensor(mixT12[:, 4 * grp:4 * grp + 4, :], at_oT[:, grp],
                                      at_g5[:, 4 * grp:4 * grp + 4], mul)\
                        .then_inc(sem("at_mixT"), 1)

                attention(n, 0, causal, True, last=lambda: reciprocals(0))
                attention(n + 1, 1, causal, False, last=lambda: (mixed(0), reciprocals(1)))
                mixed(1)
                finish(MOBA)

            if first != CONV:
                dve.wait_ge(const_in, 32)
            run = {CONV: conv_mixers, MOE0: lambda: experts(MOE0, 0), STICK: stick_breaking,
                   MOE1: lambda: experts(MOE1, 1), SSD: ssd_dilated, MOBA: block_attention}
            if first != CONV:
                wait_x(dve, first)
            for stage in on:
                run[stage]()


INPUTS = ["x", "even_w_in", "even_w_out", "odd_w_qkv", "odd_w_o", "ln_mix_g", "ln_mix_b",
          "ln_ffn_g", "ln_ffn_b", "expert_w_up", "expert_w_down", "even_w_in_2", "even_w_out_2",
          "odd_w_in_2", "odd_w_out_2"]


def small_params(a):
    p = np.zeros((P, PARAM_WORDS), np.float32)

    def put(name, value):
        p[:, PARAM[name][0]:PARAM[name][1]] = value.reshape(P, -1)

    def column(v):
        return v.reshape(-1, P).T

    def row(v):
        return np.broadcast_to(v.reshape(1, -1), (P, v.size))

    put("conv_a", a["even_conv_a"][0].reshape(CONV_A, 4, P).transpose(2, 1, 0))
    put("conv_b", a["even_conv_b_w"][0].reshape(CONV_B, 4, P).transpose(2, 1, 0))
    put("conv_bb", column(a["even_conv_b_bias"][0]))
    put("norm_g", column(a["even_norm_b_g"][0]))
    put("norm_b", column(a["even_norm_b_b"][0]))
    w = np.concatenate([a["router_group_w"], a["router_expert_w"]], 2)
    put("router_w", w.reshape(2, KT, P, 36).transpose(2, 0, 1, 3))
    put("router_b", row(np.concatenate([a["router_group_b"], a["router_expert_b"]], 1)))
    put("dt_w", a["even_w_in_2"][0][:, 3072:3088].reshape(KT, P, 16).transpose(1, 0, 2))
    put("conv2_w", a["even_conv_w_2"][0].reshape(16, P, 4).transpose(1, 0, 2))
    put("conv2_b", column(a["even_conv_b_2"][0]))
    put("norm4", column(a["even_norm_w_2"][0]))
    put("norm5", column(a["odd_norm_w_2"][0]))
    put("ssd_norm", column(a["even_ssd_norm_w_2"][0]))
    put("dt_b", row(a["even_dt_bias_2"][0]))
    put("a_log", row(a["even_a_log_2"][0]))
    put("d_skip", row(a["even_d_skip_2"][0]))
    put("qk4", row(np.concatenate([a["even_q_norm_2"][0], a["even_k_norm_2"][0]])))
    put("qk5", row(np.concatenate([a["odd_q_norm_2"][0], a["odd_k_norm_2"][0]])))
    return p


def kernel(**inputs):
    import concourse.bacc as bacc
    from concourse.bass_utils import run_bass_kernel_spmd

    nc = bacc.Bacc("TRN2", target_bir_lowering=False, num_devices=1)
    host = {k: np.asarray(v) for k, v in inputs.items()}
    arrays = {name: np.ascontiguousarray(host[name]) for name in INPUTS}
    arrays["params"] = small_params(host)
    arrays["constants"] = constants()
    dram = {name: nc.dram_tensor(f"in_{name}", v.shape, mybir.dt.from_np(v.dtype),
                                 kind="ExternalInput").ap() for name, v in arrays.items()}
    out = nc.dram_tensor("out_x", (1, TOK, D), F32, kind="ExternalOutput").ap()
    build(nc, dram, out, *STAGES)
    r = run_bass_kernel_spmd(nc, [{f"in_{k}": v for k, v in arrays.items()}], core_ids=[0])
    return r.results[0]["out_x"]


STAGES = (0, 5)
```
